# Optimizing a Trainium2 kernel written in Bass

```python
import jax, jax.numpy as jnp
from jax import lax
import numpy as np

D_MODEL = 1024
BATCH = 1
SEQ = 128
DEPTH = 1
DEC_BATCH = 1
DEC_SEQ = 512
PAST_LEN = 128

GRID_W = 64
D_RNN = D_MODEL
RNN_HEADS = 16
RNN_BLOCK = D_RNN // RNN_HEADS
RG_CONV_W = 4
RG_C = 8.0
D_CONV = D_MODEL
CONV_K = 31
N_EXPERTS = 16
EC_CAPACITY = 2
D_FF_E = 2 * D_MODEL
D_IN = D_RNN + 2 * D_CONV + 2 * D_MODEL
EPS = 1e-6

kernel_name = 'hybrid_rglru_conformer_ecmoe_diffusion_step'

def rmsnorm(x, g):
    xf = x.astype(jnp.float32)
    y = xf * lax.rsqrt(jnp.mean(xf * xf, axis=-1, keepdims=True) + EPS)
    return (y * g.astype(jnp.float32)).astype(x.dtype)

def layernorm(x, g, b):
    xf = x.astype(jnp.float32)
    mu = jnp.mean(xf, axis=-1, keepdims=True)
    var = jnp.mean(jnp.square(xf - mu), axis=-1, keepdims=True)
    y = (xf - mu) * lax.rsqrt(var + EPS)
    return (y * g.astype(jnp.float32) + b.astype(jnp.float32)).astype(x.dtype)

def dwconv_seq(u, w, b, pad_l, pad_r):
    C = u.shape[-1]
    y = lax.conv_general_dilated(u, w[:, None, :].astype(u.dtype), window_strides=(1,),
                                 padding=[(pad_l, pad_r)],
                                 dimension_numbers=('NWC', 'WIO', 'NWC'),
                                 feature_group_count=C)
    return y + b.astype(u.dtype)

def dwconv_grid_vertical(u, w, b):
    B, L, C = u.shape
    rows = L // GRID_W
    ug = u.reshape(B, rows, GRID_W, C)
    y = lax.conv_general_dilated(ug, w[:, None, None, :].astype(u.dtype), window_strides=(1, 1),
                                 padding=[(CONV_K // 2, CONV_K // 2), (0, 0)],
                                 dimension_numbers=('NHWC', 'HWIO', 'NHWC'),
                                 feature_group_count=C)
    return y.reshape(B, L, C) + b.astype(u.dtype)

def _lru_combine(left, right):
    a1, b1 = left
    a2, b2 = right
    return a1 * a2, a2 * b1 + b2

def rglru_direction(xc, gate_w, gate_b, lam, h0, reverse):
    B, L, R = xc.shape
    xh = xc.reshape(B, L, RNN_HEADS, RNN_BLOCK)
    gates = jnp.einsum('blhi,ghij->gblhj', xh, gate_w.astype(jnp.float32)).reshape(2, B, L, R)
    gates = gates + gate_b.astype(jnp.float32)[:, None, None, :]
    r = jax.nn.sigmoid(gates[0])
    i = jax.nn.sigmoid(gates[1])
    log_a = -RG_C * r * jax.nn.softplus(-lam.astype(jnp.float32))
    a = jnp.exp(log_a)
    bterm = jnp.sqrt(-jnp.expm1(2.0 * log_a)) * (i * xc)
    a_cum, h_zero = lax.associative_scan(_lru_combine, (a, bterm), reverse=reverse, axis=1)
    h = a_cum * h0[:, None, :] + h_zero
    h_last = h[:, 0] if reverse else h[:, -1]
    return h, h_last

def rglru_branch(xr, h0_f, h0_b, conv_w, conv_b, gate_w, gate_b, lam):
    pad_l = RG_CONV_W // 2
    xc = dwconv_seq(xr, conv_w, conv_b, pad_l, RG_CONV_W - 1 - pad_l).astype(jnp.float32)
    h_f, last_f = rglru_direction(xc, gate_w[0], gate_b[0], lam[0], h0_f.astype(jnp.float32), False)
    h_b, last_b = rglru_direction(xc, gate_w[1], gate_b[1], lam[1], h0_b.astype(jnp.float32), True)
    return (h_f + h_b).astype(xr.dtype), last_f, last_b

def conformer_branch(xv, xg, grid, dw_w, dw_b, ln_g, ln_b):
    u = xv * jax.nn.sigmoid(xg)
    if grid:
        u = dwconv_grid_vertical(u, dw_w, dw_b)
    else:
        u = dwconv_seq(u, dw_w, dw_b, CONV_K // 2, CONV_K // 2)
    return jax.nn.silu(layernorm(u, ln_g, ln_b))

def ec_moe(v, w_router, w_e1, w_e3, w_e2):
    B, n, D = v.shape
    cap = EC_CAPACITY * n // N_EXPERTS
    affin = jax.nn.softmax((v @ w_router).astype(jnp.float32), axis=-1)
    g, idx = lax.top_k(jnp.swapaxes(affin, 1, 2), cap)
    xe = jax.vmap(lambda xb, ib: xb[ib])(v, idx)
    hdn = jax.nn.silu(jnp.einsum('becd,edf->becf', xe, w_e1)) * jnp.einsum('becd,edf->becf', xe, w_e3)
    ye = jnp.einsum('becf,efd->becd', hdn, w_e2) * g[..., None].astype(v.dtype)
    out = jax.vmap(lambda ib, yb: jnp.zeros((n, D), yb.dtype).at[ib.reshape(-1)].add(yb.reshape(-1, D)))(idx, ye)
    return out

def trunk_layer(x, mod, h0_f, h0_b, grid, norm1_g, norm2_g, w_in, rnn_conv_w, rnn_conv_b,
                rnn_gate_w, rnn_gate_b, rnn_lambda, w_rnn_out, conv_dw_w, conv_dw_b,
                conv_ln_g, conv_ln_b, w_conv_out, w_out, w_router, w_e1, w_e3, w_e2):
    sh1, sc1, g1, sh2, sc2, g2 = jnp.split(mod[:, None, :].astype(x.dtype), 6, axis=-1)
    u = rmsnorm(x, norm1_g) * (1 + sc1) + sh1
    z = u @ w_in
    xr, xv, xg, ga, gb = jnp.split(z, [D_RNN, D_RNN + D_CONV, D_RNN + 2 * D_CONV,
                                      D_RNN + 2 * D_CONV + D_MODEL], axis=-1)
    y_a, last_f, last_b = rglru_branch(xr, h0_f, h0_b, rnn_conv_w, rnn_conv_b,
                                       rnn_gate_w, rnn_gate_b, rnn_lambda)
    y_b = conformer_branch(xv, xg, grid, conv_dw_w, conv_dw_b, conv_ln_g, conv_ln_b)
    merged = jax.nn.sigmoid(ga) * (y_a @ w_rnn_out) + jax.nn.sigmoid(gb) * (y_b @ w_conv_out)
    x = x + g1 * (merged @ w_out)
    v = rmsnorm(x, norm2_g) * (1 + sc2) + sh2
    x = x + g2 * ec_moe(v, w_router, w_e1, w_e3, w_e2)
    return x, last_f, last_b

def setup_inputs(seed: int = 0) -> dict:
    key = jax.random.key(seed)
    ks = jax.random.split(key, 32)
    f32 = jnp.float32
    nrm = lambda k, shape, s: jax.random.normal(k, shape, f32) * s
    u = jax.random.uniform(ks[12], (DEPTH, 2, D_RNN), f32, minval=0.9, maxval=0.999)
    a0 = u ** (1.0 / RG_C)
    lam = jnp.log(a0) - jnp.log1p(-a0)
    return {
        'x_prompt': nrm(ks[0], (BATCH, SEQ, D_MODEL), 1.0),
        'x_sample': nrm(ks[1], (DEC_BATCH, DEC_SEQ, D_MODEL), 1.0),
        'state_rglru': nrm(ks[2], (DEC_BATCH, DEPTH, 2, D_RNN), 0.5),
        'c': nrm(ks[3], (DEC_BATCH, D_MODEL), 1.0),
        'c_ctx': nrm(ks[4], (D_MODEL,), 1.0),
        'norm1_g': 1.0 + nrm(ks[5], (DEPTH, D_MODEL), 0.02),
        'norm2_g': 1.0 + nrm(ks[6], (DEPTH, D_MODEL), 0.02),
        'w_mod': nrm(ks[7], (DEPTH, D_MODEL, 6 * D_MODEL), 0.5 * D_MODEL ** -0.5),
        'b_mod': nrm(ks[8], (DEPTH, 6 * D_MODEL), 0.01),
        'w_in': nrm(ks[9], (DEPTH, D_MODEL, D_IN), D_MODEL ** -0.5),
        'rnn_conv_w': nrm(ks[10], (DEPTH, RG_CONV_W, D_RNN), RG_CONV_W ** -0.5),
        'rnn_conv_b': nrm(ks[11], (DEPTH, D_RNN), 0.01),
        'rnn_gate_w': nrm(ks[13], (DEPTH, 2, 2, RNN_HEADS, RNN_BLOCK, RNN_BLOCK), RNN_BLOCK ** -0.5),
        'rnn_gate_b': nrm(ks[14], (DEPTH, 2, 2, D_RNN), 0.01),
        'rnn_lambda': lam,
        'w_rnn_out': nrm(ks[15], (DEPTH, D_RNN, D_MODEL), D_RNN ** -0.5),
        'conv_dw_w': nrm(ks[16], (DEPTH, CONV_K, D_CONV), CONV_K ** -0.5),
        'conv_dw_b': nrm(ks[17], (DEPTH, D_CONV), 0.01),
        'conv_ln_g': 1.0 + nrm(ks[18], (DEPTH, D_CONV), 0.02),
        'conv_ln_b': nrm(ks[19], (DEPTH, D_CONV), 0.01),
        'w_conv_out': nrm(ks[20], (DEPTH, D_CONV, D_MODEL), D_CONV ** -0.5),
        'w_out': nrm(ks[21], (DEPTH, D_MODEL, D_MODEL), D_MODEL ** -0.5),
        'w_router': nrm(ks[22], (DEPTH, D_MODEL, N_EXPERTS), D_MODEL ** -0.5),
        'w_e1': nrm(ks[23], (DEPTH, N_EXPERTS, D_MODEL, D_FF_E), D_MODEL ** -0.5),
        'w_e3': nrm(ks[24], (DEPTH, N_EXPERTS, D_MODEL, D_FF_E), D_MODEL ** -0.5),
        'w_e2': nrm(ks[25], (DEPTH, N_EXPERTS, D_FF_E, D_MODEL), D_FF_E ** -0.5),
        'final_norm_g': 1.0 + nrm(ks[26], (D_MODEL,), 0.02),
    }

def reference(x_prompt, x_sample, state_rglru, c, c_ctx, norm1_g, norm2_g, w_mod, b_mod, w_in,
              rnn_conv_w, rnn_conv_b, rnn_gate_w, rnn_gate_b, rnn_lambda, w_rnn_out,
              conv_dw_w, conv_dw_b, conv_ln_g, conv_ln_b, w_conv_out, w_out, w_router,
              w_e1, w_e3, w_e2, final_norm_g):
    x = x_prompt
    bp = x.shape[0]
    zeros_h = jnp.zeros((bp, D_RNN), jnp.float32)
    ctx_states = []
    for l in range(DEPTH):
        lp = (norm1_g[l], norm2_g[l], w_in[l], rnn_conv_w[l], rnn_conv_b[l], rnn_gate_w[l],
              rnn_gate_b[l], rnn_lambda[l], w_rnn_out[l], conv_dw_w[l], conv_dw_b[l],
              conv_ln_g[l], conv_ln_b[l], w_conv_out[l], w_out[l], w_router[l],
              w_e1[l], w_e3[l], w_e2[l])
        mod_ctx = jax.nn.silu(c_ctx)[None, :] @ w_mod[l] + b_mod[l]
        x, last_f, last_b = trunk_layer(x, mod_ctx, zeros_h, zeros_h, False, *lp)
        ctx_states.append(jnp.stack([last_f, last_b], axis=1).astype(x_prompt.dtype))
    y_prompt = rmsnorm(x, final_norm_g)
    new_state_rglru = jnp.stack(ctx_states, axis=1)

    x = x_sample
    for l in range(DEPTH):
        lp = (norm1_g[l], norm2_g[l], w_in[l], rnn_conv_w[l], rnn_conv_b[l], rnn_gate_w[l],
              rnn_gate_b[l], rnn_lambda[l], w_rnn_out[l], conv_dw_w[l], conv_dw_b[l],
              conv_ln_g[l], conv_ln_b[l], w_conv_out[l], w_out[l], w_router[l],
              w_e1[l], w_e3[l], w_e2[l])
        mod = jax.nn.silu(c) @ w_mod[l] + b_mod[l]
        x, _, _ = trunk_layer(x, mod, state_rglru[:, l, 0], state_rglru[:, l, 1], True, *lp)
    y_sample = rmsnorm(x, final_norm_g)
    return (y_prompt, y_sample, new_state_rglru)


_drawn_inputs = setup_inputs


def setup_inputs(seed=0):
    import zlib

    import numpy as np

    out = dict(_drawn_inputs(seed))
    spreads = {}
    factors = {'norm1_g': 5.482,
     'norm2_g': 8.0,
     'rnn_gate_b': 8.0,
     'conv_dw_b': 8.0,
     'conv_ln_g': 8.0,
     'conv_ln_b': 8.0,
     'final_norm_g': 2.781}
    for name, (base, spread) in spreads.items():
        noise = np.random.default_rng([zlib.crc32(name.encode()), seed]).standard_normal(out[name].shape)
        drawn = base * np.exp(spread * noise) if base else spread * noise
        out[name] = __import__('jax').numpy.asarray(drawn.astype(out[name].dtype))
    for name, factor in factors.items():
        out[name] = (out[name] * factor).astype(out[name].dtype)
    return out
```

```python
from contextlib import ExitStack

import concourse.bass as bass
from concourse import mybir

P = 128
D = 1024
KD = D // P
NP, NS = 128, 512
N = NP + NS
NT = N // P
HALF = N // 2
GRID_W = 64
GRID_H = NS // GRID_W
TAPS4 = 4
TAPS31 = 31
MID = TAPS31 // 2
E = 16
FF = 2 * D
KF = FF // P
CAP_P = 2 * NP // E
CAP_S = 2 * NS // E
CAP = CAP_S + CAP_P
DIN = 5 * D
EPS = 1e-6
RG_C = 8.0

S0 = NP + 3
LX = 644
LXP = LX + TAPS4

ALU = mybir.AluOpType
ACT = mybir.ActivationFunctionType
AX = mybir.AxisListType
F32 = mybir.dt.float32
F32R = mybir.dt.float32r
U32 = mybir.dt.uint32

C_BMOD, C_N1, C_N2, C_C, C_CTX, C_LNG, C_LNB, C_TAB = 0, 48, 56, 64, 72, 80, 88, 96
G_STATE, G_RCB, G_CDB, G_RCW, G_GB, G_LAM, G_CDW, G_NLAM = 0, 2, 3, 4, 8, 12, 14, 45
NG = 47
NCOLS = C_TAB + 8 * NG

SLOT = 4096
NSLOT = 6
WA_OFF = 0
TEMPS = 2 * SLOT
MOE_SLOTS = [2, 3, 0, 1, 4, 5]


class Steps:

    def __init__(self, eng, sem):
        self.eng, self.sem, self.n = eng, sem, 0

    def did(self, ins):
        ins.then_inc(self.sem, 1)
        self.n += 1

    def wait(self, back=0):
        if self.n > back:
            self.eng.wait_ge(self.sem, self.n - back)

    def restart(self):
        self.wait()
        self.eng.sem_clear(self.sem)
        self.n = 0


def conv_ranges():
    prompt, sample = [], []
    for k in range(TAPS31):
        s = k - MID
        if s:
            a, b = max(0, -s), min(NP, NP - s)
            prompt.append((k, a, b, s))
        if s and abs(s) < GRID_H:
            a, b = max(0, -s) * GRID_W, (GRID_H - max(0, s)) * GRID_W
            sample.append((k, NP + a, NP + b, s * GRID_W))
    out = []
    while prompt or sample:
        out += [c.pop(0) for c in (prompt, sample) if c]
    return out


def trunk_layer(nc, a):
    x_prompt = a["x_prompt"][0]
    x_sample = a["x_sample"][0].rearrange("(t p) d -> t p d", p=P)
    w_in = a["w_in"][0].rearrange("(k p) c -> p k c", p=P)
    w_mod = a["w_mod"][0].rearrange("(k p) c -> p k c", p=P)
    w_ro = a["w_rnn_out"][0].rearrange("(k p) c -> p k c", p=P)
    w_co = a["w_conv_out"][0].rearrange("(k p) c -> p k c", p=P)
    w_out = a["w_out"][0].rearrange("(k p) c -> p k c", p=P)
    w_router = a["w_router"][0].rearrange("(k p) e -> p k e", p=P)
    w_e1 = a["w_e1"][0].rearrange("e (k p) f -> e p k f", p=P)
    w_e3 = a["w_e3"][0].rearrange("e (k p) f -> e p k f", p=P)
    w_e2 = a["w_e2"][0].rearrange("e (k p) f -> e p k f", p=P)
    w_e2_rows = a["w_e2"][0].rearrange("e (q k p) f -> p (e q) k f", k=4, p=P)
    gate_w = a["rnn_gate_w"][0].rearrange("a g h i j -> i (a g) h j")

    mod_rows = nc.dram_tensor("mod_rows", [2, 6 * D], F32, kind="Internal").ap()
    xn_dram = nc.dram_tensor("xn_dram", [N, D], F32, kind="Internal").ap()
    acc_dram = nc.dram_tensor("acc_dram", [N, D], F32, kind="Internal").ap()

    with ExitStack() as ctx:
        place = {}

        def sb(name, shape, dt=F32):
            place[name] = -(-nc.sbuf_base // 32) * 32
            return ctx.enter_context(nc.sbuf_tensor(name, shape, dt))

        def rounded(name, under, at, *shape):
            return nc.alloc_sbuf_tensor_at(name, [P, *shape], F32R, offset=place[under] + 4 * at)

        def sem(name):
            return ctx.enter_context(nc.semaphore(name))

        ring = sb("ring", [P, NSLOT * SLOT])
        uT = sb("uT", [P, KD, N])
        xr = sb("xr", [P, NT, D])
        ya = sb("ya", [P, KD, N])
        cu = sb("cu", [P, KD, N])
        xpad = sb("xpad", [P, 2, LXP])
        sg = sb("sg", [P, 2, N])
        gw = sb("gw", [P, 2, 4, P])
        cols = sb("cols", [P, NCOLS])
        cur = sb("cur", [P, NG, 2])
        modc = sb("modc", [P, 48, 2])
        a1 = sb("a1", [P, KD, 2])
        a2 = sb("a2", [P, KD, 2])
        ident = sb("ident", [P, P])
        ones = sb("ones", [P, P])
        vecs = sb("vecs", [P, 4, P])
        silu_c = sb("silu_c", [P, KD, 2])
        sp = sb("sp", [P, 5, 16])
        last = sb("last", [P, 2, KD])
        last_t = sb("last_t", [16, P])
        wr = sb("wr", [P, KD, E])
        rstat = sb("rstat", [P, 4, NT])
        soft = sb("soft", [P, NT, E])
        sstat = sb("sstat", [P, 3, NT])
        lg = sb("lg", [E, N])
        idx = sb("idx", [E, CAP], U32)
        idx_f = sb("idx_f", [E, CAP])
        gates_e = sb("gates_e", [E, CAP])
        idx_t = sb("idx_t", [CAP, E + 1], U32)
        gate_t = sb("gate_t", [CAP, E])
        idx_g = sb("idx_g", [CAP, 1], U32)
        idx_s = sb("idx_s", [CAP, 1], U32)
        ps = ctx.enter_context(nc.psum_tensor("ps", [P, 8, 512], F32))

        def flat(t):
            return t[:, :, :].rearrange("p a b -> p (a b)")

        ya_f, cu_f = flat(ya), flat(cu)

        def slot(s, n=1):
            return ring[:, s * SLOT:(s + n) * SLOT]

        def temps(at, *shape):
            n = 1
            for s in shape:
                n *= s
            v = ring[:, TEMPS + at:TEMPS + at + n]
            names = "abcd"[:len(shape)]
            if len(shape) == 1:
                return v
            return v.rearrange(f"p ({' '.join(names)}) -> p {' '.join(names)}",
                               **dict(zip(names[1:], shape[1:])))

        at = 0
        lr_r = temps(at, 2, 2, LX)
        lr_i = temps(at + 4 * LX, 2, 2, LX)
        lr_a = temps(at + 8 * LX, 2, 2, LX)
        lr_q = temps(at + 12 * LX, 2, 2, LX)
        at = 16 * LX
        glu = temps(at, 2, N)
        cv = temps(at + 2 * N, 2, N)
        xc = temps(at + 4 * N, 2, LX)
        at = 4 * SLOT - 4 * N
        ln_mu = temps(at, N)
        ln_rs = temps(at + N, N)
        ln_sq = temps(at + 2 * N, 2, N)
        merged = temps(2 * SLOT, NT, D)
        xn2 = merged
        xn1 = cu_f.rearrange("p (t d) -> p t d", t=NT)
        mod_row = ya_f[0:2, 0:2 * D]
        mT = uT
        vT = uT
        g1b = cu_f[:, 0:2 * D].rearrange("p (s d) -> p s d", s=2)
        bias1 = cu_f[:, 2 * D:3 * D]
        bias2 = cu_f[:, 3 * D:4 * D]
        prod = cu_f[:, 4 * D:5 * D].rearrange("p (b c) -> p b c", b=2)
        g2b = ya_f[0:CAP, 0:D]
        xe = ya_f[0:CAP, D:2 * D]
        ye = ya_f[0:CAP, 2 * D:3 * D]
        xeT = ya_f[:, 3 * D:3 * D + KD * CAP].rearrange("p (k c) -> p k c", k=KD)
        xe_hi = rounded("xe_hi", "ya", 3 * D + KD * CAP, KD, CAP)
        xe_lo = rounded("xe_lo", "ya", 3 * D, KD, CAP)
        h_hi = rounded("h_hi", "cu", 3 * D, KF, CAP)
        h_lo = rounded("h_lo", "sg", 0, KF, CAP)
        w_hi = [rounded("w_hi0", "uT", 0, 4, D), rounded("w_hi1", "xr", 0, 4, D)]
        ring_lo = rounded("ring_lo", "ring", 0, NSLOT, 4, D)
        hs = cu_f[0:CAP, 0:FF]
        gf = cu_f[:, 2 * D:3 * D]

        vec_loaded = sem("vec_loaded")
        x_loaded = sem("x_loaded")
        wr_loaded = sem("wr_loaded")
        consts_ready = sem("consts_ready")
        cols_turned = sem("cols_turned")
        cols_ready = sem("cols_ready")
        silu_ready = sem("silu_ready")
        exp_lam_ready = sem("exp_lam_ready")
        decay_ready = sem("decay_ready")
        mod_loaded = [sem(f"mod_loaded{s}") for s in range(4)]
        mod_used = [sem(f"mod_used{s}") for s in range(4)]
        mod_row_ready = sem("mod_row_ready")
        mod_row_stored = sem("mod_row_stored")
        mod_turned = sem("mod_turned")
        modc_ready = sem("modc_ready")
        a12_ready = sem("a12_ready")
        ssq_ready = sem("ssq_ready")
        ms_ready = sem("ms_ready")
        root_ready = sem("root_ready")
        r_ready = sem("r_ready")
        xn1_ready = sem("xn1_ready")
        xt_turned = sem("xt_turned")
        ut_sample = sem("ut_sample")
        ut_prompt = sem("ut_prompt")

        wa_loaded = [sem(f"wa_loaded{k}") for k in range(3)]
        gw_loaded = sem("gw_loaded")
        xr_done = sem("xr_done")
        xv_done = sem("xv_done")
        xg_done = sem("xg_done")
        gate_done = sem("gate_done")
        xr_copied = sem("xr_copied")
        cur_ready = sem("cur_ready")
        tap0_ready = sem("tap0_ready")
        xc_ready = sem("xc_ready")
        xg_sig = sem("xg_sig")
        glu_ready = sem("glu_ready")
        gate_sig = sem("gate_sig")
        decay_sq = sem("decay_sq")
        in_sq = sem("in_sq")
        in_root = sem("in_root")
        ix_ready = sem("ix_ready")
        conv_done = sem("conv_done")
        cv_copied = sem("cv_copied")
        lru_done = sem("lru_done")
        last_turned = sem("last_turned")
        last_ready = sem("last_ready")
        state_stored = sem("state_stored")

        ln_summed = sem("ln_summed")
        ln_centred = sem("ln_centred")
        ln_squared = sem("ln_squared")
        ln_sq_used = sem("ln_sq_used")
        ln_var = sem("ln_var")
        ln_root = sem("ln_root")
        ln_scaled = sem("ln_scaled")
        yb_ready = sem("yb_ready")

        wb_loaded = [sem(f"wb_loaded{p}") for p in range(2)]
        gab_done = sem("gab_done")
        pab_done = sem("pab_done")
        gab_sig = sem("gab_sig")
        merged_ready = sem("merged_ready")
        mt_turned = sem("mt_turned")
        mt_sample = sem("mt_sample")
        mt_prompt = sem("mt_prompt")
        rows_loaded = sem("rows_loaded")
        rows_ready = sem("rows_ready")
        wc_loaded = [sem(f"wc_loaded{h}") for h in range(2)]
        wo_done = sem("wo_done")
        x2_ready = sem("x2_ready")
        ssq2_ready = sem("ssq2_ready")
        ms2_ready = sem("ms2_ready")
        root2_ready = sem("root2_ready")
        r2_ready = sem("r2_ready")
        xn2_ready = sem("xn2_ready")
        rows_stored = sem("rows_stored")
        vt_turned = sem("vt_turned")
        vt_dve = sem("vt_dve")
        vt_act = sem("vt_act")
        logit_done = sem("logit_done")
        lg_ready = sem("lg_ready")
        lg_turned = sem("lg_turned")
        max_ready = sem("max_ready")
        exp_ready = sem("exp_ready")
        soft_ready = sem("soft_ready")
        soft_turned = sem("soft_turned")
        top_ready = sem("top_ready")
        top_turned = sem("top_turned")
        idx_ready = sem("idx_ready")

        w_loaded = [sem(f"w_loaded{s}") for s in range(NSLOT)]
        unit_hi = sem("unit_hi")
        unit_split = sem("unit_split")
        unit_used = sem("unit_used")
        xe_modulated = sem("xe_modulated")
        xe_hi_ready = sem("xe_hi_ready")
        h_hi_ready = sem("h_hi_ready")
        xe_loaded = sem("xe_loaded")
        xe_turned = sem("xe_turned")
        xeT_ready = sem("xeT_ready")
        h1_silu = sem("h1_silu")
        h_ready = sem("h_ready")
        h_turned = sem("h_turned")
        hT_ready = sem("hT_ready")
        ye_ready = sem("ye_ready")
        scattered = sem("scattered")
        gf_loaded = sem("gf_loaded")
        fin_loaded = [sem(f"fin_loaded{t}") for t in range(NT)]
        fin_ssq = sem("fin_ssq")
        fin_ms = sem("fin_ms")
        fin_root = sem("fin_root")
        out_ready = sem("out_ready")
        out_stored = sem("out_stored")
        dve_step = sem("dve_step")
        act_step = sem("act_step")
        pool_step = sem("pool_step")

        block = ctx.enter_context(nc.Block())

        def wa(kind):
            return ring[:, WA_OFF + 2048 * kind:WA_OFF + 2048 * (kind + 1)].rearrange("p (k c) -> p k c", k=KD)

        def wb(p, m):
            at = 2 * p * SLOT + 2048 * m
            return ring[:, at:at + 2048].rearrange("p (k c) -> p k c", k=KD)

        def sg_ab(g):
            return flat(sg)[:, 512 * g:512 * g + 512].rearrange("p (m c) -> p m c", m=2)

        def chunk_source(e, m):
            if m < 8:
                w = (w_e1, w_e3)[m // 2 % 2]
                return w[e, :, 4 * (m % 2):4 * (m % 2) + 4, (m // 4) * D:(m // 4 + 1) * D]
            return w_e2[e, :, 4 * (m - 8):4 * (m - 8) + 4, :]

        def chunk(m):
            return slot(MOE_SLOTS[m % NSLOT]).rearrange("p (k c) -> p k c", k=4)

        def w_lo(m):
            return ring_lo[:, MOE_SLOTS[m % NSLOT], :, :]

        def units(i, m, half=1):
            return i * 24 + (2 * m + half + 1)

        def product_done(eng, i, m):
            eng.wait_ge(unit_used, units(i, m))

        @block.sync
        def _(eng):
            def load_mod(i, s):
                eng.dma_start(slot(s).rearrange("p (k c) -> p k c", k=2),
                              w_mod[:, 2 * s:2 * s + 2, bass.ds(i * (2 * D), 2 * D)]).then_inc(mod_loaded[s], 16)

            def load_a(i, kind):
                eng.dma_start(wa(kind), w_in[:, :, bass.ds(i * 256 + kind * D, 256)]).then_inc(wa_loaded[kind], 16)

            def load_gates(i):
                for t in range(2):
                    for half in range(2):
                        eng.dma_start(gw[64 * half:64 * half + 64, t, :, 64 * half:64 * half + 64],
                                      gate_w[:, :, bass.ds(i * 4 + (2 * t + half), 1), :].rearrange("i g h j -> i g (h j)"))\
                            .then_inc(gw_loaded, 16)

            for s in range(4):
                load_mod(0, s)
            with eng.Fori(0, 2) as i:
                for s in range(4):
                    eng.wait_ge(mod_used[s], i + 1)
                    load_mod(i + 1, s)
            eng.wait_ge(mod_used[0], 3)
            eng.wait_ge(mod_used[1], 3)
            for kind in range(3):
                load_a(0, kind)
            eng.wait_ge(consts_ready, 4)
            load_gates(0)
            with eng.Fori(0, 3) as i:
                for kind, done in enumerate((xr_done, xv_done, xg_done)):
                    eng.wait_ge(done, i * 2 + 2)
                    load_a(i + 1, kind)
                eng.wait_ge(gate_done, i * 8 + 8)
                load_gates(i + 1)
            for done in (xr_done, xv_done, xg_done):
                eng.wait_ge(done, 8)

            def load_b(i, p):
                at = i * 512 + p * 256
                for m, (w, off) in enumerate(((w_in, 3 * D), (w_in, 4 * D), (w_ro, 0), (w_co, 0))):
                    eng.dma_start(wb(p, m), w[:, :, bass.ds(at + off, 256)]).then_inc(wb_loaded[p], 16)

            load_b(0, 0)
            eng.wait_ge(lru_done, 4)
            load_b(0, 1)
            eng.wait_ge(last_ready, 1)
            eng.dma_start(a["new_state"][0, 0].rearrange("s (k p) -> (s k) p", p=P), last_t[:, :]).then_inc(state_stored, 16)
            eng.wait_ge(pab_done, NT)
            load_b(1, 0)
            eng.wait_ge(pab_done, 2 * NT)
            load_b(1, 1)
            eng.wait_ge(pab_done, 3 * NT)
            for h in range(2):
                eng.dma_start(slot(h).rearrange("p (k c) -> p k c", k=KD), w_out[:, :, 512 * h:512 * h + 512])\
                    .then_inc(wc_loaded[h], 16)
            eng.wait_ge(pab_done, 4 * NT)
            eng.wait_ge(mod_row_stored, 16 * 3)
            for s in range(2):
                eng.dma_start(g1b[:, s, :], mod_rows[s:s + 1, 2 * D:3 * D].broadcast_to([P, D])).then_inc(rows_loaded, 16)
            eng.dma_start(bias1, a["b_mod"][0:1, 2 * D:3 * D].broadcast_to([P, D])).then_inc(rows_loaded, 16)
            eng.dma_start(bias2, a["b_mod"][0:1, 5 * D:6 * D].broadcast_to([P, D])).then_inc(rows_loaded, 16)
            eng.dma_start(g2b[0:CAP_S, :], mod_rows[1:2, 5 * D:6 * D].broadcast_to([CAP_S, D])).then_inc(rows_loaded, 16)
            eng.dma_start(g2b[CAP_S:CAP, :], mod_rows[0:1, 5 * D:6 * D].broadcast_to([CAP_P, D])).then_inc(rows_loaded, 16)

            def load_chunk(e, m):
                eng.dma_start(chunk(m), chunk_source(e, m)).then_inc(w_loaded[MOE_SLOTS[m % NSLOT]], 16)

            load_chunk(0, 0)
            load_chunk(0, 1)
            eng.wait_ge(wo_done, 2 * NT)
            load_chunk(0, 2)
            load_chunk(0, 3)
            eng.wait_ge(vt_turned, NT)
            eng.wait_ge(rows_stored, 16 * 2 * NT)
            load_chunk(0, 4)
            load_chunk(0, 5)
            eng.dma_start(gf, a["final_norm_g"].rearrange("(o d) -> o d", o=1).broadcast_to([P, D])).then_inc(gf_loaded, 16)
            with eng.Fori(0, E - 1) as i:
                for n in range(12):
                    m = (n + NSLOT) % 12
                    e = i + (n + NSLOT) // 12
                    if m < 8:
                        w = (w_e1, w_e3)[m // 2 % 2][bass.ds(e, 1), :, :, :].rearrange("e p k f -> p (e k) f")
                        src = w[:, 4 * (m % 2):4 * (m % 2) + 4, (m // 4) * D:(m // 4 + 1) * D]
                    else:
                        src = w_e2_rows[:, bass.ds(e * 4 + (m - 8), 1), :, :].rearrange("p q k f -> p (q k) f")
                    product_done(eng, i, n)
                    eng.dma_start(chunk(m), src).then_inc(w_loaded[MOE_SLOTS[m % NSLOT]], 16)
            for m in range(NSLOT, 12):
                product_done(eng, E - 1, m - NSLOT)
                load_chunk(E - 1, m)
            eng.wait_ge(scattered, 16 * E)
            for t in range(NT):
                eng.dma_start(xr[:, t, :], acc_dram[P * t:P * t + P, :]).then_inc(fin_loaded[t], 16)
            for t in range(NT):
                eng.wait_ge(out_ready, t + 1)
                eng.dma_start(a["y_prompt"][0] if t == 0 else a["y_sample"][0].rearrange("(t p) d -> t p d", p=P)[t - 1],
                              xr[:, t, :]).then_inc(out_stored, 16)
            eng.wait_ge(out_stored, 16 * NT)
            eng.wait_ge(state_stored, 16)

        @block.gpsimd
        def _(eng):
            step = Steps(eng, pool_step)
            step.did(eng.memset(ident[:, :], 0.0))
            step.wait()
            eng.affine_select(out=ident[:, :], in_=ident[:, :], compare_op=ALU.not_equal, fill=1.0,
                              base=0, pattern=[[-1, P]], channel_multiplier=1).then_inc(consts_ready, 1)
            eng.memset(ones[:, :], 1.0).then_inc(consts_ready, 1)
            eng.memset(xpad[:, :, :], 0.0).then_inc(consts_ready, 1)
            eng.memset(gw[:, :, :, :], 0.0).then_inc(consts_ready, 1)

            with eng.Fori(0, 3) as i:
                eng.wait_ge(mod_row_ready, i + 1)
                eng.dma_start(mod_rows[:, bass.ds(i * (2 * D), 2 * D)], mod_row).then_inc(mod_row_stored, 16)

            with eng.Fori(0, 4) as i:
                for n in range(4):
                    t, d = n // 2, n % 2
                    eng.wait_ge(gate_sig, i * 8 + (2 * n + 2))
                    eng.wait_ge(xc_ready, i * 2 + (t + 1))
                    eng.tensor_tensor(lr_i[:, t, d, :], lr_i[:, t, d, :], xc[:, t, :], ALU.mult).then_inc(ix_ready, 1)
                for t in range(2):
                    eng.wait_ge(conv_done, i * 2 + (t + 1))
                    eng.tensor_copy(cu[:, bass.ds(i * 2 + t, 1), :], cv[:, t:t + 1, :]).then_inc(cv_copied, 1)

            def gather(col):
                step.did(eng.tensor_copy(idx_g[:, :], idx_t[:, bass.ds(col, 1)]))
                step.wait()
                eng.indirect_dma_start(out=xe, out_offset=None, in_=xn_dram,
                                       in_offset=bass.IndirectOffsetOnAxis(ap=idx_g[:, 0:1], axis=0))\
                    .then_inc(xe_loaded, 16)

            eng.wait_ge(idx_ready, 3)
            eng.wait_ge(rows_stored, 16 * 2 * NT)
            gather(0)
            step.restart()
            with eng.Fori(0, E) as i:
                eng.wait_ge(xe_turned, i + 1)
                eng.wait_ge(xe_loaded, i * 16 + 16)
                gather(i + 1)
                step.did(eng.tensor_copy(idx_s[:, :], idx_t[:, bass.ds(i, 1)]))
                step.wait()
                eng.wait_ge(ye_ready, i + 1)
                eng.indirect_dma_start(out=acc_dram, out_offset=bass.IndirectOffsetOnAxis(ap=idx_s[:, 0:1], axis=0),
                                       in_=ye, in_offset=None, compute_op=ALU.add).then_inc(scattered, 16)
                step.restart()
                eng.wait_ge(scattered, i * 16 + 16)

        @block.scalar
        def _(eng):
            def vec_in(rows, tile, src):
                n = src.shape[0]
                eng.dma_start(vecs[rows:rows + n, tile, :], src).then_inc(vec_loaded, 16)

            def rows_of(v):
                return v.rearrange("(r p) -> r p", p=P)

            vec_in(C_C, 0, rows_of(a["c"][0]))
            vec_in(C_CTX, 0, rows_of(a["c_ctx"]))
            vec_in(C_BMOD, 0, rows_of(a["b_mod"][0]))
            vec_in(C_N1, 0, rows_of(a["norm1_g"][0]))
            vec_in(C_N2, 0, rows_of(a["norm2_g"][0]))
            vec_in(C_LNG, 0, rows_of(a["conv_ln_g"][0]))
            vec_in(C_LNB, 0, rows_of(a["conv_ln_b"][0]))
            vec_in(C_TAB, 0, a["state_rglru"][0, 0].rearrange("s (r p) -> (s r) p", p=P))
            vec_in(C_TAB + 8 * G_RCB, 0, rows_of(a["rnn_conv_b"][0]))
            vec_in(C_TAB + 8 * G_CDB, 0, rows_of(a["conv_dw_b"][0]))
            vec_in(0, 1, a["rnn_conv_w"][0].rearrange("s (r p) -> (s r) p", p=P))
            vec_in(32, 1, a["rnn_gate_b"][0].rearrange("s g (r p) -> (s g r) p", p=P))
            vec_in(64, 1, a["rnn_lambda"][0].rearrange("s (r p) -> (s r) p", p=P))
            taps = a["conv_dw_w"][0].rearrange("s (r p) -> (s r) p", p=P)
            vec_in(0, 2, taps[0:P])
            vec_in(0, 3, taps[P:8 * TAPS31])
            for t in range(NT):
                eng.dma_start(xr[:, t, :], x_prompt if t == 0 else x_sample[t - 1]).then_inc(x_loaded, 16)
            eng.dma_start(wr[:, :, :], w_router).then_inc(wr_loaded, 16)
            step = Steps(eng, act_step)

            eng.wait_ge(cols_ready, 1)
            for s, c in enumerate((C_CTX, C_C)):
                eng.activation(silu_c[:, :, s], cols[:, c:c + KD], ACT.Silu).then_inc(silu_ready, 1)
            lam = cols[:, C_TAB + 8 * G_LAM:C_TAB + 8 * G_LAM + 16]
            step.did(eng.activation(sp[:, 0, :], lam, ACT.Abs))
            step.wait()
            eng.activation(sp[:, 1, :], sp[:, 0, :], ACT.Exp, scale=-1.0).then_inc(exp_lam_ready, 1)
            eng.wait_ge(x_loaded, 16 * NT)
            for t in range(NT):
                if t:
                    eng.wait_ge(ssq_ready, t)
                eng.activation(xn1[:, t, :], xr[:, t, :], ACT.Square, accum_out=rstat[:, 0, t:t + 1]).then_inc(ssq_ready, 1)
            eng.wait_ge(ms_ready, 1)
            eng.activation(rstat[:, 2, :], rstat[:, 1, :], ACT.Sqrt).then_inc(root_ready, 1)
            eng.wait_ge(r_ready, 1)
            for t in range(NT):
                eng.activation(xn1[:, t, :], xr[:, t, :], ACT.Copy, scale=rstat[:, 3, t:t + 1]).then_inc(xn1_ready, 1)
            eng.wait_ge(a12_ready, 2)
            for k in range(KD):
                eng.wait_ge(xt_turned, k + 1)
                eng.activation(uT[:, k, 0:NP], ps[:, 2 * (k % 4) + 1, 0:NP], ACT.Identity,
                               scale=a1[:, k, 0:1], bias=modc[:, k, 0:1]).then_inc(ut_prompt, 1)

            step.restart()
            eng.wait_ge(consts_ready, 4)
            with eng.Fori(0, 4) as i:
                for t in range(2):
                    eng.wait_ge(xr_done, i * 2 + (t + 1))
                    b = 2 * t
                    eng.activation(xpad[:, t, 2:2 + NP], ps[:, b, 0:NP], ACT.Copy)
                    eng.activation(xpad[:, t, S0 + 2:S0 + 2 + HALF - NP], ps[:, b, NP:HALF], ACT.Copy)
                    eng.activation(xpad[:, t, S0 + 2 + HALF - NP:S0 + 2 + NS], ps[:, b + 1, 0:HALF], ACT.Copy)\
                        .then_inc(xr_copied, 1)
                eng.wait_ge(cur_ready, i + 1)
                eng.wait_ge(xr_copied, i * 2 + 2)
                for t in range(2):
                    eng.activation(xc[:, t, :], xpad[:, t, 0:LX], ACT.Identity, scale=cur[:, G_RCW, t:t + 1],
                                   bias=cur[:, G_RCB, t:t + 1]).then_inc(tap0_ready, 1)
                for t in range(2):
                    eng.wait_ge(xg_done, i * 2 + (t + 1))
                    b = (6, 2)[t]
                    eng.activation(sg[:, t, :].rearrange("p (h c) -> p h c", h=2), ps[:, b:b + 2, 0:HALF], ACT.Sigmoid)\
                        .then_inc(xg_sig, 1)
                for n in range(8):
                    t, d, g = n // 4, n // 2 % 2, n % 2
                    b = 2 * ((6 + n) % 4)
                    dst = (lr_r, lr_i)[g][:, t, d, :].rearrange("p (h c) -> p h c", h=2)
                    eng.wait_ge(gate_done, i * 8 + (n + 1))
                    eng.activation(dst, ps[:, b:b + 2, 0:LX // 2], ACT.Sigmoid,
                                   bias=cur[:, G_GB + 2 * d + g, t:t + 1]).then_inc(gate_sig, 1)
                eng.wait_ge(gate_sig, i * 8 + 8)
                for n in range(4):
                    t, d = n // 2, n % 2
                    step.did(eng.activation(lr_a[:, t, d, :], lr_r[:, t, d, :], ACT.Exp, scale=cur[:, G_NLAM + d, t:t + 1]))
                    step.did(eng.activation(lr_r[:, t, d, :], lr_r[:, t, d, :], ACT.Tanh, scale=cur[:, G_LAM + d, t:t + 1]))
                    step.wait(1)
                    eng.activation(lr_q[:, t, d, :], lr_a[:, t, d, :], ACT.Square).then_inc(decay_sq, 1)
                for n in range(4):
                    t, d = n // 2, n % 2
                    eng.wait_ge(in_sq, i * 4 + (n + 1))
                    eng.activation(lr_q[:, t, d, :], lr_q[:, t, d, :], ACT.Sqrt).then_inc(in_root, 1)
                step.restart()

            for k in range(KD):
                eng.wait_ge(ln_centred, k + 1)
                if k >= 2:
                    eng.wait_ge(ln_sq_used, k - 1)
                eng.activation(ln_sq[:, k % 2, :], cu[:, k, :], ACT.Square).then_inc(ln_squared, 1)
            eng.wait_ge(ln_var, 1)
            eng.activation(ln_rs, ln_rs, ACT.Sqrt).then_inc(ln_root, 1)
            for k in range(KD):
                eng.wait_ge(ln_scaled, k + 1)
                eng.activation(cu[:, k, :], cu[:, k, :], ACT.Silu, scale=cols[:, C_LNG + k:C_LNG + k + 1],
                               bias=cols[:, C_LNB + k:C_LNB + k + 1]).then_inc(yb_ready, 1)

            with eng.Fori(0, 2) as i:
                for s in range(2 * NT):
                    g = s % 2
                    eng.wait_ge(gab_done, i * (2 * NT) + (s + 1))
                    eng.activation(sg_ab(g), ps[:, 4 * g:4 * g + 2, 0:256], ACT.Sigmoid).then_inc(gab_sig, 1)
            for k in range(KD):
                eng.wait_ge(mt_turned, k + 1)
                eng.activation(mT[:, k, 0:NP], ps[:, 2 * (k % 4) + 1, 0:NP], ACT.Copy).then_inc(mt_prompt, 1)

            for t in range(NT):
                eng.wait_ge(x2_ready, 2 * (t + 1))
                if t:
                    eng.wait_ge(xn2_ready, t)
                eng.activation(xn2[:, t, :], xr[:, t, :], ACT.Square, accum_out=rstat[:, 0, t:t + 1]).then_inc(ssq2_ready, 1)
                eng.wait_ge(ms2_ready, t + 1)
                eng.activation(rstat[:, 2, t:t + 1], rstat[:, 1, t:t + 1], ACT.Sqrt).then_inc(root2_ready, 1)
                eng.wait_ge(r2_ready, t + 1)
                eng.activation(xn2[:, t, :], xr[:, t, :], ACT.Copy, scale=rstat[:, 3, t:t + 1]).then_inc(xn2_ready, 1)
                eng.wait_ge(xn2_ready, t + 1)
                eng.dma_start(xn_dram[P * t:P * t + P, :], xn2[:, t, :]).then_inc(rows_stored, 16)
                eng.dma_start(acc_dram[P * t:P * t + P, :], xr[:, t, :]).then_inc(rows_stored, 16)
            for t in range(NT):
                eng.wait_ge(vt_turned, t + 1)
                for k in range(4, KD):
                    ins = eng.activation(vT[:, k, P * t:P * t + P], ps[:, 2 * (t % 2) + 1, P * (k - 4):P * (k - 3)], ACT.Identity,
                                         scale=a2[:, k, min(t, 1):min(t, 1) + 1], bias=modc[:, 24 + k, min(t, 1):min(t, 1) + 1])
                ins.then_inc(vt_act, 1)
            for t in range(NT):
                eng.wait_ge(max_ready, 1)
                eng.activation(soft[:, t, :], ps[:, 5, 16 * t:16 * t + 16], ACT.Exp, bias=sstat[:, 0, t:t + 1],
                               accum_out=sstat[:, 1, t:t + 1]).then_inc(exp_ready, 1)

            def hi_piece(i, m, free):
                eng.wait_ge(w_loaded[MOE_SLOTS[m % NSLOT]], i * 32 + 16 * (m // NSLOT + 1))
                for half in range(2):
                    if free is not None:
                        eng.wait_ge(unit_used, units(*free, half))
                    eng.activation(w_hi[m % 2][:, 2 * half:2 * half + 2, :], chunk(m)[:, 2 * half:2 * half + 2, :],
                                   ACT.Copy).then_inc(unit_hi, 1)

            def hi_xe(n):
                eng.wait_ge(xe_modulated, n)
                eng.activation(xe_hi[:, :, :], xeT[:, :, :], ACT.Copy).then_inc(xe_hi_ready, 1)

            def swish(i, half):
                product_done(eng, i, 4 * half + 1)
                eng.activation(hs[:, half * D:(half + 1) * D].rearrange("c (b f) -> c b f", b=2), ps[0:CAP, 0:2, :],
                               ACT.Silu).then_inc(h1_silu, 1)

            def hi_h(i, half):
                eng.wait_ge(h_turned, i * 2 + (half + 1))
                eng.activation(h_hi[:, 8 * half:8 * half + 8, :].rearrange("p (b k) c -> p b (k c)", b=2),
                               ps[:, 6:8, 0:4 * CAP], ACT.Copy).then_inc(h_hi_ready, 1)

            def act_expert(i, final):
                for m in range(2, 12):
                    hi_piece(i, m, (i, m - 2))
                    if m == 3:
                        swish(i, 0)
                    if m == 7:
                        swish(i, 1)
                        hi_h(i, 0)
                    if m == 10:
                        hi_h(i, 1)
                hi_xe(i + 2)
                if not final:
                    for m in range(2):
                        hi_piece(i + 1, m, (i, m + 10))

            eng.wait_ge(logit_done, NT)
            eng.wait_ge(rows_stored, 16 * 2 * NT)
            for m in range(2):
                hi_piece(0, m, None)
            hi_xe(1)
            with eng.Fori(0, E - 1) as i:
                act_expert(i, False)
            act_expert(E - 1, True)

            for t in range(NT):
                eng.wait_ge(fin_loaded[t], 16)
                eng.activation(xn1[:, t % 2, :], xr[:, t, :], ACT.Square, accum_out=rstat[:, 0, t:t + 1]).then_inc(fin_ssq, 1)
                eng.wait_ge(fin_ms, t + 1)
                eng.activation(rstat[:, 2, t:t + 1], rstat[:, 1, t:t + 1], ACT.Sqrt).then_inc(fin_root, 1)

        @block.vector
        def _(eng):
            step = Steps(eng, dve_step)
            eng.wait_ge(cols_turned, 1)
            eng.tensor_copy(cols[:, 0:C_TAB + 8 * G_NLAM], ps[:, 0, 0:C_TAB + 8 * G_NLAM]).then_inc(cols_ready, 1)
            lam = cols[:, C_TAB + 8 * G_LAM:C_TAB + 8 * G_LAM + 16]
            nlam = cols[:, C_TAB + 8 * G_NLAM:C_TAB + 8 * G_NLAM + 16]
            z, s, s2, poly = sp[:, 1, :], sp[:, 2, :], sp[:, 3, :], sp[:, 4, :]
            eng.wait_ge(exp_lam_ready, 1)
            step.did(eng.tensor_scalar(s2, z, 2.0, None, ALU.add))
            step.wait()
            step.did(eng.reciprocal(poly, s2))
            step.wait()
            step.did(eng.tensor_tensor(s, z, poly, ALU.mult))
            step.wait()
            step.did(eng.tensor_tensor(s2, s, s, ALU.mult))
            step.wait()
            step.did(eng.tensor_scalar(poly, s2, 1.0 / 17, 1.0 / 15, ALU.mult, ALU.add))
            for n in range(6, -1, -1):
                step.wait()
                step.did(eng.tensor_tensor(poly, poly, s2, ALU.mult))
                step.wait()
                step.did(eng.tensor_scalar(poly, poly, 1.0 / (2 * n + 1), None, ALU.add))
            step.wait()
            step.did(eng.tensor_tensor(poly, poly, s, ALU.mult))
            step.did(eng.tensor_scalar(s2, lam, -1.0, 0.0, ALU.mult, ALU.max))
            step.wait()
            step.did(eng.scalar_tensor_tensor(out=s, in0=poly, scalar=2.0, in1=s2, op0=ALU.mult, op1=ALU.add))
            step.wait()
            step.did(eng.tensor_scalar(lam, s, RG_C, None, ALU.mult))
            eng.tensor_scalar(nlam, s, -RG_C, None, ALU.mult).then_inc(decay_ready, 1)

            def inverse_root(ssq_sem, n, ms_sem, root_sem, t0, t1):
                eng.wait_ge(ssq_sem, n)
                eng.tensor_scalar(rstat[:, 1, t0:t1], rstat[:, 0, t0:t1], 1.0 / D, EPS, ALU.mult, ALU.add).then_inc(ms_sem, 1)

            inverse_root(ssq_ready, NT, ms_ready, root_ready, 0, NT)
            eng.wait_ge(root_ready, 1)
            eng.reciprocal(rstat[:, 3, :], rstat[:, 2, :]).then_inc(r_ready, 1)

            with eng.Fori(0, 3) as i:
                eng.wait_ge(mod_used[3], i + 1)
                eng.tensor_copy(mod_row.rearrange("s (b c) -> s b c", b=4), ps[0:2, 1:5, :]).then_inc(mod_row_ready, 1)
                eng.wait_ge(mod_turned, i + 1)
                src = ps[:, 5, 0:32].rearrange("p (j s) -> p j s", s=2)
                bias = cols[:, bass.ds(i * 16, 16)].rearrange("p (j o) -> p j o", o=1)
                for h in range(2):
                    ins = eng.tensor_tensor(modc[:, bass.ds(i * 16, 16), h:h + 1], src[:, :, h:h + 1], bias, ALU.add)
                ins.then_inc(modc_ready, 1)
                eng.wait_ge(mod_row_stored, i * 16 + 16)
            eng.wait_ge(modc_ready, 3)
            for n, (dst, v, c) in enumerate(((a1, 1, C_N1), (a2, 4, C_N2))):
                for s in range(2):
                    ins = eng.scalar_tensor_tensor(out=dst[:, :, s], in0=modc[:, v * KD:v * KD + KD, s], scalar=1.0,
                                                   in1=cols[:, c:c + KD], op0=ALU.add, op1=ALU.mult)
                    if s == 0:
                        step.did(ins)
                ins.then_inc(a12_ready, 1)
            eng.wait_ge(a12_ready, 2)
            for k in range(KD):
                eng.wait_ge(xt_turned, k + 1)
                eng.tensor_scalar(uT[:, k, NP:N], ps[:, 2 * (k % 4), :], a1[:, k, 1:2], modc[:, k, 1:2], ALU.mult, ALU.add)\
                    .then_inc(ut_sample, 1)
            eng.wait_ge(decay_ready, 1)

            table = cols[:, C_TAB:NCOLS].rearrange("p (g c) -> p g c", c=KD)
            ranges = conv_ranges()
            step.restart()
            with eng.Fori(0, 4) as i:
                eng.tensor_copy(cur[:, :, :], table[:, :, bass.ds(i * 2, 2)]).then_inc(cur_ready, 1)
                eng.wait_ge(cur_ready, i + 1)
                for k in range(1, TAPS4):
                    for t in range(2):
                        if k == 1:
                            eng.wait_ge(tap0_ready, i * 2 + (t + 1))
                        else:
                            step.wait(0 if k == TAPS4 - 1 and t == 1 else 1)
                        ins = eng.scalar_tensor_tensor(out=xc[:, t, :], in0=xpad[:, t, k:k + LX], scalar=cur[:, G_RCW + k, t:t + 1],
                                                       in1=xc[:, t, :], op0=ALU.mult, op1=ALU.add)
                        if k < TAPS4 - 1:
                            step.did(ins)
                        else:
                            ins.then_inc(xc_ready, 1)
                for t in range(2):
                    b = (4, 0)[t]
                    eng.wait_ge(xv_done, i * 2 + (t + 1))
                    eng.wait_ge(xg_sig, i * 2 + (t + 1))
                    eng.tensor_tensor(glu[:, t, :].rearrange("p (h c) -> p h c", h=2), ps[:, b:b + 2, 0:HALF],
                                      sg[:, t, :].rearrange("p (h c) -> p h c", h=2), ALU.mult).then_inc(glu_ready, 1)
                eng.wait_ge(glu_ready, i * 2 + 2)
                for t in range(2):
                    step.did(eng.tensor_scalar(cv[:, t, :], glu[:, t, :], cur[:, G_CDW + MID, t:t + 1], cur[:, G_CDB, t:t + 1],
                                               ALU.mult, ALU.add))
                    behind = {True: step.n, False: step.n}
                    for n, (k, lo, hi, s) in enumerate(ranges):
                        eng.wait_ge(dve_step, behind[lo < NP])
                        ins = eng.scalar_tensor_tensor(out=cv[:, t, lo:hi], in0=glu[:, t, lo + s:hi + s],
                                                       scalar=cur[:, G_CDW + k, t:t + 1], in1=cv[:, t, lo:hi],
                                                       op0=ALU.mult, op1=ALU.add)
                        if n < len(ranges) - 1:
                            step.did(ins)
                            behind[lo < NP] = step.n
                        else:
                            ins.then_inc(conv_done, 1)
                for n in range(4):
                    t, d = n // 2, n % 2
                    eng.wait_ge(decay_sq, i * 4 + (n + 1))
                    eng.scalar_tensor_tensor(out=lr_q[:, t, d, :], in0=lr_q[:, t, d, :], scalar=1.0, in1=lr_r[:, t, d, :],
                                             op0=ALU.add, op1=ALU.mult).then_inc(in_sq, 1)
                for n in range(4):
                    t, d = n // 2, n % 2
                    eng.wait_ge(in_root, i * 4 + (n + 1))
                    eng.wait_ge(ix_ready, i * 4 + (n + 1))
                    step.did(eng.tensor_tensor(lr_q[:, t, d, :], lr_q[:, t, d, :], lr_i[:, t, d, :], ALU.mult))
                step.wait()
                for n in range(4):
                    t, d = n // 2, n % 2
                    for lo, hi, h0 in ((0, NP, 0.0), (S0, S0 + NS, cur[:, G_STATE + d, t:t + 1])):
                        h, av, bv = lr_r[:, t, d, lo:hi], lr_a[:, t, d, lo:hi], lr_q[:, t, d, lo:hi]
                        if d:
                            h, av, bv = h[:, ::-1], av[:, ::-1], bv[:, ::-1]
                        step.did(eng.tensor_tensor_scan(out=h, data0=av, data1=bv, initial=h0, op0=ALU.mult, op1=ALU.add))
                step.wait()
                for t in range(2):
                    for lo, to, n in ((0, 0, NP), (S0, NP, NS)):
                        step.did(eng.tensor_tensor(ya[:, bass.ds(i * 2 + t, 1), to:to + n].rearrange("p a c -> p (a c)"),
                                                   lr_r[:, t, 0, lo:lo + n], lr_r[:, t, 1, lo:lo + n], ALU.add))
                step.did(eng.tensor_copy(last[:, 0, bass.ds(i * 2, 2)], lr_r[:, :, 0, NP - 1]))
                eng.wait_ge(cv_copied, i * 2 + 2)
                eng.tensor_copy(last[:, 1, bass.ds(i * 2, 2)], lr_r[:, :, 1, 0]).then_inc(lru_done, 1)
                step.restart()
            eng.wait_ge(last_turned, 1)
            eng.tensor_copy(last_t[:, :], ps[0:16, 7, 0:P]).then_inc(last_ready, 1)

            eng.wait_ge(ln_summed, 1)
            step.did(eng.tensor_scalar(ln_mu.rearrange("p (h c) -> p h c", h=2), ps[:, 0:2, 0:HALF], -1.0 / D, None, ALU.mult))
            step.wait()
            for k in range(KD):
                eng.tensor_tensor(cu[:, k, :], cu[:, k, :], ln_mu, ALU.add).then_inc(ln_centred, 1)
            eng.wait_ge(ln_sq_used, KD)
            eng.tensor_scalar(ln_rs.rearrange("p (h c) -> p h c", h=2), ps[:, 2:4, 0:HALF], 1.0 / D, EPS, ALU.mult, ALU.add)\
                .then_inc(ln_var, 1)
            eng.wait_ge(ln_root, 1)
            step.did(eng.reciprocal(ln_rs, ln_rs))
            step.wait()
            eng.wait_ge(ln_centred, KD)
            for k in range(KD):
                eng.tensor_tensor(cu[:, k, :], cu[:, k, :], ln_rs, ALU.mult).then_inc(ln_scaled, 1)

            step.restart()
            with eng.Fori(0, 2) as i:
                for s in range(2 * NT):
                    p, t, g = s // NT, s % NT, s % 2
                    eng.wait_ge(gab_sig, i * (2 * NT) + (s + 1))
                    eng.wait_ge(pab_done, i * (2 * NT) + (s + 1))
                    step.did(eng.tensor_tensor(sg_ab(g), sg_ab(g), ps[:, 4 * g + 2:4 * g + 4, 0:256], ALU.mult))
                    step.wait()
                    eng.tensor_tensor(merged[:, t, bass.ds(i * 512 + p * 256, 256)], sg_ab(g)[:, 0, :], sg_ab(g)[:, 1, :], ALU.add)\
                        .then_inc(merged_ready, 1)
                step.restart()
            for k in range(KD):
                eng.wait_ge(mt_turned, k + 1)
                eng.tensor_copy(mT[:, k, NP:N], ps[:, 2 * (k % 4), :]).then_inc(mt_sample, 1)
            eng.wait_ge(rows_loaded, 16 * 6)
            for s in range(2):
                step.did(eng.tensor_tensor(g1b[:, s, :], g1b[:, s, :], bias1, ALU.add))
            eng.tensor_tensor(g2b, g2b, bias2[0:CAP, :], ALU.add).then_inc(rows_ready, 1)
            step.wait()

            def residual(t):
                for h in range(2):
                    n = 2 * t + h
                    eng.wait_ge(wo_done, n + 1)
                    step.did(eng.tensor_tensor(prod[:, h, :], ps[:, n % 8, :], g1b[:, min(t, 1), 512 * h:512 * h + 512], ALU.mult))
                    step.wait()
                    eng.tensor_tensor(xr[:, t, 512 * h:512 * h + 512], xr[:, t, 512 * h:512 * h + 512], prod[:, h, :], ALU.add)\
                        .then_inc(x2_ready, 1)
                inverse_root(ssq2_ready, t + 1, ms2_ready, root2_ready, t, t + 1)
                eng.wait_ge(root2_ready, t + 1)
                eng.reciprocal(rstat[:, 3, t:t + 1], rstat[:, 2, t:t + 1]).then_inc(r2_ready, 1)

            for t in range(NT):
                residual(t)
            for t in range(NT):
                eng.wait_ge(vt_turned, t + 1)
                for k in range(4):
                    ins = eng.tensor_scalar(vT[:, k, P * t:P * t + P], ps[:, 2 * (t % 2), P * k:P * k + P],
                                            a2[:, k, min(t, 1):min(t, 1) + 1], modc[:, 24 + k, min(t, 1):min(t, 1) + 1],
                                            ALU.mult, ALU.add)
                ins.then_inc(vt_dve, 1)
            for t in range(NT):
                eng.wait_ge(logit_done, t + 1)
                eng.tensor_copy(lg[:, P * t:P * t + P], ps[0:E, 4, P * (t % 4):P * (t % 4) + P]).then_inc(lg_ready, 1)
            eng.wait_ge(lg_turned, 1)
            step.did(eng.tensor_reduce(sstat[:, 2, :], ps[:, 5, 0:16 * NT].rearrange("p (t e) -> p t e", e=E), AX.X, ALU.max))
            step.wait()
            eng.tensor_scalar(sstat[:, 0, :], sstat[:, 2, :], -1.0, None, ALU.mult).then_inc(max_ready, 1)
            eng.wait_ge(exp_ready, NT)
            step.did(eng.reciprocal(sstat[:, 2, :], sstat[:, 1, :]))
            step.wait()
            for t in range(NT):
                eng.tensor_scalar(soft[:, t, :], soft[:, t, :], sstat[:, 2, t:t + 1], None, ALU.mult).then_inc(soft_ready, 1)
            eng.wait_ge(soft_turned, NT)
            step.did(eng.tensor_copy(lg[:, 0:NP], ps[0:E, 6, 0:NP]))
            step.did(eng.tensor_copy(lg[:, NP:N], ps[0:E, 7, :]))
            step.wait()
            for rows, first, rounds in ((lg[:, NP:N], 0, CAP_S // 8), (lg[:, 0:NP], CAP_S, CAP_P // 8)):
                for r in range(rounds):
                    best = gates_e[:, first + 8 * r:first + 8 * r + 8]
                    step.did(eng.max(best, rows))
                    step.wait()
                    step.did(eng.max_index(idx[:, first + 8 * r:first + 8 * r + 8], best, rows))
                    if r < rounds - 1:
                        step.wait()
                        step.did(eng.match_replace(rows, best, rows, -1.0))
                        step.wait()
            step.wait()
            step.did(eng.tensor_scalar(idx_f[:, 0:CAP_S], idx[:, 0:CAP_S], float(NP), None, ALU.add))
            eng.tensor_copy(idx_f[:, CAP_S:CAP], idx[:, CAP_S:CAP]).then_inc(top_ready, 1)
            eng.wait_ge(top_turned, 1)
            eng.tensor_copy(idx_t[:, 0:E], ps[0:CAP, 0, 0:E]).then_inc(idx_ready, 1)
            eng.tensor_copy(idx_t[:, E:E + 1], ps[0:CAP, 0, E - 1:E]).then_inc(idx_ready, 1)
            eng.tensor_copy(gate_t[:, :], ps[0:CAP, 0, E:2 * E]).then_inc(idx_ready, 1)
            eng.wait_ge(idx_ready, 3)
            eng.wait_ge(rows_ready, 1)

            def modulate_xe():
                for k in range(KD):
                    b, c = 6 + k // 4, CAP * (k % 4)
                    for s, lo, hi in ((1, 0, CAP_S), (0, CAP_S, CAP)):
                        ins = eng.tensor_scalar(xeT[:, k, lo:hi], ps[:, b, c + lo:c + hi], a2[:, k, s:s + 1],
                                                modc[:, 24 + k, s:s + 1], ALU.mult, ALU.add)
                ins.then_inc(xe_modulated, 1)

            def split_piece(i, m):
                for half in range(2):
                    w = chunk(m)[:, 2 * half:2 * half + 2, :]
                    eng.wait_ge(unit_hi, units(i, m, half))
                    eng.tensor_tensor(w_lo(m)[:, 2 * half:2 * half + 2, :], w,
                                      w_hi[m % 2][:, 2 * half:2 * half + 2, :].bitcast(F32), ALU.subtract)\
                        .then_inc(unit_split, 1)

            def split_xe(n):
                eng.wait_ge(xe_turned, n)
                modulate_xe()
                eng.wait_ge(xe_hi_ready, n)
                eng.tensor_tensor(xe_lo[:, :, :], xeT[:, :, :], xe_hi[:, :, :].bitcast(F32), ALU.subtract).then_inc(xeT_ready, 1)

            def hidden(i, half):
                eng.wait_ge(h1_silu, i * 2 + (half + 1))
                product_done(eng, i, 4 * half + 3)
                v = hs[:, half * D:(half + 1) * D].rearrange("c (b f) -> c b f", b=2)
                eng.tensor_tensor(v, v, ps[0:CAP, 2:4, :], ALU.mult).then_inc(h_ready, 1)

            def split_h(i, half):
                eng.wait_ge(h_hi_ready, i * 2 + (half + 1))
                hi, lo = (x[:, 8 * half:8 * half + 8, :].rearrange("p (b k) c -> p b (k c)", b=2) for x in (h_hi, h_lo))
                eng.tensor_tensor(lo, ps[:, 6:8, 0:4 * CAP], hi.bitcast(F32), ALU.subtract).then_inc(hT_ready, 1)

            def output(i):
                product_done(eng, i, 11)
                gate = gate_t[:, E - 1:E] if i is E - 1 else gate_t[:, bass.ds(i, 1)]
                eng.scalar_tensor_tensor(out=ye.rearrange("c (b f) -> c b f", b=2), in0=ps[0:CAP, 4:6, :], scalar=gate,
                                         in1=g2b.rearrange("c (b f) -> c b f", b=2), op0=ALU.mult, op1=ALU.mult)\
                    .then_inc(ye_ready, 1)

            def dve_expert(i, final):
                for m in range(2, 12):
                    split_piece(i, m)
                    if m == 5:
                        hidden(i, 0)
                    if m == 7:
                        split_h(i, 0)
                    if m == 9:
                        hidden(i, 1)
                    if m == 10:
                        split_h(i, 1)
                split_xe(i + 2)
                if not final:
                    for m in range(2):
                        split_piece(i + 1, m)
                output(i)

            for m in range(2):
                split_piece(0, m)
            split_xe(1)
            with eng.Fori(0, E - 1) as i:
                dve_expert(i, False)
            dve_expert(E - 1, True)

            eng.wait_ge(gf_loaded, 16)
            for t in range(NT):
                inverse_root(fin_ssq, t + 1, fin_ms, fin_root, t, t + 1)
                eng.wait_ge(fin_root, t + 1)
                step.did(eng.reciprocal(rstat[:, 3, t:t + 1], rstat[:, 2, t:t + 1]))
                step.wait()
                eng.scalar_tensor_tensor(out=xr[:, t, :], in0=xr[:, t, :], scalar=rstat[:, 3, t:t + 1], in1=gf,
                                         op0=ALU.mult, op1=ALU.mult).then_inc(out_ready, 1)

        @block.tensor
        def _(eng):
            eng.wait_ge(consts_ready, 4)
            eng.wait_ge(vec_loaded, 16 * 15)
            for tile, rows, to in ((0, P, 0), (1, 80, P), (2, P, 208), (3, 8 * TAPS31 - P, 336)):
                ins = eng.transpose(ps[:, 0, to:to + rows], vecs[0:rows, tile, :], ident[0:rows, 0:rows])
            ins.then_inc(cols_turned, 1)

            eng.wait_ge(silu_ready, 2)
            with eng.Fori(0, 3) as i:
                for s in range(4):
                    eng.wait_ge(mod_loaded[s], i * 16 + 16)
                    w = slot(s).rearrange("p (k c) -> p k c", k=2)
                    for kk in range(2):
                        k = 2 * s + kk
                        for b in range(4):
                            ins = eng.matmul(ps[0:2, 1 + b, :], silu_c[:, k, :], w[:, kk, 512 * b:512 * b + 512],
                                             start=k == 0, stop=k == KD - 1)
                    ins.then_inc(mod_used[s], 1)
                eng.wait_ge(mod_row_ready, i + 1)
                for j in range(16):
                    ins = eng.matmul(ps[:, 5, 2 * j:2 * j + 2], mod_row[:, P * j:P * j + P], ident[0:2, 0:2], start=True, stop=True)
                ins.then_inc(mod_turned, 1)
            eng.wait_ge(modc_ready, 3)

            def turn_rows(rows, wait_rows, done, emptied):
                for k in range(KD):
                    if k >= 4:
                        for e in emptied:
                            eng.wait_ge(e, k - 3)
                    for t in range(NT):
                        if wait_rows is not None and k == 0:
                            eng.wait_ge(wait_rows, t + 1)
                        b = 2 * (k % 4) + (t == 0)
                        c = 0 if t == 0 else P * (t - 1)
                        ins = eng.transpose(ps[:, b, c:c + P], rows[:, t, P * k:P * k + P], ident[:, :])
                    ins.then_inc(done, 1)

            turn_rows(xn1, xn1_ready, xt_turned, (ut_sample, ut_prompt))
            eng.wait_ge(ut_sample, KD)
            eng.wait_ge(ut_prompt, KD)

            with eng.Fori(0, 4) as i:
                for n, (kind, t, done) in enumerate(((0, 0, xr_done), (0, 1, xr_done), (1, 0, xv_done), (2, 0, xg_done),
                                                     (1, 1, xv_done), (2, 1, xg_done))):
                    if t == 0:
                        eng.wait_ge(wa_loaded[kind], i * 16 + 16)
                    if n >= 4:
                        eng.wait_ge(xr_copied, i * 2 + (n - 3))
                    b = 2 * (n % 4)
                    for k in range(KD):
                        for h in range(2):
                            ins = eng.matmul(ps[:, b + h, 0:HALF], wa(kind)[:, k, P * t:P * t + P],
                                             uT[:, k, HALF * h:HALF * h + HALF], start=k == 0, stop=k == KD - 1)
                    ins.then_inc(done, 1)
                eng.wait_ge(gw_loaded, i * 64 + 64)
                for n in range(8):
                    t, d, g = n // 4, n // 2 % 2, n % 2
                    b = 2 * ((6 + n) % 4)
                    if g == 0 and d == 0:
                        eng.wait_ge(xc_ready, i * 2 + (t + 1))
                    if n == 0 or n == 2:
                        eng.wait_ge(glu_ready, i * 2 + (n // 2 + 1))
                    if n >= 4:
                        eng.wait_ge(gate_sig, i * 8 + (n - 3))
                    for h in range(2):
                        ins = eng.matmul(ps[:, b + h, 0:LX // 2], gw[:, t, 2 * d + g, :],
                                         xc[:, t, LX // 2 * h:LX // 2 * (h + 1)], start=True, stop=True)
                    ins.then_inc(gate_done, 1)
                eng.wait_ge(gate_sig, i * 8 + 8)

            eng.wait_ge(lru_done, 4)
            eng.transpose(ps[0:16, 7, 0:P], flat(last), ident[:, :]).then_inc(last_turned, 1)
            for h in range(2):
                for k in range(KD):
                    ins = eng.matmul(ps[:, h, 0:HALF], ones[:, :], cu[:, k, HALF * h:HALF * h + HALF],
                                     start=k == 0, stop=k == KD - 1)
            ins.then_inc(ln_summed, 1)
            for k in range(KD):
                eng.wait_ge(ln_squared, k + 1)
                for h in range(2):
                    ins = eng.matmul(ps[:, 2 + h, 0:HALF], ones[:, :], ln_sq[:, k % 2, HALF * h:HALF * h + HALF],
                                     start=k == 0, stop=k == KD - 1)
                ins.then_inc(ln_sq_used, 1)
            eng.wait_ge(yb_ready, KD)
            eng.wait_ge(last_ready, 1)

            with eng.Fori(0, 2) as i:
                for s in range(2 * NT):
                    p, t, g = s // NT, s % NT, s % 2
                    if t == 0:
                        eng.wait_ge(wb_loaded[p], i * 64 + 64)
                    if s >= 2:
                        eng.wait_ge(merged_ready, i * (2 * NT) + (s - 1))
                    for m, (x, done) in enumerate(((uT, None), (uT, gab_done), (ya, None), (cu, pab_done))):
                        for k in range(KD):
                            ins = eng.matmul(ps[:, 4 * g + m, 0:256], x[:, k, P * t:P * t + P], wb(p, m)[:, k, :],
                                             start=k == 0, stop=k == KD - 1)
                        if done is not None:
                            ins.then_inc(done, 1)
                eng.wait_ge(merged_ready, i * (2 * NT) + 2 * NT)
            turn_rows(merged, None, mt_turned, (mt_sample, mt_prompt))
            eng.wait_ge(mt_sample, KD)
            eng.wait_ge(mt_prompt, KD)
            for t in range(NT):
                for h in range(2):
                    n = 2 * t + h
                    if t == 0:
                        eng.wait_ge(wc_loaded[h], 16)
                    if n >= 8:
                        eng.wait_ge(x2_ready, n - 7)
                    w = slot(h).rearrange("p (k c) -> p k c", k=KD)
                    for k in range(KD):
                        ins = eng.matmul(ps[:, n % 8, :], mT[:, k, P * t:P * t + P], w[:, k, :],
                                         start=k == 0, stop=k == KD - 1)
                    ins.then_inc(wo_done, 1)
            eng.wait_ge(x2_ready, 2 * NT)

            for t in range(NT):
                eng.wait_ge(xn2_ready, t + 1)
                if t >= 2:
                    eng.wait_ge(vt_dve, t - 1)
                    eng.wait_ge(vt_act, t - 1)
                for k in range(KD):
                    ins = eng.transpose(ps[:, 2 * (t % 2) + k // 4, P * (k % 4):P * (k % 4) + P], xn2[:, t, P * k:P * k + P],
                                        ident[:, :])
                ins.then_inc(vt_turned, 1)
            eng.wait_ge(wr_loaded, 16)
            for t in range(NT):
                eng.wait_ge(vt_dve, t + 1)
                eng.wait_ge(vt_act, t + 1)
                if t >= 1:
                    eng.wait_ge(lg_ready, t)
                for k in range(KD):
                    ins = eng.matmul(ps[0:E, 4, P * (t % 4):P * (t % 4) + P], wr[:, k, :], vT[:, k, P * t:P * t + P],
                                     start=k == 0, stop=k == KD - 1)
                ins.then_inc(logit_done, 1)
            for t in range(NT):
                eng.wait_ge(lg_ready, t + 1)
                ins = eng.transpose(ps[:, 5, 16 * t:16 * t + 16], lg[:, P * t:P * t + P], ident[0:E, 0:E])
            ins.then_inc(lg_turned, 1)
            for t in range(NT):
                eng.wait_ge(soft_ready, t + 1)
                b, c = (6, 0) if t == 0 else (7, P * (t - 1))
                eng.transpose(ps[0:E, b, c:c + P], soft[:, t, :], ident[:, :]).then_inc(soft_turned, 1)
            eng.wait_ge(top_ready, 1)
            eng.transpose(ps[0:CAP, 0, 0:E], idx_f[:, :], ident[0:E, 0:E])
            eng.transpose(ps[0:CAP, 0, E:2 * E], gates_e[:, :], ident[0:E, 0:E]).then_inc(top_turned, 1)

            def turn_xe(n):
                eng.wait_ge(xe_loaded, n * 16)
                for k in range(KD):
                    ins = eng.transpose(ps[:, 6 + k // 4, CAP * (k % 4):CAP * (k % 4) + CAP], xe[:, P * k:P * k + P],
                                        ident[0:CAP, 0:CAP])
                ins.then_inc(xe_turned, 1)

            def turn_h(half):
                for k in range(8):
                    ins = eng.transpose(ps[:, 6 + k // 4, CAP * (k % 4):CAP * (k % 4) + CAP],
                                        hs[:, (8 * half + k) * P:(8 * half + k + 1) * P], ident[0:CAP, 0:CAP])
                ins.then_inc(h_turned, 1)

            eng.wait_ge(idx_ready, 3)
            turn_xe(1)
            with eng.Fori(0, E) as i:
                eng.wait_ge(xeT_ready, i + 1)

                def rows_times(m, bank, x_hi, x_lo, k0, first, last_one):
                    eng.wait_ge(unit_split, units(i, m))
                    for kk in range(4):
                        for b in range(2):
                            for n, (x, w) in enumerate(((x_hi, w_hi[m % 2]), (x_hi, w_lo(m)), (x_lo, w_hi[m % 2]))):
                                ins = eng.matmul(ps[0:CAP, bank + b, :], x[:, k0 + kk, :],
                                                 w[:, kk, 512 * b:512 * b + 512],
                                                 start=first and kk == 0 and n == 0, stop=last_one and kk == 3 and n == 2)
                        if kk % 2:
                            ins.then_inc(unit_used, 1)

                def token_product(m, bank):
                    for part in range(2):
                        rows_times(m + part, bank, xe_hi, xe_lo, 4 * part, part == 0, part == 1)

                def hidden_product(m):
                    rows_times(m, 4, h_hi, h_lo, 4 * (m - 8), m == 8, m == 11)

                token_product(0, 0)
                token_product(2, 2)
                eng.wait_ge(h1_silu, i * 2 + 1)
                token_product(4, 0)
                eng.wait_ge(h_ready, i * 2 + 1)
                turn_h(0)
                token_product(6, 2)
                eng.wait_ge(hT_ready, i * 2 + 1)
                hidden_product(8)
                eng.wait_ge(h_ready, i * 2 + 2)
                turn_h(1)
                hidden_product(9)
                eng.wait_ge(hT_ready, i * 2 + 2)
                turn_xe(i + 2)
                hidden_product(10)
                hidden_product(11)


_INS = ["x_prompt", "x_sample", "state_rglru", "c", "c_ctx", "norm1_g", "norm2_g", "w_mod", "b_mod", "w_in",
        "rnn_conv_w", "rnn_conv_b", "rnn_gate_w", "rnn_gate_b", "rnn_lambda", "w_rnn_out", "conv_dw_w", "conv_dw_b",
        "conv_ln_g", "conv_ln_b", "w_conv_out", "w_out", "w_router", "w_e1", "w_e3", "w_e2", "final_norm_g"]
_OUTS = [("y_prompt", (1, NP, D)), ("y_sample", (1, NS, D)), ("new_state", (1, 1, 2, D))]


def kernel(**inputs):
    import numpy as np
    from concourse import bacc
    from concourse.bass_utils import run_bass_kernel_spmd

    nc = bacc.Bacc("TRN2", target_bir_lowering=False, num_devices=1)
    arrays, args = {}, {}
    for name in _INS:
        x = np.ascontiguousarray(inputs[name])
        arrays[f"in_{name}"] = x
        args[name] = nc.dram_tensor(f"in_{name}", x.shape, mybir.dt.from_np(x.dtype), kind="ExternalInput").ap()
    for name, shape in _OUTS:
        args[name] = nc.dram_tensor(f"out_{name}", shape, F32, kind="ExternalOutput").ap()
    trunk_layer(nc, args)
    r = run_bass_kernel_spmd(nc, [arrays], core_ids=[0])
    return tuple(r.results[0][f"out_{name}"] for name, _ in _OUTS)
```

```python
from contextlib import ExitStack

import concourse.bass as bass
from concourse import mybir

P = 128
D = 1024
KD = D // P
NP, NS = 128, 512
N = NP + NS
NT = N // P
HALF = N // 2
GRID_W = 64
GRID_H = NS // GRID_W
TAPS4 = 4
TAPS31 = 31
MID = TAPS31 // 2
E = 16
FF = 2 * D
KF = FF // P
CAP_P = 2 * NP // E
CAP_S = 2 * NS // E
CAP = CAP_S + CAP_P
DIN = 5 * D
EPS = 1e-6
RG_C = 8.0

S0 = NP + 3
LX = 644
LXP = LX + TAPS4

ALU = mybir.AluOpType
ACT = mybir.ActivationFunctionType
AX = mybir.AxisListType
F32 = mybir.dt.float32
F32R = mybir.dt.float32r
U32 = mybir.dt.uint32

C_BMOD, C_N1, C_N2, C_LNG, C_LNB, C_TAB = 0, 48, 56, 64, 72, 80
G_STATE, G_RCB, G_CDB, G_RCW, G_GB, G_LAM, G_CDW, G_NLAM = 0, 2, 3, 4, 8, 12, 14, 45
NG = 47
NCOLS = C_TAB + 8 * NG

SLOT = 4096
NSLOT = 6
WA_OFF = 0
TEMPS = 2 * SLOT
MOE_SLOTS = [0, 1, 2, 3, 4, 5]


class Steps:

    def __init__(self, eng, sem):
        self.eng, self.sem, self.n = eng, sem, 0

    def did(self, ins):
        ins.then_inc(self.sem, 1)
        self.n += 1

    def wait(self, back=0):
        if self.n > back:
            self.eng.wait_ge(self.sem, self.n - back)

    def restart(self):
        self.wait()
        self.eng.sem_clear(self.sem)
        self.n = 0


def conv_ranges():
    prompt, sample = [], []
    for k in range(TAPS31):
        s = k - MID
        if s:
            a, b = max(0, -s), min(NP, NP - s)
            prompt.append((k, a, b, s))
        if s and abs(s) < GRID_H:
            a, b = max(0, -s) * GRID_W, (GRID_H - max(0, s)) * GRID_W
            sample.append((k, NP + a, NP + b, s * GRID_W))
    out = []
    while prompt or sample:
        out += [c.pop(0) for c in (prompt, sample) if c]
    return out


def trunk_layer(nc, a):
    x_prompt = a["x_prompt"][0]
    x_sample = a["x_sample"][0].rearrange("(t p) d -> t p d", p=P)
    w_in = a["w_in"][0].rearrange("(k p) c -> p k c", p=P)
    w_mod = a["w_mod"][0].rearrange("(k p) c -> p k c", p=P)
    w_ro = a["w_rnn_out"][0].rearrange("(k p) c -> p k c", p=P)
    w_co = a["w_conv_out"][0].rearrange("(k p) c -> p k c", p=P)
    w_out = a["w_out"][0].rearrange("(k p) c -> p k c", p=P)
    w_router = a["w_router"][0].rearrange("(k p) e -> p k e", p=P)
    w_e1 = a["w_e1"][0].rearrange("e (k p) f -> e p k f", p=P)
    w_e3 = a["w_e3"][0].rearrange("e (k p) f -> e p k f", p=P)
    w_e2 = a["w_e2"][0].rearrange("e (k p) f -> e p k f", p=P)
    w_e2_rows = a["w_e2"][0].rearrange("e (q k p) f -> p (e q) k f", k=4, p=P)
    gate_w = a["rnn_gate_w"][0].rearrange("a g h i j -> i (a g) h j")

    mod_rows = nc.dram_tensor("mod_rows", [4, 6 * D], F32, kind="Internal").ap()
    xn_dram = nc.dram_tensor("xn_dram", [N, D], F32, kind="Internal").ap()
    acc_dram = nc.dram_tensor("acc_dram", [N, D], F32, kind="Internal").ap()

    with ExitStack() as ctx:
        place = {}

        def sb(name, shape, dt=F32):
            place[name] = -(-nc.sbuf_base // 32) * 32
            return ctx.enter_context(nc.sbuf_tensor(name, shape, dt))

        def rounded(name, under, at, *shape):
            return nc.alloc_sbuf_tensor_at(name, [P, *shape], F32R, offset=place[under] + 4 * at)

        def sem(name):
            return ctx.enter_context(nc.semaphore(name))

        ring = sb("ring", [P, NSLOT * SLOT])
        uT = sb("uT", [P, KD, N])
        xr = sb("xr", [P, NT, D])
        ya = sb("ya", [P, KD, N])
        cu = sb("cu", [P, KD, N])
        xpad = sb("xpad", [P, 2, LXP])
        sg = sb("sg", [P, 2, N])
        gw = sb("gw", [P, 2, 4, P])
        cols = sb("cols", [P, NCOLS])
        cur = sb("cur", [P, NG, 2])
        modc = sb("modc", [P, 48, 2])
        a1 = sb("a1", [P, KD, 2])
        a2 = sb("a2", [P, KD, 2])
        ident = sb("ident", [P, P])
        ones = sb("ones", [P, P])
        vecs = sb("vecs", [P, 4, P])
        c_rows = sb("c_rows", [2 * KD, P])
        mod_tiles = sb("mod_tiles", [4 * 16, P])
        silu_c = sb("silu_c", [P, KD, 4])
        silu_parts = sb("silu_parts", [P, KD, 4], F32R)
        sp = sb("sp", [P, 5, 16])
        ln_sq = sb("ln_sq", [P, 2, N])
        last = sb("last", [P, 2, KD])
        last_t = sb("last_t", [16, P])
        wr = sb("wr", [P, KD, E])
        rstat = sb("rstat", [P, 4, NT])
        soft = sb("soft", [P, NT, E])
        sstat = sb("sstat", [P, 3, NT])
        lg = sb("lg", [E, N])
        idx = sb("idx", [E, CAP], U32)
        idx_f = sb("idx_f", [E, CAP])
        gates_e = sb("gates_e", [E, CAP])
        idx_t = sb("idx_t", [CAP, E + 1], U32)
        gate_t = sb("gate_t", [CAP, E])
        idx_g = sb("idx_g", [CAP, 1], U32)
        idx_s = sb("idx_s", [CAP, 1], U32)
        ps = ctx.enter_context(nc.psum_tensor("ps", [P, 8, 512], F32))

        def flat(t):
            return t[:, :, :].rearrange("p a b -> p (a b)")

        ya_f, cu_f = flat(ya), flat(cu)

        def slot(s, n=1):
            return ring[:, s * SLOT:(s + n) * SLOT]

        def temps(at, *shape):
            n = 1
            for s in shape:
                n *= s
            v = ring[:, TEMPS + at:TEMPS + at + n]
            names = "abcd"[:len(shape)]
            if len(shape) == 1:
                return v
            return v.rearrange(f"p ({' '.join(names)}) -> p {' '.join(names)}",
                               **dict(zip(names[1:], shape[1:])))

        at = 0
        lr_r = temps(at, 2, 2, LX)
        lr_i = temps(at + 4 * LX, 2, 2, LX)
        lr_a = temps(at + 8 * LX, 2, 2, LX)
        lr_q = temps(at + 12 * LX, 2, 2, LX)
        at = 16 * LX
        glu = temps(at, 2, N)
        cv = temps(at + 2 * N, 2, N)
        xc = temps(at + 4 * N, 2, LX)
        ln_mu = gw[:, :, :, :].rearrange("p a b c -> p (a b c)")[:, 0:N]
        ln_rs = ring[:, 2 * SLOT:2 * SLOT + N]
        at = 2 * SLOT + D
        merged = ring[:, at:at + NT * D].rearrange("p (t d) -> p t d", t=NT)
        vT = ring[:, at:at + N * KD].rearrange("p (k c) -> p k c", k=KD)
        u_hi = rounded("u_hi", "ring", at + NT * D, KD, N)
        y_hi = rounded("y_hi", "ring", at + 2 * NT * D, KD, N)
        u_lo = rounded("u_lo", "uT", 0, KD, N)
        ya_lo = rounded("ya_lo", "ya", 0, KD, N)
        yb_lo = rounded("yb_lo", "cu", 0, KD, N)
        xn2 = ring[:, at + 2 * NT * D:at + 3 * NT * D].rearrange("p (t d) -> p t d", t=NT)
        b_raw = ring[:, 2 * D:6 * D].rearrange("p (n k c) -> p n k c", n=4, k=2)
        b_lo = rounded("b_lo", "ring", 2 * D, 4, 2, 512)
        b_hi = [rounded(f"b_hi{n}", "ring", c, 2, 512) for n, c in enumerate((0, D, 6 * D, 7 * D))]
        g0_w = [ring[:, c:c + 2 * D].rearrange("p (k c) -> p k c", k=4) for c in (6 * D, 0)]
        gate_rows = [flat(sg)[:, 0:512], flat(sg)[:, 512:1024], flat(xpad)[:, 0:512], flat(xpad)[:, 512:1024], flat(vecs)]
        xn1 = cu_f.rearrange("p (t d) -> p t d", t=NT)
        mod_row = ya_f[0:4, 0:2 * D]
        mod_lo = rounded("mod_lo", "ring", 0, 4, 2, 2 * D)
        mod_hi = rounded("mod_hi", "ring", 4 * SLOT, 2, 2, 2 * D)
        g1b = cu_f[:, 0:2 * D].rearrange("p (s d) -> p s d", s=2)
        bias1 = cu_f[:, 2 * D:3 * D]
        bias2 = cu_f[:, 3 * D:4 * D]
        g1b_lo = ya_f[:, D:3 * D].rearrange("p (s d) -> p s d", s=2)
        g2b_lo = ya_f[0:CAP, 3 * D:4 * D]
        prod = cu_f[:, 4 * D:5 * D].rearrange("p (b c) -> p b c", b=2)
        g2b = ya_f[0:CAP, 0:D]
        xe = ya_f[0:CAP, D:2 * D]
        ye = ya_f[0:CAP, 2 * D:3 * D]
        xeT = ya_f[:, 3 * D:3 * D + KD * CAP].rearrange("p (k c) -> p k c", k=KD)
        xe_hi = rounded("xe_hi", "ya", 3 * D + KD * CAP, KD, CAP)
        xe_lo = rounded("xe_lo", "ya", 3 * D, KD, CAP)
        h_hi = rounded("h_hi", "cu", 3 * D, KF, CAP)
        h_lo = rounded("h_lo", "sg", 0, KF, CAP)
        w_hi = [rounded("w_hi0", "uT", 0, 4, D), rounded("w_hi1", "xr", 0, 4, D)]
        ring_lo = rounded("ring_lo", "ring", 0, NSLOT, 4, D)
        hs = cu_f[0:CAP, 0:FF]
        gf = cu_f[:, 2 * D:3 * D]

        vec_loaded = sem("vec_loaded")
        x_loaded = sem("x_loaded")
        wr_loaded = sem("wr_loaded")
        consts_ready = sem("consts_ready")
        cols_turned = sem("cols_turned")
        cols_ready = sem("cols_ready")
        c_loaded = sem("c_loaded")
        c_turned = sem("c_turned")
        silu_ready = sem("silu_ready")
        silu_split = sem("silu_split")
        exp_lam_ready = sem("exp_lam_ready")
        decay_ready = sem("decay_ready")
        mod_loaded = [sem(f"mod_loaded{s}") for s in range(8)]
        mod_hi_ready = sem("mod_hi_ready")
        mod_split = sem("mod_split")
        mod_used = sem("mod_used")
        mod_row_ready = sem("mod_row_ready")
        mod_row_stored = sem("mod_row_stored")
        mod_tiled = sem("mod_tiled")
        mod_turned = sem("mod_turned")
        modc_ready = sem("modc_ready")
        a12_ready = sem("a12_ready")
        ssq_ready = sem("ssq_ready")
        ms_ready = sem("ms_ready")
        root_ready = sem("root_ready")
        r_ready = sem("r_ready")
        xn1_ready = sem("xn1_ready")
        xt_turned = sem("xt_turned")
        ut_sample = sem("ut_sample")
        ut_prompt = sem("ut_prompt")

        wa_loaded = [sem(f"wa_loaded{k}") for k in range(3)]
        gw_loaded = sem("gw_loaded")
        xr_done = sem("xr_done")
        xv_done = sem("xv_done")
        xg_done = sem("xg_done")
        gate_done = sem("gate_done")
        xr_copied = sem("xr_copied")
        cur_ready = sem("cur_ready")
        tap0_ready = sem("tap0_ready")
        xc_ready = sem("xc_ready")
        xg_sig = sem("xg_sig")
        glu_ready = sem("glu_ready")
        gate_sig = sem("gate_sig")
        decay_sq = sem("decay_sq")
        in_sq = sem("in_sq")
        in_root = sem("in_root")
        ix_ready = sem("ix_ready")
        conv_done = sem("conv_done")
        cv_copied = sem("cv_copied")
        lru_done = sem("lru_done")
        last_turned = sem("last_turned")
        last_ready = sem("last_ready")
        state_stored = sem("state_stored")

        ln_summed = sem("ln_summed")
        ln_centred = sem("ln_centred")
        ln_squared = sem("ln_squared")
        ln_sq_used = sem("ln_sq_used")
        ln_var = sem("ln_var")
        ln_root = sem("ln_root")
        ln_scaled = sem("ln_scaled")

        g0_loaded = [sem(f"g0_loaded{n}") for n in range(2)]
        g0_used = sem("g0_used")
        piece_loaded = [sem(f"piece_loaded{n}") for n in range(4)]
        piece_hi = sem("piece_hi")
        piece_split = sem("piece_split")
        piece_used = sem("piece_used")
        tile_done = sem("tile_done")
        gate_ready = sem("gate_ready")
        m_ready = sem("m_ready")
        y_hi_ready = sem("y_hi_ready")
        y_split = sem("y_split")
        u_hi_ready = sem("u_hi_ready")
        u_split = sem("u_split")
        yb_hi_ready = sem("yb_hi_ready")
        yb_split = sem("yb_split")
        mt_turned = sem("mt_turned")
        mt_hi_ready = sem("mt_hi_ready")
        mt_split = sem("mt_split")
        rows_loaded = sem("rows_loaded")
        rows_ready = sem("rows_ready")
        x2_ready = sem("x2_ready")
        ssq2_ready = sem("ssq2_ready")
        ms2_ready = sem("ms2_ready")
        root2_ready = sem("root2_ready")
        r2_ready = sem("r2_ready")
        xn2_ready = sem("xn2_ready")
        rows_stored = sem("rows_stored")
        vt_turned = sem("vt_turned")
        vt_dve = sem("vt_dve")
        vt_act = sem("vt_act")
        logit_done = sem("logit_done")
        lg_ready = sem("lg_ready")
        lg_turned = sem("lg_turned")
        max_ready = sem("max_ready")
        exp_ready = sem("exp_ready")
        soft_ready = sem("soft_ready")
        soft_turned = sem("soft_turned")
        top_ready = sem("top_ready")
        top_turned = sem("top_turned")
        idx_ready = sem("idx_ready")

        w_loaded = [sem(f"w_loaded{s}") for s in range(NSLOT)]
        unit_hi = sem("unit_hi")
        unit_split = sem("unit_split")
        unit_used = sem("unit_used")
        xe_modulated = sem("xe_modulated")
        xe_hi_ready = sem("xe_hi_ready")
        h_hi_ready = sem("h_hi_ready")
        xe_loaded = sem("xe_loaded")
        xe_turned = sem("xe_turned")
        xeT_ready = sem("xeT_ready")
        h1_silu = sem("h1_silu")
        h_ready = sem("h_ready")
        h_turned = sem("h_turned")
        hT_ready = sem("hT_ready")
        ye_ready = sem("ye_ready")
        scattered = sem("scattered")
        gf_loaded = sem("gf_loaded")
        fin_loaded = [sem(f"fin_loaded{t}") for t in range(NT)]
        fin_ssq = sem("fin_ssq")
        fin_ms = sem("fin_ms")
        fin_root = sem("fin_root")
        out_ready = sem("out_ready")
        out_stored = sem("out_stored")
        dve_step = sem("dve_step")
        act_step = sem("act_step")
        pool_step = sem("pool_step")

        block = ctx.enter_context(nc.Block())

        def wa(kind):
            return ring[:, WA_OFF + 2048 * kind:WA_OFF + 2048 * (kind + 1)].rearrange("p (k c) -> p k c", k=KD)

        GROUPS = [(w_in, 3 * D), (w_ro, 0), (w_in, 3 * D + 512), (w_ro, 512),
                  (w_in, 4 * D), (w_co, 0), (w_in, 4 * D + 512), (w_co, 512), (w_out, 0), (w_out, 512)]
        BANKS = [0, 1, 2, 3, 4, 7]

        def piece_done(eng, q):
            if q % 4 == 3:
                eng.wait_ge(tile_done, NT * (q // 4 + 2))
            else:
                eng.wait_ge(piece_used, 3 * (q // 4) + q % 4 + 1)

        def tile_bank(n):
            return BANKS[n % 6]

        def chunk_source(e, m):
            if m < 8:
                w = (w_e1, w_e3)[m // 2 % 2]
                return w[e, :, 4 * (m % 2):4 * (m % 2) + 4, (m // 4) * D:(m // 4 + 1) * D]
            return w_e2[e, :, 4 * (m - 8):4 * (m - 8) + 4, :]

        def chunk(m):
            return slot(MOE_SLOTS[m % NSLOT]).rearrange("p (k c) -> p k c", k=4)

        def w_lo(m):
            return ring_lo[:, MOE_SLOTS[m % NSLOT], :, :]

        def units(i, m, half=1):
            return i * 24 + (2 * m + half + 1)

        def product_done(eng, i, m):
            eng.wait_ge(unit_used, units(i, m))

        @block.sync
        def _(eng):
            def load_mod(n):
                i, s = n // 4, n % 4
                for half in range(2):
                    if n >= 4:
                        eng.wait_ge(mod_used, 2 * (n - 4) + half + 1)
                    eng.dma_start(slot(s)[:, 2 * D * half:2 * D * half + 2 * D],
                                  w_mod[:, 2 * s + half, i * (2 * D):(i + 1) * (2 * D)]).then_inc(mod_loaded[2 * s + half], 16)

            def load_a(i, kind):
                eng.dma_start(wa(kind), w_in[:, :, bass.ds(i * 256 + kind * D, 256)]).then_inc(wa_loaded[kind], 16)

            def load_gates(i):
                for t in range(2):
                    for half in range(2):
                        eng.dma_start(gw[64 * half:64 * half + 64, t, :, 64 * half:64 * half + 64],
                                      gate_w[:, :, bass.ds(i * 4 + (2 * t + half), 1), :].rearrange("i g h j -> i g (h j)"))\
                            .then_inc(gw_loaded, 16)

            for n in range(4):
                load_mod(n)
            for t in range(NT):
                eng.dma_start(xr[:, t, :], x_prompt if t == 0 else x_sample[t - 1]).then_inc(x_loaded, 16)
            eng.dma_start(wr[:, :, :], w_router).then_inc(wr_loaded, 16)
            for n in range(4, 12):
                load_mod(n)
            eng.wait_ge(mod_used, 2 * 9 + 2)
            for kind in range(3):
                load_a(0, kind)
            eng.wait_ge(consts_ready, 4)
            load_gates(0)
            with eng.Fori(0, 3) as i:
                for kind, done in enumerate((xr_done, xv_done, xg_done)):
                    eng.wait_ge(done, i * 2 + 2)
                    load_a(i + 1, kind)
                eng.wait_ge(gate_done, i * 8 + 8)
                load_gates(i + 1)
            for done in (xr_done, xv_done, xg_done):
                eng.wait_ge(done, 8)

            def load_piece(q):
                w, c = GROUPS[q // 4 + 1]
                eng.dma_start(b_raw[:, q % 4, :, :], w[:, 2 * (q % 4):2 * (q % 4) + 2, c:c + 512]).then_inc(piece_loaded[q % 4], 16)

            w, c = GROUPS[0]
            for n in range(2):
                eng.dma_start(g0_w[n], w[:, 4 * n:4 * n + 4, c:c + 512]).then_inc(g0_loaded[n], 16)
            for q in range(4):
                load_piece(q)
            eng.wait_ge(last_ready, 1)
            eng.dma_start(a["new_state"][0, 0].rearrange("s (k p) -> (s k) p", p=P), last_t[:, :]).then_inc(state_stored, 16)
            for q in range(4, 32):
                piece_done(eng, q - 4)
                load_piece(q)
            eng.wait_ge(tile_done, NT * 8)
            eng.wait_ge(mod_row_stored, 16 * 3)
            for g, first in ((g1b, 0), (g1b_lo, 2)):
                for s in range(2):
                    eng.dma_start(g[:, s, :], mod_rows[first + s:first + s + 1, 2 * D:3 * D].broadcast_to([P, D]))\
                        .then_inc(rows_loaded, 16)
            eng.dma_start(bias1, a["b_mod"][0:1, 2 * D:3 * D].broadcast_to([P, D])).then_inc(rows_loaded, 16)
            eng.dma_start(bias2, a["b_mod"][0:1, 5 * D:6 * D].broadcast_to([P, D])).then_inc(rows_loaded, 16)
            for g, first in ((g2b, 0), (g2b_lo, 2)):
                for s, lo, hi in ((1, 0, CAP_S), (0, CAP_S, CAP)):
                    eng.dma_start(g[lo:hi, :], mod_rows[first + s:first + s + 1, 5 * D:6 * D].broadcast_to([hi - lo, D]))\
                        .then_inc(rows_loaded, 16)

            def load_chunk(e, m):
                eng.dma_start(chunk(m), chunk_source(e, m)).then_inc(w_loaded[MOE_SLOTS[m % NSLOT]], 16)

            for q in range(32, 36):
                piece_done(eng, q - 4)
                load_piece(q)
            eng.wait_ge(tile_done, NT * 10)
            load_chunk(0, 0)
            load_chunk(0, 1)
            eng.wait_ge(logit_done, NT)
            load_chunk(0, 2)
            load_chunk(0, 3)
            eng.wait_ge(vt_turned, NT)
            eng.wait_ge(rows_stored, 16 * 2 * NT)
            load_chunk(0, 4)
            load_chunk(0, 5)
            eng.dma_start(gf, a["final_norm_g"].rearrange("(o d) -> o d", o=1).broadcast_to([P, D])).then_inc(gf_loaded, 16)
            with eng.Fori(0, E - 1) as i:
                for n in range(12):
                    m = (n + NSLOT) % 12
                    e = i + (n + NSLOT) // 12
                    if m < 8:
                        w = (w_e1, w_e3)[m // 2 % 2][bass.ds(e, 1), :, :, :].rearrange("e p k f -> p (e k) f")
                        src = w[:, 4 * (m % 2):4 * (m % 2) + 4, (m // 4) * D:(m // 4 + 1) * D]
                    else:
                        src = w_e2_rows[:, bass.ds(e * 4 + (m - 8), 1), :, :].rearrange("p q k f -> p (q k) f")
                    product_done(eng, i, n)
                    eng.dma_start(chunk(m), src).then_inc(w_loaded[MOE_SLOTS[m % NSLOT]], 16)
            for m in range(NSLOT, 12):
                product_done(eng, E - 1, m - NSLOT)
                load_chunk(E - 1, m)
            eng.wait_ge(scattered, 16 * E)
            for t in range(NT):
                eng.dma_start(xr[:, t, :], acc_dram[P * t:P * t + P, :]).then_inc(fin_loaded[t], 16)
            for t in range(NT):
                eng.wait_ge(out_ready, t + 1)
                eng.dma_start(a["y_prompt"][0] if t == 0 else a["y_sample"][0].rearrange("(t p) d -> t p d", p=P)[t - 1],
                              xr[:, t, :]).then_inc(out_stored, 16)
            eng.wait_ge(out_stored, 16 * NT)
            eng.wait_ge(state_stored, 16)

        @block.gpsimd
        def _(eng):
            step = Steps(eng, pool_step)
            step.did(eng.memset(silu_c[:, :, :], 0.0))
            step.did(eng.memset(ident[:, :], 0.0))
            step.wait()
            eng.affine_select(out=ident[:, :], in_=ident[:, :], compare_op=ALU.not_equal, fill=1.0,
                              base=0, pattern=[[-1, P]], channel_multiplier=1).then_inc(consts_ready, 1)
            eng.memset(ones[:, :], 1.0).then_inc(consts_ready, 1)
            eng.memset(xpad[:, :, :], 0.0).then_inc(consts_ready, 1)
            eng.memset(gw[:, :, :, :], 0.0).then_inc(consts_ready, 1)

            def vec_in(rows, tile, src):
                n = src.shape[0]
                eng.dma_start(vecs[rows:rows + n, tile, :], src).then_inc(vec_loaded, 16)

            def rows_of(v):
                return v.rearrange("(r p) -> r p", p=P)

            vec_in(C_BMOD, 0, rows_of(a["b_mod"][0]))
            vec_in(C_N1, 0, rows_of(a["norm1_g"][0]))
            vec_in(C_N2, 0, rows_of(a["norm2_g"][0]))
            vec_in(C_LNG, 0, rows_of(a["conv_ln_g"][0]))
            vec_in(C_LNB, 0, rows_of(a["conv_ln_b"][0]))
            vec_in(C_TAB, 0, a["state_rglru"][0, 0].rearrange("s (r p) -> (s r) p", p=P))
            vec_in(C_TAB + 8 * G_RCB, 0, rows_of(a["rnn_conv_b"][0]))
            vec_in(C_TAB + 8 * G_CDB, 0, rows_of(a["conv_dw_b"][0]))
            vec_in(0, 1, a["rnn_conv_w"][0].rearrange("s (r p) -> (s r) p", p=P))
            vec_in(32, 1, a["rnn_gate_b"][0].rearrange("s g (r p) -> (s g r) p", p=P))
            vec_in(64, 1, a["rnn_lambda"][0].rearrange("s (r p) -> (s r) p", p=P))
            taps = a["conv_dw_w"][0].rearrange("s (r p) -> (s r) p", p=P)
            vec_in(0, 2, taps[0:P])
            vec_in(0, 3, taps[P:8 * TAPS31])

            for i in range(3):
                eng.wait_ge(mod_row_ready, i + 1)
                eng.dma_start(mod_rows[:, i * (2 * D):(i + 1) * (2 * D)], mod_row).then_inc(mod_row_stored, 16)

            with eng.Fori(0, 4) as i:
                for n in range(4):
                    t, d = n // 2, n % 2
                    eng.wait_ge(gate_sig, i * 8 + (2 * n + 2))
                    eng.wait_ge(xc_ready, i * 2 + (t + 1))
                    eng.tensor_tensor(lr_i[:, t, d, :], lr_i[:, t, d, :], xc[:, t, :], ALU.mult).then_inc(ix_ready, 1)
                for t in range(2):
                    eng.wait_ge(conv_done, i * 2 + (t + 1))
                    eng.tensor_copy(cu[:, bass.ds(i * 2 + t, 1), :], cv[:, t:t + 1, :]).then_inc(cv_copied, 1)

            def gather(col):
                step.did(eng.tensor_copy(idx_g[:, :], idx_t[:, bass.ds(col, 1)]))
                step.wait()
                eng.indirect_dma_start(out=xe, out_offset=None, in_=xn_dram,
                                       in_offset=bass.IndirectOffsetOnAxis(ap=idx_g[:, 0:1], axis=0))\
                    .then_inc(xe_loaded, 16)

            eng.wait_ge(idx_ready, 3)
            eng.wait_ge(rows_stored, 16 * 2 * NT)
            gather(0)
            step.restart()
            with eng.Fori(0, E) as i:
                eng.wait_ge(xe_turned, i + 1)
                eng.wait_ge(xe_loaded, i * 16 + 16)
                gather(i + 1)
                step.did(eng.tensor_copy(idx_s[:, :], idx_t[:, bass.ds(i, 1)]))
                step.wait()
                eng.wait_ge(ye_ready, i + 1)
                eng.indirect_dma_start(out=acc_dram, out_offset=bass.IndirectOffsetOnAxis(ap=idx_s[:, 0:1], axis=0),
                                       in_=ye, in_offset=None, compute_op=ALU.add).then_inc(scattered, 16)
                step.restart()
                eng.wait_ge(scattered, i * 16 + 16)

        @block.scalar
        def _(eng):
            for at, c in ((0, a["c_ctx"]), (KD, a["c"][0])):
                eng.dma_start(c_rows[at:at + KD, :], c.rearrange("(r p) -> r p", p=P)).then_inc(c_loaded, 16)
            step = Steps(eng, act_step)

            eng.wait_ge(c_turned, 1)
            step.did(eng.activation(silu_c[:, :, 0:2].rearrange("p k s -> p s k"),
                                    ps[:, 7, 0:2 * KD].rearrange("p (s k) -> p s k", s=2), ACT.Silu))
            step.wait()
            eng.activation(silu_parts[:, :, 0:2].rearrange("p k s -> p s k"), silu_c[:, :, 0:2].rearrange("p k s -> p s k"), ACT.Copy).then_inc(silu_ready, 1)

            def mod_high(n):
                for half in range(2):
                    eng.wait_ge(mod_loaded[2 * (n % 4) + half], 16 * (n // 4 + 1))
                    if n >= 4:
                        eng.wait_ge(mod_used, 2 * (n - 4) + half + 1)
                    eng.activation(mod_hi[:, n // 2 % 2, half, :], slot(n % 4)[:, 2 * D * half:2 * D * half + 2 * D], ACT.Copy)\
                        .then_inc(mod_hi_ready, 1)

            def mod_sums(i):
                eng.wait_ge(mod_used, 8 * i + 8)
                if i:
                    eng.wait_ge(mod_row_stored, 16 * i)
                    eng.wait_ge(mod_turned, i)
                b = 4 * (i % 2)
                eng.activation(mod_row.rearrange("s (b c) -> s b c", b=4), ps[0:4, b:b + 4, :], ACT.Copy).then_inc(mod_row_ready, 1)
                eng.wait_ge(mod_row_ready, i + 1)
                eng.dma_start(mod_tiles[:, :], mod_row.rearrange("s (j p) -> s j p", p=P)).then_inc(mod_tiled, 16)

            mod_high(0)
            mod_high(2)
            eng.wait_ge(x_loaded, 16 * NT)
            for t in range(NT):
                if t:
                    eng.wait_ge(ssq_ready, t)
                eng.activation(xn1[:, t, :], xr[:, t, :], ACT.Square, accum_out=rstat[:, 0, t:t + 1]).then_inc(ssq_ready, 1)
            eng.wait_ge(ms_ready, 1)
            eng.activation(rstat[:, 2, :], rstat[:, 1, :], ACT.Sqrt).then_inc(root_ready, 1)
            mod_high(4)
            mod_sums(0)
            eng.wait_ge(r_ready, 1)
            for t in range(NT):
                eng.activation(xn1[:, t, :], xr[:, t, :], ACT.Copy, scale=rstat[:, 3, t:t + 1]).then_inc(xn1_ready, 1)
            mod_high(6)

            def ut_part(k):
                eng.wait_ge(xt_turned, k + 1)
                eng.activation(uT[:, k, 0:NP], ps[:, 2 * (k % 2) + 1, 0:NP], ACT.Identity,
                               scale=a1[:, k, 0:1], bias=modc[:, k, 0:1]).then_inc(ut_prompt, 1)

            eng.wait_ge(a12_ready, 1)
            for n in (7, 8):
                for k in range(KD // 2):
                    ut_part(KD // 2 * (n - 7) + k)
                if n == 8:
                    mod_high(n)
            mod_high(10)
            mod_sums(1)
            eng.wait_ge(cols_ready, 1)
            lam = cols[:, C_TAB + 8 * G_LAM:C_TAB + 8 * G_LAM + 16]
            step.did(eng.activation(sp[:, 0, :], lam, ACT.Abs))
            step.wait()
            eng.activation(sp[:, 1, :], sp[:, 0, :], ACT.Exp, scale=-1.0).then_inc(exp_lam_ready, 1)
            mod_sums(2)

            step.restart()
            eng.wait_ge(consts_ready, 4)
            with eng.Fori(0, 4) as i:
                for t in range(2):
                    eng.wait_ge(xr_done, i * 2 + (t + 1))
                    b = 2 * t
                    eng.activation(xpad[:, t, 2:2 + NP], ps[:, b, 0:NP], ACT.Copy)
                    eng.activation(xpad[:, t, S0 + 2:S0 + 2 + HALF - NP], ps[:, b, NP:HALF], ACT.Copy)
                    eng.activation(xpad[:, t, S0 + 2 + HALF - NP:S0 + 2 + NS], ps[:, b + 1, 0:HALF], ACT.Copy)\
                        .then_inc(xr_copied, 1)
                eng.wait_ge(cur_ready, i + 1)
                eng.wait_ge(xr_copied, i * 2 + 2)
                for t in range(2):
                    eng.activation(xc[:, t, :], xpad[:, t, 0:LX], ACT.Identity, scale=cur[:, G_RCW, t:t + 1],
                                   bias=cur[:, G_RCB, t:t + 1]).then_inc(tap0_ready, 1)
                for t in range(2):
                    eng.wait_ge(xg_done, i * 2 + (t + 1))
                    b = (6, 2)[t]
                    eng.activation(sg[:, t, :].rearrange("p (h c) -> p h c", h=2), ps[:, b:b + 2, 0:HALF], ACT.Sigmoid)\
                        .then_inc(xg_sig, 1)
                for n in range(8):
                    t, d, g = n // 4, n // 2 % 2, n % 2
                    b = 2 * ((6 + n) % 4)
                    dst = (lr_r, lr_i)[g][:, t, d, :].rearrange("p (h c) -> p h c", h=2)
                    eng.wait_ge(gate_done, i * 8 + (n + 1))
                    eng.activation(dst, ps[:, b:b + 2, 0:LX // 2], ACT.Sigmoid,
                                   bias=cur[:, G_GB + 2 * d + g, t:t + 1]).then_inc(gate_sig, 1)
                eng.wait_ge(gate_sig, i * 8 + 8)
                for n in range(4):
                    t, d = n // 2, n % 2
                    step.did(eng.activation(lr_a[:, t, d, :], lr_r[:, t, d, :], ACT.Exp, scale=cur[:, G_NLAM + d, t:t + 1]))
                    step.did(eng.activation(lr_r[:, t, d, :], lr_r[:, t, d, :], ACT.Tanh, scale=cur[:, G_LAM + d, t:t + 1]))
                    step.wait(1)
                    eng.activation(lr_q[:, t, d, :], lr_a[:, t, d, :], ACT.Square).then_inc(decay_sq, 1)
                for n in range(4):
                    t, d = n // 2, n % 2
                    eng.wait_ge(in_sq, i * 4 + (n + 1))
                    eng.activation(lr_q[:, t, d, :], lr_q[:, t, d, :], ACT.Sqrt).then_inc(in_root, 1)
                step.restart()

            def piece_high(q):
                eng.wait_ge(piece_loaded[q % 4], 16 * (q // 4 + 1))
                if q < 2:
                    eng.wait_ge(tile_done, NT)
                elif q < 4:
                    eng.wait_ge(g0_used, 1)
                else:
                    piece_done(eng, q - 4)
                eng.activation(b_hi[q % 4][:, :, :], b_raw[:, q % 4, :, :], ACT.Copy).then_inc(piece_hi, 1)

            def gates_of(g):
                for t in range(NT):
                    eng.wait_ge(tile_done, NT * g + t + 1)
                    if g:
                        eng.wait_ge(m_ready, NT * (g // 2 - 1) + t + 1)
                    eng.activation(gate_rows[t], ps[:, tile_bank(NT * g + t), :], ACT.Sigmoid).then_inc(gate_ready, 1)

            def squares(k0, k1):
                for k in range(k0, k1):
                    eng.wait_ge(ln_centred, k + 1)
                    if k >= 2:
                        eng.wait_ge(ln_sq_used, k - 1)
                    eng.activation(ln_sq[:, k % 2, :], cu[:, k, :], ACT.Square).then_inc(ln_squared, 1)

            def yb_high(k0, k1):
                for k in range(k0, k1):
                    eng.wait_ge(ln_scaled, k + 1)
                    for out in (y_hi, cu):
                        ins = eng.activation(out[:, k, :], cu[:, k, :], ACT.Silu, scale=cols[:, C_LNG + k:C_LNG + k + 1],
                                             bias=cols[:, C_LNB + k:C_LNB + k + 1])
                    ins.then_inc(yb_hi_ready, 1)

            gates_of(0)
            eng.wait_ge(lru_done, 4)
            for h in range(2):
                eng.activation(y_hi[:, 4 * h:4 * h + 4, :], ya[:, 4 * h:4 * h + 4, :], ACT.Copy).then_inc(y_hi_ready, 1)
            piece_high(0)
            piece_high(1)
            squares(0, 2)
            piece_high(2)
            squares(2, 4)
            piece_high(3)
            for h in range(2):
                eng.activation(u_hi[:, 4 * h:4 * h + 4, :], uT[:, 4 * h:4 * h + 4, :], ACT.Copy).then_inc(u_hi_ready, 1)
            squares(4, 6)
            piece_high(4)
            squares(6, 8)
            piece_high(5)
            eng.wait_ge(ln_var, 1)
            eng.activation(ln_rs, ln_rs, ACT.Sqrt).then_inc(ln_root, 1)
            piece_high(6)
            piece_high(7)
            for g in range(2, 8):
                if g == 4:
                    eng.wait_ge(tile_done, NT * 4)
                    yb_high(0, 4)
                piece_high(4 * g)
                if g == 4:
                    yb_high(4, 8)
                piece_high(4 * g + 1)
                if g % 2 == 0:
                    gates_of(g)
                piece_high(4 * g + 2)
                piece_high(4 * g + 3)
            for k in range(KD):
                eng.wait_ge(mt_turned, k + 1)
                eng.activation(u_hi[:, k, :], ps[:, 2 * (k % 4):2 * (k % 4) + 2, :].rearrange("p b c -> p (b c)")[:, 0:N], ACT.Copy)\
                    .then_inc(mt_hi_ready, 1)
            for q in range(32, 36):
                piece_high(q)

            def norm_rows(t):
                eng.wait_ge(x2_ready, NT + t + 1)
                if t:
                    eng.wait_ge(xn2_ready, t)
                eng.activation(xn2[:, t, :], xr[:, t, :], ACT.Square, accum_out=rstat[:, 0, t:t + 1]).then_inc(ssq2_ready, 1)
                eng.wait_ge(ms2_ready, t + 1)
                eng.activation(rstat[:, 2, t:t + 1], rstat[:, 1, t:t + 1], ACT.Sqrt).then_inc(root2_ready, 1)
                eng.wait_ge(r2_ready, t + 1)
                eng.activation(xn2[:, t, :], xr[:, t, :], ACT.Copy, scale=rstat[:, 3, t:t + 1]).then_inc(xn2_ready, 1)
                eng.wait_ge(xn2_ready, t + 1)
                eng.dma_start(xn_dram[P * t:P * t + P, :], xn2[:, t, :]).then_inc(rows_stored, 16)
                eng.dma_start(acc_dram[P * t:P * t + P, :], xr[:, t, :]).then_inc(rows_stored, 16)

            def modulate_half(t):
                eng.wait_ge(vt_turned, t + 1)
                for k in range(4, KD):
                    ins = eng.activation(vT[:, k, P * t:P * t + P], ps[:, 2 * (t % 2) + 1, P * (k - 4):P * (k - 3)], ACT.Identity,
                                         scale=a2[:, k, min(t, 1):min(t, 1) + 1], bias=modc[:, 24 + k, min(t, 1):min(t, 1) + 1])
                ins.then_inc(vt_act, 1)

            for t in range(NT - 1):
                norm_rows(t)
                if t:
                    modulate_half(t - 1)
            modulate_half(NT - 2)
            norm_rows(NT - 1)
            modulate_half(NT - 1)
            for t in range(NT):
                eng.wait_ge(max_ready, 1)
                eng.activation(soft[:, t, :], ps[:, 5, 16 * t:16 * t + 16], ACT.Exp, bias=sstat[:, 0, t:t + 1],
                               accum_out=sstat[:, 1, t:t + 1]).then_inc(exp_ready, 1)

            def hi_piece(i, m, free):
                eng.wait_ge(w_loaded[MOE_SLOTS[m % NSLOT]], i * 32 + 16 * (m // NSLOT + 1))
                for half in range(2):
                    if free is not None:
                        eng.wait_ge(unit_used, units(*free, half))
                    eng.activation(w_hi[m % 2][:, 2 * half:2 * half + 2, :], chunk(m)[:, 2 * half:2 * half + 2, :],
                                   ACT.Copy).then_inc(unit_hi, 1)

            def hi_xe(n):
                eng.wait_ge(xe_modulated, n)
                eng.activation(xe_hi[:, :, :], xeT[:, :, :], ACT.Copy).then_inc(xe_hi_ready, 1)

            def swish(i, half):
                product_done(eng, i, 4 * half + 1)
                eng.activation(hs[:, half * D:(half + 1) * D].rearrange("c (b f) -> c b f", b=2), ps[0:CAP, 0:2, :],
                               ACT.Silu).then_inc(h1_silu, 1)

            def hi_h(i, half):
                eng.wait_ge(h_turned, i * 2 + (half + 1))
                eng.activation(h_hi[:, 8 * half:8 * half + 8, :].rearrange("p (b k) c -> p b (k c)", b=2),
                               ps[:, 6:8, 0:4 * CAP], ACT.Copy).then_inc(h_hi_ready, 1)

            def act_expert(i, final):
                for m in range(2, 12):
                    hi_piece(i, m, (i, m - 2))
                    if m == 3:
                        swish(i, 0)
                    if m == 7:
                        swish(i, 1)
                        hi_h(i, 0)
                    if m == 10:
                        hi_h(i, 1)
                hi_xe(i + 2)
                if not final:
                    for m in range(2):
                        hi_piece(i + 1, m, (i, m + 10))

            eng.wait_ge(logit_done, NT)
            eng.wait_ge(rows_stored, 16 * 2 * NT)
            for m in range(2):
                hi_piece(0, m, None)
            hi_xe(1)
            with eng.Fori(0, E - 1) as i:
                act_expert(i, False)
            act_expert(E - 1, True)

            for t in range(NT):
                eng.wait_ge(fin_loaded[t], 16)
                eng.activation(xn1[:, t % 2, :], xr[:, t, :], ACT.Square, accum_out=rstat[:, 0, t:t + 1]).then_inc(fin_ssq, 1)
                eng.wait_ge(fin_ms, t + 1)
                eng.activation(rstat[:, 2, t:t + 1], rstat[:, 1, t:t + 1], ACT.Sqrt).then_inc(fin_root, 1)

        @block.vector
        def _(eng):
            step = Steps(eng, dve_step)

            def inverse_root(ssq_sem, n, ms_sem, root_sem, t0, t1):
                eng.wait_ge(ssq_sem, n)
                eng.tensor_scalar(rstat[:, 1, t0:t1], rstat[:, 0, t0:t1], 1.0 / D, EPS, ALU.mult, ALU.add).then_inc(ms_sem, 1)

            def mod_low(n):
                for half in range(2):
                    eng.wait_ge(mod_hi_ready, n + half + 1)
                    eng.tensor_tensor(mod_lo[:, n % 4, half, :], slot(n % 4)[:, 2 * D * half:2 * D * half + 2 * D],
                                      mod_hi[:, n // 2 % 2, half, :].bitcast(F32), ALU.subtract).then_inc(mod_split, 1)

            def mod_columns(i):
                eng.wait_ge(mod_turned, i + 1)
                src = ps[:, 4 * (i % 2), 0:64].rearrange("p (s j) -> p s j", s=4)
                for h in range(2):
                    step.did(eng.tensor_tensor(modc[:, 16 * i:16 * i + 16, h], src[:, 2 + h, :], cols[:, 16 * i:16 * i + 16], ALU.add))
                step.wait()
                for h in range(2):
                    ins = eng.tensor_tensor(modc[:, 16 * i:16 * i + 16, h], src[:, h, :], modc[:, 16 * i:16 * i + 16, h], ALU.add)
                ins.then_inc(modc_ready, 1)

            def modulated(dst, v, c):
                eng.wait_ge(modc_ready, 1 if v == 1 else 3)
                for s in range(2):
                    ins = eng.scalar_tensor_tensor(out=dst[:, :, s], in0=modc[:, v * KD:v * KD + KD, s], scalar=1.0,
                                                   in1=cols[:, c:c + KD], op0=ALU.add, op1=ALU.mult)
                ins.then_inc(a12_ready, 1)
                eng.wait_ge(a12_ready, 1 if v == 1 else 2)

            eng.wait_ge(silu_ready, 1)
            eng.tensor_tensor(silu_parts[:, :, 2:4].rearrange("p k s -> p s k"), silu_c[:, :, 0:2].rearrange("p k s -> p s k"),
                              silu_parts[:, :, 0:2].bitcast(F32).rearrange("p k s -> p s k"), ALU.subtract).then_inc(silu_split, 1)
            mod_low(0)
            mod_low(2)
            inverse_root(ssq_ready, NT, ms_ready, root_ready, 0, NT)
            eng.wait_ge(cols_turned, 1)
            eng.tensor_copy(cols[:, 0:C_TAB + 8 * G_NLAM], ps[:, 6, 0:C_TAB + 8 * G_NLAM]).then_inc(cols_ready, 1)
            eng.wait_ge(root_ready, 1)
            eng.reciprocal(rstat[:, 3, :], rstat[:, 2, :]).then_inc(r_ready, 1)
            mod_low(4)
            mod_low(6)
            mod_columns(0)
            modulated(a1, 1, C_N1)
            for n in (7, 8):
                for k in range(KD // 2 * (n - 7), KD // 2 * (n - 6)):
                    eng.wait_ge(xt_turned, k + 1)
                    eng.tensor_scalar(uT[:, k, NP:N], ps[:, 2 * (k % 2), :], a1[:, k, 1:2], modc[:, k, 1:2], ALU.mult, ALU.add)\
                        .then_inc(ut_sample, 1)
                if n == 8:
                    mod_low(n)
            mod_low(10)
            mod_columns(1)
            lam = cols[:, C_TAB + 8 * G_LAM:C_TAB + 8 * G_LAM + 16]
            nlam = cols[:, C_TAB + 8 * G_NLAM:C_TAB + 8 * G_NLAM + 16]
            z, s, s2, poly = sp[:, 1, :], sp[:, 2, :], sp[:, 3, :], sp[:, 4, :]
            eng.wait_ge(exp_lam_ready, 1)
            step.did(eng.tensor_scalar(s2, z, 2.0, None, ALU.add))
            step.wait()
            step.did(eng.reciprocal(poly, s2))
            step.wait()
            step.did(eng.tensor_tensor(s, z, poly, ALU.mult))
            step.wait()
            step.did(eng.tensor_tensor(s2, s, s, ALU.mult))
            step.wait()
            step.did(eng.tensor_scalar(poly, s2, 1.0 / 17, 1.0 / 15, ALU.mult, ALU.add))
            for n in range(6, -1, -1):
                step.wait()
                step.did(eng.tensor_tensor(poly, poly, s2, ALU.mult))
                step.wait()
                step.did(eng.tensor_scalar(poly, poly, 1.0 / (2 * n + 1), None, ALU.add))
            step.wait()
            step.did(eng.tensor_tensor(poly, poly, s, ALU.mult))
            step.did(eng.tensor_scalar(s2, lam, -1.0, 0.0, ALU.mult, ALU.max))
            step.wait()
            step.did(eng.scalar_tensor_tensor(out=s, in0=poly, scalar=2.0, in1=s2, op0=ALU.mult, op1=ALU.add))
            step.wait()
            step.did(eng.tensor_scalar(lam, s, RG_C, None, ALU.mult))
            eng.tensor_scalar(nlam, s, -RG_C, None, ALU.mult).then_inc(decay_ready, 1)

            mod_columns(2)
            modulated(a2, 4, C_N2)
            eng.wait_ge(decay_ready, 1)
            eng.wait_ge(mod_row_stored, 48)

            table = cols[:, C_TAB:NCOLS].rearrange("p (g c) -> p g c", c=KD)
            ranges = conv_ranges()
            step.restart()
            with eng.Fori(0, 4) as i:
                eng.tensor_copy(cur[:, :, :], table[:, :, bass.ds(i * 2, 2)]).then_inc(cur_ready, 1)
                eng.wait_ge(cur_ready, i + 1)
                for k in range(1, TAPS4):
                    for t in range(2):
                        if k == 1:
                            eng.wait_ge(tap0_ready, i * 2 + (t + 1))
                        else:
                            step.wait(0 if k == TAPS4 - 1 and t == 1 else 1)
                        ins = eng.scalar_tensor_tensor(out=xc[:, t, :], in0=xpad[:, t, k:k + LX], scalar=cur[:, G_RCW + k, t:t + 1],
                                                       in1=xc[:, t, :], op0=ALU.mult, op1=ALU.add)
                        if k < TAPS4 - 1:
                            step.did(ins)
                        else:
                            ins.then_inc(xc_ready, 1)
                for t in range(2):
                    b = (4, 0)[t]
                    eng.wait_ge(xv_done, i * 2 + (t + 1))
                    eng.wait_ge(xg_sig, i * 2 + (t + 1))
                    eng.tensor_tensor(glu[:, t, :].rearrange("p (h c) -> p h c", h=2), ps[:, b:b + 2, 0:HALF],
                                      sg[:, t, :].rearrange("p (h c) -> p h c", h=2), ALU.mult).then_inc(glu_ready, 1)
                eng.wait_ge(glu_ready, i * 2 + 2)
                for t in range(2):
                    step.did(eng.tensor_scalar(cv[:, t, :], glu[:, t, :], cur[:, G_CDW + MID, t:t + 1], cur[:, G_CDB, t:t + 1],
                                               ALU.mult, ALU.add))
                    behind = {True: step.n, False: step.n}
                    for n, (k, lo, hi, s) in enumerate(ranges):
                        eng.wait_ge(dve_step, behind[lo < NP])
                        ins = eng.scalar_tensor_tensor(out=cv[:, t, lo:hi], in0=glu[:, t, lo + s:hi + s],
                                                       scalar=cur[:, G_CDW + k, t:t + 1], in1=cv[:, t, lo:hi],
                                                       op0=ALU.mult, op1=ALU.add)
                        if n < len(ranges) - 1:
                            step.did(ins)
                            behind[lo < NP] = step.n
                        else:
                            ins.then_inc(conv_done, 1)
                for n in range(4):
                    t, d = n // 2, n % 2
                    eng.wait_ge(decay_sq, i * 4 + (n + 1))
                    eng.scalar_tensor_tensor(out=lr_q[:, t, d, :], in0=lr_q[:, t, d, :], scalar=1.0, in1=lr_r[:, t, d, :],
                                             op0=ALU.add, op1=ALU.mult).then_inc(in_sq, 1)
                for n in range(4):
                    t, d = n // 2, n % 2
                    eng.wait_ge(in_root, i * 4 + (n + 1))
                    eng.wait_ge(ix_ready, i * 4 + (n + 1))
                    step.did(eng.tensor_tensor(lr_q[:, t, d, :], lr_q[:, t, d, :], lr_i[:, t, d, :], ALU.mult))
                step.wait()
                for n in range(4):
                    t, d = n // 2, n % 2
                    for lo, hi, h0 in ((0, NP, 0.0), (S0, S0 + NS, cur[:, G_STATE + d, t:t + 1])):
                        h, av, bv = lr_r[:, t, d, lo:hi], lr_a[:, t, d, lo:hi], lr_q[:, t, d, lo:hi]
                        if d:
                            h, av, bv = h[:, ::-1], av[:, ::-1], bv[:, ::-1]
                        step.did(eng.tensor_tensor_scan(out=h, data0=av, data1=bv, initial=h0, op0=ALU.mult, op1=ALU.add))
                step.wait()
                for t in range(2):
                    for lo, to, n in ((0, 0, NP), (S0, NP, NS)):
                        step.did(eng.tensor_tensor(ya[:, bass.ds(i * 2 + t, 1), to:to + n].rearrange("p a c -> p (a c)"),
                                                   lr_r[:, t, 0, lo:lo + n], lr_r[:, t, 1, lo:lo + n], ALU.add))
                step.did(eng.tensor_copy(last[:, 0, bass.ds(i * 2, 2)], lr_r[:, :, 0, NP - 1]))
                eng.wait_ge(cv_copied, i * 2 + 2)
                eng.tensor_copy(last[:, 1, bass.ds(i * 2, 2)], lr_r[:, :, 1, 0]).then_inc(lru_done, 1)
                step.restart()
            def piece_low(q):
                eng.wait_ge(piece_hi, q + 1)
                eng.tensor_tensor(b_lo[:, q % 4, :, :], b_raw[:, q % 4, :, :], b_hi[q % 4][:, :, :].bitcast(F32), ALU.subtract)\
                    .then_inc(piece_split, 1)

            def centre(k0, k1):
                for k in range(k0, k1):
                    eng.tensor_tensor(cu[:, k, :], cu[:, k, :], ln_mu, ALU.add).then_inc(ln_centred, 1)

            def yb_low(k0, k1):
                for k in range(k0, k1):
                    eng.wait_ge(yb_hi_ready, k + 1)
                    eng.tensor_tensor(yb_lo[:, k, :], cu[:, k, :], y_hi[:, k, :].bitcast(F32), ALU.subtract).then_inc(yb_split, 1)

            def merge_tiles(g):
                for t in range(NT):
                    n = NT * g + t
                    eng.wait_ge(tile_done, n + 1)
                    eng.wait_ge(gate_ready, NT * (g // 2) + t + 1)
                    m = merged[:, t, 512 * (g // 2 % 2):512 * (g // 2 % 2) + 512]
                    if g < 4:
                        eng.tensor_tensor(m, gate_rows[t], ps[:, tile_bank(n), :], ALU.mult).then_inc(m_ready, 1)
                    else:
                        step.did(eng.tensor_tensor(gate_rows[t], gate_rows[t], ps[:, tile_bank(n), :], ALU.mult))
                        step.wait()
                        eng.tensor_tensor(m, m, gate_rows[t], ALU.add).then_inc(m_ready, 1)

            for h in range(2):
                eng.wait_ge(y_hi_ready, h + 1)
                eng.tensor_tensor(ya_lo[:, 4 * h:4 * h + 4, :], ya[:, 4 * h:4 * h + 4, :], y_hi[:, 4 * h:4 * h + 4, :].bitcast(F32),
                                  ALU.subtract).then_inc(y_split, 1)
            eng.wait_ge(last_turned, 1)
            eng.tensor_copy(last_t[:, :], ps[0:16, 7, 0:P]).then_inc(last_ready, 1)
            piece_low(0)
            piece_low(1)
            eng.wait_ge(ln_summed, 1)
            step.did(eng.tensor_scalar(ln_mu.rearrange("p (h c) -> p h c", h=2), ps[:, 5:7, 0:HALF], -1.0 / D, None, ALU.mult))
            step.wait()
            centre(0, 4)
            piece_low(2)
            centre(4, 8)
            piece_low(3)
            for h in range(2):
                eng.wait_ge(u_hi_ready, h + 1)
                eng.tensor_tensor(u_lo[:, 4 * h:4 * h + 4, :], uT[:, 4 * h:4 * h + 4, :], u_hi[:, 4 * h:4 * h + 4, :].bitcast(F32),
                                  ALU.subtract).then_inc(u_split, 1)
            piece_low(4)
            piece_low(5)
            eng.wait_ge(ln_sq_used, KD)
            eng.tensor_scalar(ln_rs.rearrange("p (h c) -> p h c", h=2), ps[:, 5:7, 0:HALF], 1.0 / D, EPS, ALU.mult, ALU.add)\
                .then_inc(ln_var, 1)
            merge_tiles(1)
            piece_low(6)
            piece_low(7)
            eng.wait_ge(ln_root, 1)
            step.did(eng.reciprocal(ln_rs, ln_rs))
            eng.wait_ge(ln_centred, KD)
            for g in range(2, 8):
                if g == 4:
                    yb_low(0, 4)
                piece_low(4 * g)
                if g == 2:
                    step.wait()
                    for k in range(KD):
                        eng.tensor_tensor(cu[:, k, :], cu[:, k, :], ln_rs, ALU.mult).then_inc(ln_scaled, 1)
                if g == 4:
                    yb_low(4, 8)
                piece_low(4 * g + 1)
                if g % 2:
                    merge_tiles(g)
                piece_low(4 * g + 2)
                piece_low(4 * g + 3)
            for k in range(KD):
                eng.wait_ge(mt_hi_ready, k + 1)
                eng.tensor_tensor(u_lo[:, k, :], ps[:, 2 * (k % 4):2 * (k % 4) + 2, :].rearrange("p b c -> p (b c)")[:, 0:N],
                                  u_hi[:, k, :].bitcast(F32), ALU.subtract).then_inc(mt_split, 1)
            eng.wait_ge(rows_loaded, 16 * 10)
            step.did(eng.tensor_tensor(g1b, g1b, g1b_lo, ALU.add))
            step.did(eng.tensor_tensor(g2b, g2b, g2b_lo, ALU.add))
            step.wait()
            for s in range(2):
                step.did(eng.tensor_tensor(g1b[:, s, :], g1b[:, s, :], bias1, ALU.add))
            eng.tensor_tensor(g2b, g2b, bias2[0:CAP, :], ALU.add).then_inc(rows_ready, 1)
            step.wait()

            def residual(h, t):
                n = NT * (8 + h) + t
                eng.wait_ge(tile_done, n + 1)
                b = 5 + t % 2 if h else tile_bank(n)
                x = xr[:, t, 512 * h:512 * h + 512]
                step.did(eng.tensor_tensor(prod[:, t % 2, :], ps[:, b, :], g1b[:, min(t, 1), 512 * h:512 * h + 512], ALU.mult))
                step.wait()
                eng.tensor_tensor(x, x, prod[:, t % 2, :], ALU.add).then_inc(x2_ready, 1)

            def modulate_half(t):
                eng.wait_ge(vt_turned, t + 1)
                for k in range(4):
                    ins = eng.tensor_scalar(vT[:, k, P * t:P * t + P], ps[:, 2 * (t % 2), P * k:P * k + P],
                                            a2[:, k, min(t, 1):min(t, 1) + 1], modc[:, 24 + k, min(t, 1):min(t, 1) + 1],
                                            ALU.mult, ALU.add)
                ins.then_inc(vt_dve, 1)

            def logits(t):
                eng.wait_ge(logit_done, t + 1)
                eng.tensor_copy(lg[:, P * t:P * t + P], ps[0:E, 4, P * (t % 4):P * (t % 4) + P]).then_inc(lg_ready, 1)

            for t in range(NT):
                residual(0, t)
            for q in range(32, 36):
                piece_low(q)
            for t in range(NT):
                residual(1, t)
                inverse_root(ssq2_ready, t + 1, ms2_ready, root2_ready, t, t + 1)
                eng.wait_ge(root2_ready, t + 1)
                eng.reciprocal(rstat[:, 3, t:t + 1], rstat[:, 2, t:t + 1]).then_inc(r2_ready, 1)
                if t:
                    modulate_half(t - 1)
                if t >= 2:
                    logits(t - 2)
            modulate_half(NT - 1)
            logits(NT - 2)
            logits(NT - 1)
            eng.wait_ge(lg_turned, 1)
            step.did(eng.tensor_reduce(sstat[:, 2, :], ps[:, 5, 0:16 * NT].rearrange("p (t e) -> p t e", e=E), AX.X, ALU.max))
            step.wait()
            eng.tensor_scalar(sstat[:, 0, :], sstat[:, 2, :], -1.0, None, ALU.mult).then_inc(max_ready, 1)
            eng.wait_ge(exp_ready, NT)
            step.did(eng.reciprocal(sstat[:, 2, :], sstat[:, 1, :]))
            step.wait()
            for t in range(NT):
                eng.tensor_scalar(soft[:, t, :], soft[:, t, :], sstat[:, 2, t:t + 1], None, ALU.mult).then_inc(soft_ready, 1)
            eng.wait_ge(soft_turned, NT)
            step.did(eng.tensor_copy(lg[:, 0:NP], ps[0:E, 6, 0:NP]))
            step.did(eng.tensor_copy(lg[:, NP:N], ps[0:E, 7, :]))
            step.wait()
            for rows, first, rounds in ((lg[:, NP:N], 0, CAP_S // 8), (lg[:, 0:NP], CAP_S, CAP_P // 8)):
                for r in range(rounds):
                    best = gates_e[:, first + 8 * r:first + 8 * r + 8]
                    step.did(eng.max(best, rows))
                    step.wait()
                    step.did(eng.max_index(idx[:, first + 8 * r:first + 8 * r + 8], best, rows))
                    if r < rounds - 1:
                        step.wait()
                        step.did(eng.match_replace(rows, best, rows, -1.0))
                        step.wait()
            step.wait()
            step.did(eng.tensor_scalar(idx_f[:, 0:CAP_S], idx[:, 0:CAP_S], float(NP), None, ALU.add))
            eng.tensor_copy(idx_f[:, CAP_S:CAP], idx[:, CAP_S:CAP]).then_inc(top_ready, 1)
            eng.wait_ge(top_turned, 1)
            eng.tensor_copy(idx_t[:, 0:E], ps[0:CAP, 0, 0:E]).then_inc(idx_ready, 1)
            eng.tensor_copy(idx_t[:, E:E + 1], ps[0:CAP, 0, E - 1:E]).then_inc(idx_ready, 1)
            eng.tensor_copy(gate_t[:, :], ps[0:CAP, 0, E:2 * E]).then_inc(idx_ready, 1)
            eng.wait_ge(idx_ready, 3)
            eng.wait_ge(rows_ready, 1)

            def modulate_xe():
                for k in range(KD):
                    b, c = 6 + k // 4, CAP * (k % 4)
                    for s, lo, hi in ((1, 0, CAP_S), (0, CAP_S, CAP)):
                        ins = eng.tensor_scalar(xeT[:, k, lo:hi], ps[:, b, c + lo:c + hi], a2[:, k, s:s + 1],
                                                modc[:, 24 + k, s:s + 1], ALU.mult, ALU.add)
                ins.then_inc(xe_modulated, 1)

            def split_piece(i, m):
                for half in range(2):
                    w = chunk(m)[:, 2 * half:2 * half + 2, :]
                    eng.wait_ge(unit_hi, units(i, m, half))
                    eng.tensor_tensor(w_lo(m)[:, 2 * half:2 * half + 2, :], w,
                                      w_hi[m % 2][:, 2 * half:2 * half + 2, :].bitcast(F32), ALU.subtract)\
                        .then_inc(unit_split, 1)

            def split_xe(n):
                eng.wait_ge(xe_turned, n)
                modulate_xe()
                eng.wait_ge(xe_hi_ready, n)
                eng.tensor_tensor(xe_lo[:, :, :], xeT[:, :, :], xe_hi[:, :, :].bitcast(F32), ALU.subtract).then_inc(xeT_ready, 1)

            def hidden(i, half):
                eng.wait_ge(h1_silu, i * 2 + (half + 1))
                product_done(eng, i, 4 * half + 3)
                v = hs[:, half * D:(half + 1) * D].rearrange("c (b f) -> c b f", b=2)
                eng.tensor_tensor(v, v, ps[0:CAP, 2:4, :], ALU.mult).then_inc(h_ready, 1)

            def split_h(i, half):
                eng.wait_ge(h_hi_ready, i * 2 + (half + 1))
                hi, lo = (x[:, 8 * half:8 * half + 8, :].rearrange("p (b k) c -> p b (k c)", b=2) for x in (h_hi, h_lo))
                eng.tensor_tensor(lo, ps[:, 6:8, 0:4 * CAP], hi.bitcast(F32), ALU.subtract).then_inc(hT_ready, 1)

            def output(i):
                product_done(eng, i, 11)
                gate = gate_t[:, E - 1:E] if i is E - 1 else gate_t[:, bass.ds(i, 1)]
                eng.scalar_tensor_tensor(out=ye.rearrange("c (b f) -> c b f", b=2), in0=ps[0:CAP, 4:6, :], scalar=gate,
                                         in1=g2b.rearrange("c (b f) -> c b f", b=2), op0=ALU.mult, op1=ALU.mult)\
                    .then_inc(ye_ready, 1)

            def dve_expert(i, final):
                for m in range(2, 12):
                    split_piece(i, m)
                    if m == 5:
                        hidden(i, 0)
                    if m == 7:
                        split_h(i, 0)
                    if m == 9:
                        hidden(i, 1)
                    if m == 10:
                        split_h(i, 1)
                split_xe(i + 2)
                if not final:
                    for m in range(2):
                        split_piece(i + 1, m)
                output(i)

            split_piece(0, 0)
            split_xe(1)
            split_piece(0, 1)
            with eng.Fori(0, E - 1) as i:
                dve_expert(i, False)
            dve_expert(E - 1, True)

            eng.wait_ge(gf_loaded, 16)
            for t in range(NT):
                inverse_root(fin_ssq, t + 1, fin_ms, fin_root, t, t + 1)
                eng.wait_ge(fin_root, t + 1)
                step.did(eng.reciprocal(rstat[:, 3, t:t + 1], rstat[:, 2, t:t + 1]))
                step.wait()
                eng.scalar_tensor_tensor(out=xr[:, t, :], in0=xr[:, t, :], scalar=rstat[:, 3, t:t + 1], in1=gf,
                                         op0=ALU.mult, op1=ALU.mult).then_inc(out_ready, 1)

        @block.tensor
        def _(eng):
            eng.wait_ge(consts_ready, 4)
            eng.wait_ge(c_loaded, 32)
            eng.transpose(ps[:, 7, 0:2 * KD], c_rows[:, :], ident[0:2 * KD, 0:2 * KD]).then_inc(c_turned, 1)

            def mod_products(n):
                i, s = n // 4, n % 4
                for kk in range(2):
                    k = 2 * s + kk
                    if n % 2:
                        eng.wait_ge(mod_loaded[2 * s + kk], 16 * (i + 1))
                        operands = [(silu_c, slot(s)[:, 2 * D * kk:2 * D * kk + 2 * D])]
                    else:
                        eng.wait_ge(mod_split, n + kk + 1)
                        operands = [(silu_parts, mod_hi[:, n // 2 % 2, kk, :]), (silu_parts, mod_lo[:, s, kk, :])]
                    for b in range(4):
                        for part, (x, w) in enumerate(operands):
                            ins = eng.matmul(ps[0:4, 4 * (i % 2) + b, :], x[:, k, :], w[:, 512 * b:512 * b + 512],
                                             start=k == 0 and part == 0, stop=k == KD - 1)
                    ins.then_inc(mod_used, 1)

            def mod_turn(i):
                eng.wait_ge(mod_tiled, 16 * i + 16)
                eng.transpose(ps[:, 4 * (i % 2), 0:64], mod_tiles[:, :], ident[0:64, 0:64]).then_inc(mod_turned, 1)

            def turn_row_tile(rows, k, banks, done, emptied):
                if k >= banks // 2:
                    for e in emptied:
                        eng.wait_ge(e, k - banks // 2 + 1)
                for t in range(NT):
                    b = 2 * (k % (banks // 2)) + (t == 0)
                    c = 0 if t == 0 else P * (t - 1)
                    ins = eng.transpose(ps[:, b, c:c + P], rows[:, t, P * k:P * k + P], ident[:, :])
                ins.then_inc(done, 1)

            eng.wait_ge(silu_split, 1)
            for n in range(4):
                mod_products(n)
            eng.wait_ge(vec_loaded, 16 * 13)
            first = C_TAB + 8 * G_RCW
            for tile, rows, to in ((0, first, 0), (1, 80, first), (2, P, first + 80), (3, 8 * TAPS31 - P, first + 80 + P)):
                ins = eng.transpose(ps[:, 6, to:to + rows], vecs[0:rows, tile, :], ident[0:rows, 0:rows])
            ins.then_inc(cols_turned, 1)
            eng.wait_ge(cols_ready, 1)
            mod_products(4)
            mod_products(5)
            mod_turn(0)
            eng.wait_ge(xn1_ready, NT)
            eng.wait_ge(modc_ready, 1)
            mod_products(6)
            for k in range(KD // 2):
                turn_row_tile(xn1, k, 4, xt_turned, (ut_sample, ut_prompt))
            mod_products(7)
            for k in range(KD // 2, KD):
                turn_row_tile(xn1, k, 4, xt_turned, (ut_sample, ut_prompt))
            eng.wait_ge(ut_sample, KD)
            eng.wait_ge(ut_prompt, KD)
            mod_products(8)
            mod_products(9)
            mod_products(10)
            mod_turn(1)
            mod_products(11)
            mod_turn(2)
            eng.wait_ge(modc_ready, 3)

            with eng.Fori(0, 4) as i:
                for n, (kind, t, done) in enumerate(((0, 0, xr_done), (0, 1, xr_done), (1, 0, xv_done), (2, 0, xg_done),
                                                     (1, 1, xv_done), (2, 1, xg_done))):
                    if t == 0:
                        eng.wait_ge(wa_loaded[kind], i * 16 + 16)
                    if n >= 4:
                        eng.wait_ge(xr_copied, i * 2 + (n - 3))
                    b = 2 * (n % 4)
                    for k in range(KD):
                        for h in range(2):
                            ins = eng.matmul(ps[:, b + h, 0:HALF], wa(kind)[:, k, P * t:P * t + P],
                                             uT[:, k, HALF * h:HALF * h + HALF], start=k == 0, stop=k == KD - 1)
                    ins.then_inc(done, 1)
                eng.wait_ge(gw_loaded, i * 64 + 64)
                for n in range(8):
                    t, d, g = n // 4, n // 2 % 2, n % 2
                    b = 2 * ((6 + n) % 4)
                    if g == 0 and d == 0:
                        eng.wait_ge(xc_ready, i * 2 + (t + 1))
                    if n == 0 or n == 2:
                        eng.wait_ge(glu_ready, i * 2 + (n // 2 + 1))
                    if n >= 4:
                        eng.wait_ge(gate_sig, i * 8 + (n - 3))
                    for h in range(2):
                        ins = eng.matmul(ps[:, b + h, 0:LX // 2], gw[:, t, 2 * d + g, :],
                                         xc[:, t, LX // 2 * h:LX // 2 * (h + 1)], start=True, stop=True)
                    ins.then_inc(gate_done, 1)
                eng.wait_ge(gate_sig, i * 8 + 8)

            def bank_free(g, t):
                n = NT * g + t - 6
                if n >= 0:
                    eng.wait_ge(m_ready if n // NT % 2 else gate_ready, NT * (n // NT // 2) + n % NT + 1)

            def products(g, p, x_hi, x_lo):
                q = 4 * (g - 1) + p
                eng.wait_ge(piece_split, q + 1)
                for t in range(NT):
                    if p == 0:
                        bank_free(g, t)
                    for kk in range(2):
                        k = 2 * p + kk
                        for n, (x, w) in enumerate(((x_hi, b_hi[q % 4][:, kk, :]), (x_hi, b_lo[:, q % 4, kk, :]),
                                                    (x_lo, b_hi[q % 4][:, kk, :]))):
                            ins = eng.matmul(ps[:, tile_bank(NT * g + t), :], x[:, k, P * t:P * t + P], w,
                                             start=k == 0 and n == 0, stop=k == KD - 1 and n == 2)
                    if p == 3:
                        ins.then_inc(tile_done, 1)
                if p < 3:
                    ins.then_inc(piece_used, 1)

            for n in range(2):
                eng.wait_ge(g0_loaded[n], 16)
                for t in range(NT):
                    for k in range(4 * n, 4 * n + 4):
                        ins = eng.matmul(ps[:, tile_bank(t), :], uT[:, k, P * t:P * t + P], g0_w[n][:, k - 4 * n, :],
                                         start=k == 0, stop=k == KD - 1)
                    if n == 1:
                        ins.then_inc(tile_done, 1)
                if n == 0:
                    ins.then_inc(g0_used, 1)
            eng.wait_ge(lru_done, 4)
            eng.transpose(ps[0:16, 7, 0:P], flat(last), ident[:, :]).then_inc(last_turned, 1)
            for h in range(2):
                for k in range(KD):
                    ins = eng.matmul(ps[:, 5 + h, 0:HALF], ones[:, :], cu[:, k, HALF * h:HALF * h + HALF],
                                     start=k == 0, stop=k == KD - 1)
            ins.then_inc(ln_summed, 1)
            eng.wait_ge(last_ready, 1)
            for g in range(1, 8):
                for p in range(4):
                    if g % 2 == 0:
                        if g == 2:
                            eng.wait_ge(u_split, p // 2 + 1)
                        products(g, p, u_hi, u_lo)
                    elif g < 4:
                        if g == 1:
                            eng.wait_ge(y_split, p // 2 + 1)
                        products(g, p, y_hi, ya_lo)
                    else:
                        if g == 5:
                            eng.wait_ge(yb_split, 2 * p + 2)
                        products(g, p, y_hi, yb_lo)
                    if g == 1:
                        for k in (2 * p, 2 * p + 1):
                            eng.wait_ge(ln_squared, k + 1)
                            for h in range(2):
                                ins = eng.matmul(ps[:, 5 + h, 0:HALF], ones[:, :], ln_sq[:, k % 2, HALF * h:HALF * h + HALF],
                                                 start=k == 0, stop=k == KD - 1)
                            ins.then_inc(ln_sq_used, 1)
            eng.wait_ge(m_ready, NT * 4)
            for k in range(KD):
                if k >= 4:
                    eng.wait_ge(mt_split, k - 3)
                for t in range(NT):
                    ins = eng.transpose(ps[:, 2 * (k % 4) + t // 4, P * (t % 4):P * (t % 4) + P], merged[:, t, P * k:P * k + P],
                                        ident[:, :])
                ins.then_inc(mt_turned, 1)
            eng.wait_ge(mt_split, KD)
            for p in range(4):
                products(8, p, u_hi, u_lo)

            def last_products(t):
                if t >= 2:
                    eng.wait_ge(x2_ready, NT + t - 1)
                for k in range(KD):
                    if t == 0 and k % 2 == 0:
                        eng.wait_ge(piece_split, 33 + k // 2)
                    for n, (x, w) in enumerate(((u_hi, b_hi[k // 2][:, k % 2, :]), (u_hi, b_lo[:, k // 2, k % 2, :]),
                                                (u_lo, b_hi[k // 2][:, k % 2, :]))):
                        ins = eng.matmul(ps[:, 5 + t % 2, :], x[:, k, P * t:P * t + P], w,
                                         start=k == 0 and n == 0, stop=k == KD - 1 and n == 2)
                ins.then_inc(tile_done, 1)

            def turn_normed(t):
                eng.wait_ge(xn2_ready, t + 1)
                if t >= 2:
                    eng.wait_ge(vt_dve, t - 1)
                    eng.wait_ge(vt_act, t - 1)
                for k in range(KD):
                    ins = eng.transpose(ps[:, 2 * (t % 2) + k // 4, P * (k % 4):P * (k % 4) + P], xn2[:, t, P * k:P * k + P],
                                        ident[:, :])
                ins.then_inc(vt_turned, 1)

            def router(t):
                eng.wait_ge(vt_dve, t + 1)
                eng.wait_ge(vt_act, t + 1)
                if t >= 1:
                    eng.wait_ge(lg_ready, t)
                for k in range(KD):
                    ins = eng.matmul(ps[0:E, 4, P * (t % 4):P * (t % 4) + P], wr[:, k, :], vT[:, k, P * t:P * t + P],
                                     start=k == 0, stop=k == KD - 1)
                ins.then_inc(logit_done, 1)

            eng.wait_ge(wr_loaded, 16)
            for t in range(NT):
                last_products(t)
                if t == 2:
                    eng.wait_ge(x2_ready, NT)
                if t >= 2:
                    turn_normed(t - 2)
                if t >= 3:
                    router(t - 3)
            turn_normed(3)
            router(2)
            turn_normed(4)
            router(3)
            router(4)
            for t in range(NT):
                eng.wait_ge(lg_ready, t + 1)
                ins = eng.transpose(ps[:, 5, 16 * t:16 * t + 16], lg[:, P * t:P * t + P], ident[0:E, 0:E])
            ins.then_inc(lg_turned, 1)
            for t in range(NT):
                eng.wait_ge(soft_ready, t + 1)
                b, c = (6, 0) if t == 0 else (7, P * (t - 1))
                eng.transpose(ps[0:E, b, c:c + P], soft[:, t, :], ident[:, :]).then_inc(soft_turned, 1)
            eng.wait_ge(top_ready, 1)
            eng.transpose(ps[0:CAP, 0, 0:E], idx_f[:, :], ident[0:E, 0:E])
            eng.transpose(ps[0:CAP, 0, E:2 * E], gates_e[:, :], ident[0:E, 0:E]).then_inc(top_turned, 1)

            def turn_xe(n):
                eng.wait_ge(xe_loaded, n * 16)
                for k in range(KD):
                    ins = eng.transpose(ps[:, 6 + k // 4, CAP * (k % 4):CAP * (k % 4) + CAP], xe[:, P * k:P * k + P],
                                        ident[0:CAP, 0:CAP])
                ins.then_inc(xe_turned, 1)

            def turn_h(half):
                for k in range(8):
                    ins = eng.transpose(ps[:, 6 + k // 4, CAP * (k % 4):CAP * (k % 4) + CAP],
                                        hs[:, (8 * half + k) * P:(8 * half + k + 1) * P], ident[0:CAP, 0:CAP])
                ins.then_inc(h_turned, 1)

            eng.wait_ge(idx_ready, 3)
            turn_xe(1)
            with eng.Fori(0, E) as i:
                eng.wait_ge(xeT_ready, i + 1)

                def rows_times(m, bank, x_hi, x_lo, k0, first, last_one):
                    eng.wait_ge(unit_split, units(i, m))
                    for kk in range(4):
                        for b in range(2):
                            for n, (x, w) in enumerate(((x_hi, w_hi[m % 2]), (x_hi, w_lo(m)), (x_lo, w_hi[m % 2]))):
                                ins = eng.matmul(ps[0:CAP, bank + b, :], x[:, k0 + kk, :],
                                                 w[:, kk, 512 * b:512 * b + 512],
                                                 start=first and kk == 0 and n == 0, stop=last_one and kk == 3 and n == 2)
                        if kk % 2:
                            ins.then_inc(unit_used, 1)

                def token_product(m, bank):
                    for part in range(2):
                        rows_times(m + part, bank, xe_hi, xe_lo, 4 * part, part == 0, part == 1)

                def hidden_product(m):
                    rows_times(m, 4, h_hi, h_lo, 4 * (m - 8), m == 8, m == 11)

                token_product(0, 0)
                token_product(2, 2)
                eng.wait_ge(h1_silu, i * 2 + 1)
                token_product(4, 0)
                eng.wait_ge(h_ready, i * 2 + 1)
                turn_h(0)
                token_product(6, 2)
                eng.wait_ge(hT_ready, i * 2 + 1)
                hidden_product(8)
                eng.wait_ge(h_ready, i * 2 + 2)
                turn_h(1)
                hidden_product(9)
                eng.wait_ge(hT_ready, i * 2 + 2)
                turn_xe(i + 2)
                hidden_product(10)
                hidden_product(11)


_INS = ["x_prompt", "x_sample", "state_rglru", "c", "c_ctx", "norm1_g", "norm2_g", "w_mod", "b_mod", "w_in",
        "rnn_conv_w", "rnn_conv_b", "rnn_gate_w", "rnn_gate_b", "rnn_lambda", "w_rnn_out", "conv_dw_w", "conv_dw_b",
        "conv_ln_g", "conv_ln_b", "w_conv_out", "w_out", "w_router", "w_e1", "w_e3", "w_e2", "final_norm_g"]
_OUTS = [("y_prompt", (1, NP, D)), ("y_sample", (1, NS, D)), ("new_state", (1, 1, 2, D))]


def kernel(**inputs):
    import numpy as np
    from concourse import bacc
    from concourse.bass_utils import run_bass_kernel_spmd

    nc = bacc.Bacc("TRN2", target_bir_lowering=False, num_devices=1)
    arrays, args = {}, {}
    for name in _INS:
        x = np.ascontiguousarray(inputs[name])
        arrays[f"in_{name}"] = x
        args[name] = nc.dram_tensor(f"in_{name}", x.shape, mybir.dt.from_np(x.dtype), kind="ExternalInput").ap()
    for name, shape in _OUTS:
        args[name] = nc.dram_tensor(f"out_{name}", shape, F32, kind="ExternalOutput").ap()
    trunk_layer(nc, args)
    r = run_bass_kernel_spmd(nc, [arrays], core_ids=[0])
    return tuple(r.results[0][f"out_{name}"] for name, _ in _OUTS)
```

```python
from contextlib import ExitStack

import concourse.bass as bass
from concourse import mybir

P = 128
D = 1024
KD = D // P
NP, NS = 128, 512
N = NP + NS
NT = N // P
HALF = N // 2
GRID_W = 64
GRID_H = NS // GRID_W
TAPS4 = 4
TAPS31 = 31
MID = TAPS31 // 2
E = 16
FF = 2 * D
KF = FF // P
CAP_P = 2 * NP // E
CAP_S = 2 * NS // E
CAP = CAP_S + CAP_P
DIN = 5 * D
EPS = 1e-6
RG_C = 8.0

S0 = NP + 3
LX = 644
LXP = LX + TAPS4

ALU = mybir.AluOpType
ACT = mybir.ActivationFunctionType
AX = mybir.AxisListType
F32 = mybir.dt.float32
F32R = mybir.dt.float32r
U32 = mybir.dt.uint32

C_BMOD, C_N1, C_N2, C_LNG, C_LNB, C_TAB = 0, 48, 56, 64, 72, 80
G_STATE, G_RCB, G_CDB, G_RCW, G_GB, G_LAM, G_CDW, G_NLAM = 0, 2, 3, 4, 8, 12, 14, 45
NG = 47
NCOLS = C_TAB + 8 * NG

SLOT = 4096
NSLOT = 6
WA_OFF = 0
TEMPS = 2 * SLOT
GATE_BANKS = (4, 0, 6, 2)
MOE_SLOTS = [0, 1, 2, 3, 4, 5]


class Steps:

    def __init__(self, eng, sem):
        self.eng, self.sem, self.n = eng, sem, 0

    def did(self, ins):
        ins.then_inc(self.sem, 1)
        self.n += 1

    def wait(self, back=0):
        if self.n > back:
            self.eng.wait_ge(self.sem, self.n - back)

    def restart(self):
        self.wait()
        self.eng.sem_clear(self.sem)
        self.n = 0


def conv_ranges():
    prompt, sample = [], []
    for k in range(TAPS31):
        s = k - MID
        if s:
            a, b = max(0, -s), min(NP, NP - s)
            prompt.append((k, a, b, s))
        if s and abs(s) < GRID_H:
            a, b = max(0, -s) * GRID_W, (GRID_H - max(0, s)) * GRID_W
            sample.append((k, NP + a, NP + b, s * GRID_W))
    out = []
    while prompt or sample:
        out += [c.pop(0) for c in (prompt, sample) if c]
    return out


def trunk_layer(nc, a):
    x_prompt = a["x_prompt"][0]
    x_sample = a["x_sample"][0].rearrange("(t p) d -> t p d", p=P)
    w_in = a["w_in"][0].rearrange("(k p) c -> p k c", p=P)
    w_mod = a["w_mod"][0].rearrange("(k p) c -> p k c", p=P)
    w_ro = a["w_rnn_out"][0].rearrange("(k p) c -> p k c", p=P)
    w_co = a["w_conv_out"][0].rearrange("(k p) c -> p k c", p=P)
    w_out = a["w_out"][0].rearrange("(k p) c -> p k c", p=P)
    w_router = a["w_router"][0].rearrange("(k p) e -> p k e", p=P)
    w_e1 = a["w_e1"][0].rearrange("e (k p) f -> e p k f", p=P)
    w_e3 = a["w_e3"][0].rearrange("e (k p) f -> e p k f", p=P)
    w_e2 = a["w_e2"][0].rearrange("e (k p) f -> e p k f", p=P)
    w_e2_rows = a["w_e2"][0].rearrange("e (q k p) f -> p (e q) k f", k=4, p=P)
    gate_w = a["rnn_gate_w"][0].rearrange("a g h i j -> i (a g) h j")

    mod_rows = nc.dram_tensor("mod_rows", [4, 6 * D], F32, kind="Internal").ap()
    xn_dram = nc.dram_tensor("xn_dram", [N, D], F32, kind="Internal").ap()
    acc_dram = nc.dram_tensor("acc_dram", [N, D], F32, kind="Internal").ap()

    with ExitStack() as ctx:
        place = {}

        def sb(name, shape, dt=F32):
            place[name] = -(-nc.sbuf_base // 32) * 32
            return ctx.enter_context(nc.sbuf_tensor(name, shape, dt))

        def rounded(name, under, at, *shape):
            return nc.alloc_sbuf_tensor_at(name, [P, *shape], F32R, offset=place[under] + 4 * at)

        def sem(name):
            return ctx.enter_context(nc.semaphore(name))

        ring = sb("ring", [P, NSLOT * SLOT])
        uT = sb("uT", [P, KD, N])
        xr = sb("xr", [P, NT, D])
        ya = sb("ya", [P, KD, N])
        cu = sb("cu", [P, KD, N])
        xpad = sb("xpad", [P, 2, LXP])
        sg = sb("sg", [P, 2, N])
        gw = sb("gw", [P, 2, 4, P])
        cols = sb("cols", [P, NCOLS])
        cur = sb("cur", [P, NG, 2])
        cur_taps = sb("cur_taps", [P, G_RCW + 1 - G_RCB, 2])
        modc = sb("modc", [P, 48, 2])
        a1 = sb("a1", [P, KD, 2])
        a2 = sb("a2", [P, KD, 2])
        ident = sb("ident", [P, P])
        ones = sb("ones", [P, P])
        vecs = sb("vecs", [P, 4, P])
        c_rows = sb("c_rows", [2 * KD, P])
        mod_tiles = sb("mod_tiles", [4 * 16, P])
        silu_c = sb("silu_c", [P, KD, 4])
        silu_parts = sb("silu_parts", [P, KD, 4], F32R)
        sp = sb("sp", [P, 5, 16])
        ln_sq = sb("ln_sq", [P, 2, N])
        last = sb("last", [P, 2, KD])
        last_t = sb("last_t", [16, P])
        wr = sb("wr", [P, KD, E])
        rstat = sb("rstat", [P, 4, NT])
        soft = sb("soft", [P, NT, E])
        sstat = sb("sstat", [P, 3, NT])
        lg = sb("lg", [E, N])
        idx = sb("idx", [E, CAP], U32)
        idx_f = sb("idx_f", [E, CAP])
        gates_e = sb("gates_e", [E, CAP])
        idx_t = sb("idx_t", [CAP, E + 1], U32)
        gate_t = sb("gate_t", [CAP, E])
        idx_g = sb("idx_g", [CAP, 1], U32)
        idx_s = sb("idx_s", [CAP, 1], U32)
        ps = ctx.enter_context(nc.psum_tensor("ps", [P, 8, 512], F32))

        turned_merged = ps[:, 5:7, :].rearrange("p b c -> p (b c)")[:, 0:N]

        def flat(t):
            return t[:, :, :].rearrange("p a b -> p (a b)")

        ya_f, cu_f = flat(ya), flat(cu)

        def slot(s, n=1):
            return ring[:, s * SLOT:(s + n) * SLOT]

        def temps(at, *shape):
            n = 1
            for s in shape:
                n *= s
            v = ring[:, TEMPS + at:TEMPS + at + n]
            names = "abcd"[:len(shape)]
            if len(shape) == 1:
                return v
            return v.rearrange(f"p ({' '.join(names)}) -> p {' '.join(names)}",
                               **dict(zip(names[1:], shape[1:])))

        at = 0
        lr_r = temps(at, 2, 2, LX)
        lr_i = temps(at + 4 * LX, 2, 2, LX)
        lr_a = temps(at + 8 * LX, 2, 2, LX)
        lr_q = temps(at + 12 * LX, 2, 2, LX)
        at = 16 * LX
        glu = temps(at, 2, N)
        cv = temps(at + 2 * N, 2, N)
        xc = temps(at + 4 * N, 2, LX)
        ln_mu = gw[:, :, :, :].rearrange("p a b c -> p (a b c)")[:, 0:N]
        ln_rs = ring[:, 2 * SLOT:2 * SLOT + N]
        at = 2 * SLOT + D
        merged = ring[:, at:at + NT * D].rearrange("p (t d) -> p t d", t=NT)
        vT = ring[:, at:at + N * KD].rearrange("p (k c) -> p k c", k=KD)
        gate_rows2 = [ring[:, at + NT * D + 512 * t:at + NT * D + 512 * (t + 1)] for t in range(NT)]
        m_hi = rounded("m_hi", "ring", at + NT * D, KD, N)
        y_hi = rounded("y_hi", "ring", at + 2 * NT * D, KD, N)
        u_hi = rounded("u_hi", "xr", 0, KD, N)
        u_lo = rounded("u_lo", "uT", 0, KD, N)
        m_lo = rounded("m_lo", "uT", 0, KD, N)
        a_lo = rounded("a_lo", "ring", WA_OFF, 3, KD, 256)
        a_hi = [rounded(f"a_hi{n}", "ring", c, KD, 256) for n, c in enumerate((6 * D, 22 * D))]
        ya_lo = rounded("ya_lo", "ya", 0, KD, N)
        yb_lo = rounded("yb_lo", "cu", 0, KD, N)
        xn2 = ring[:, at + 2 * NT * D:at + 3 * NT * D].rearrange("p (t d) -> p t d", t=NT)
        b_raw = ring[:, 2 * D:6 * D].rearrange("p (n k c) -> p n k c", n=4, k=2)
        b_lo = rounded("b_lo", "ring", 2 * D, 4, 2, 512)
        b_hi = [rounded(f"b_hi{n}", "ring", c, 2, 512) for n, c in enumerate((0, D, 6 * D, 7 * D))]
        gate_rows = [flat(sg)[:, 0:512], flat(sg)[:, 512:1024], flat(xpad)[:, 0:512], flat(xpad)[:, 512:1024], flat(vecs)]
        xn1 = cu_f.rearrange("p (t d) -> p t d", t=NT)
        mod_row = ya_f[0:4, 0:2 * D]
        mod_lo = rounded("mod_lo", "ring", 0, 4, 2, 2 * D)
        mod_hi = rounded("mod_hi", "ring", 4 * SLOT, 2, 2, 2 * D)
        g1b = cu_f[:, 0:2 * D].rearrange("p (s d) -> p s d", s=2)
        bias1 = cu_f[:, 2 * D:3 * D]
        bias2 = ya_f[0:CAP, 4 * D:5 * D]
        g1b_lo = ya_f[:, D:3 * D].rearrange("p (s d) -> p s d", s=2)
        g2b_lo = ya_f[0:CAP, 3 * D:4 * D]
        prod = cu_f[:, 4 * D:5 * D].rearrange("p (b c) -> p b c", b=2)
        g2b = ya_f[0:CAP, 0:D]
        xe = ya_f[0:CAP, D:2 * D]
        ye = ya_f[0:CAP, 2 * D:3 * D]
        xeT = ya_f[:, 3 * D:3 * D + KD * CAP].rearrange("p (k c) -> p k c", k=KD)
        xe_hi = rounded("xe_hi", "ya", 3 * D + KD * CAP, KD, CAP)
        xe_lo = rounded("xe_lo", "ya", 3 * D, KD, CAP)
        h_hi = rounded("h_hi", "cu", 3 * D, KF, CAP)
        h_lo = rounded("h_lo", "sg", 0, KF, CAP)
        w_hi = [rounded("w_hi0", "uT", 0, 4, D), rounded("w_hi1", "xr", 0, 4, D)]
        ring_lo = rounded("ring_lo", "ring", 0, NSLOT, 4, D)
        hs = cu_f[0:CAP, 0:FF]
        gf = cu_f[:, 2 * D:3 * D]

        vec_loaded = sem("vec_loaded")
        x_loaded = sem("x_loaded")
        wr_loaded = sem("wr_loaded")
        consts_ready = sem("consts_ready")
        cols_turned = sem("cols_turned")
        cols_ready = sem("cols_ready")
        c_loaded = sem("c_loaded")
        c_turned = sem("c_turned")
        silu_ready = sem("silu_ready")
        silu_split = sem("silu_split")
        exp_lam_ready = sem("exp_lam_ready")
        decay_ready = sem("decay_ready")
        mod_loaded = [sem(f"mod_loaded{s}") for s in range(8)]
        mod_hi_ready = sem("mod_hi_ready")
        mod_split = sem("mod_split")
        mod_used = sem("mod_used")
        mod_row_ready = sem("mod_row_ready")
        mod_row_stored = sem("mod_row_stored")
        mod_tiled = sem("mod_tiled")
        mod_turned = sem("mod_turned")
        modc_ready = sem("modc_ready")
        a12_ready = sem("a12_ready")
        ssq_ready = sem("ssq_ready")
        ms_ready = sem("ms_ready")
        root_ready = sem("root_ready")
        r_ready = sem("r_ready")
        xn1_ready = sem("xn1_ready")
        xt_turned = sem("xt_turned")
        ut_sample = sem("ut_sample")
        ut_prompt = sem("ut_prompt")

        wa_loaded = [sem(f"wa_loaded{k}") for k in range(3)]
        gw_loaded = sem("gw_loaded")
        xr_done = sem("xr_done")
        xv_done = sem("xv_done")
        xg_done = sem("xg_done")
        gate_done = sem("gate_done")
        xr_copied = sem("xr_copied")
        cur_ready = sem("cur_ready")
        taps_ready = sem("taps_ready")
        tap0_ready = sem("tap0_ready")
        xc_ready = sem("xc_ready")
        xg_sig = sem("xg_sig")
        glu_ready = sem("glu_ready")
        gate_sig = sem("gate_sig")
        decay_sq = sem("decay_sq")
        in_sq = sem("in_sq")
        in_root = sem("in_root")
        ix_ready = sem("ix_ready")
        conv_done = sem("conv_done")
        cv_copied = sem("cv_copied")
        lru_done = sem("lru_done")
        last_turned = sem("last_turned")
        last_ready = sem("last_ready")
        state_stored = sem("state_stored")

        ln_summed = sem("ln_summed")
        ln_centred = sem("ln_centred")
        ln_squared = sem("ln_squared")
        ln_sq_used = sem("ln_sq_used")
        ln_var = sem("ln_var")
        ln_root = sem("ln_root")
        ln_scaled = sem("ln_scaled")

        a_hi_ready = sem("a_hi_ready")
        a_split = sem("a_split")
        x_reloaded = sem("x_reloaded")
        piece_loaded = [sem(f"piece_loaded{n}") for n in range(4)]
        piece_hi = sem("piece_hi")
        piece_split = sem("piece_split")
        piece_used = sem("piece_used")
        tile_done = sem("tile_done")
        gate_ready = sem("gate_ready")
        m_ready = sem("m_ready")
        y_hi_ready = sem("y_hi_ready")
        y_split = sem("y_split")
        u_hi_ready = sem("u_hi_ready")
        u_split = sem("u_split")
        yb_hi_ready = sem("yb_hi_ready")
        yb_split = sem("yb_split")
        mt_turned = sem("mt_turned")
        mt_hi_ready = sem("mt_hi_ready")
        mt_split = sem("mt_split")
        slot_rows_loaded = sem("slot_rows_loaded")
        rows_loaded = sem("rows_loaded")
        rows_ready = sem("rows_ready")
        x2_ready = sem("x2_ready")
        ssq2_ready = sem("ssq2_ready")
        ms2_ready = sem("ms2_ready")
        root2_ready = sem("root2_ready")
        r2_ready = sem("r2_ready")
        xn2_ready = sem("xn2_ready")
        rows_stored = sem("rows_stored")
        vt_turned = sem("vt_turned")
        vt_dve = sem("vt_dve")
        vt_act = sem("vt_act")
        logit_done = sem("logit_done")
        lg_ready = sem("lg_ready")
        lg_turned = sem("lg_turned")
        max_ready = sem("max_ready")
        exp_ready = sem("exp_ready")
        soft_ready = sem("soft_ready")
        soft_turned = sem("soft_turned")
        top_ready = sem("top_ready")
        top_turned = sem("top_turned")
        idx_ready = sem("idx_ready")

        w_loaded = [sem(f"w_loaded{s}") for s in range(NSLOT)]
        unit_hi = sem("unit_hi")
        unit_split = sem("unit_split")
        unit_used = sem("unit_used")
        xe_modulated = sem("xe_modulated")
        xe_hi_ready = sem("xe_hi_ready")
        h_hi_ready = sem("h_hi_ready")
        xe_loaded = sem("xe_loaded")
        xe_turned = sem("xe_turned")
        xeT_ready = sem("xeT_ready")
        h1_silu = sem("h1_silu")
        h_ready = sem("h_ready")
        h_turned = sem("h_turned")
        hT_ready = sem("hT_ready")
        ye_ready = sem("ye_ready")
        scattered = sem("scattered")
        gf_loaded = sem("gf_loaded")
        fin_loaded = [sem(f"fin_loaded{t}") for t in range(NT)]
        fin_ssq = sem("fin_ssq")
        fin_ms = sem("fin_ms")
        fin_root = sem("fin_root")
        out_ready = sem("out_ready")
        out_stored = sem("out_stored")
        dve_step = sem("dve_step")
        act_step = sem("act_step")
        pool_step = sem("pool_step")

        block = ctx.enter_context(nc.Block())

        def wa(kind):
            return ring[:, WA_OFF + 2048 * kind:WA_OFF + 2048 * (kind + 1)].rearrange("p (k c) -> p k c", k=KD)

        GROUPS = [(w_in, 3 * D), (w_in, 3 * D + 512), (w_ro, 0), (w_ro, 512),
                  (w_in, 4 * D), (w_co, 0), (w_in, 4 * D + 512), (w_co, 512), (w_out, 0), (w_out, 512)]
        GATES, MERGES = (0, 1, 4, 6), (2, 3, 5, 7)
        BANKS = [0, 1, 2, 3, 4, 7]

        def piece_done(eng, q):
            if q % 4 == 3:
                eng.wait_ge(tile_done, NT * (q // 4 + 1))
            else:
                eng.wait_ge(piece_used, 3 * (q // 4) + q % 4 + 1)

        def tile_bank(n):
            return BANKS[n % 6]

        def chunk_source(e, m):
            if m < 8:
                w = (w_e1, w_e3)[m // 2 % 2]
                return w[e, :, 4 * (m % 2):4 * (m % 2) + 4, (m // 4) * D:(m // 4 + 1) * D]
            return w_e2[e, :, 4 * (m - 8):4 * (m - 8) + 4, :]

        def chunk(m):
            return slot(MOE_SLOTS[m % NSLOT]).rearrange("p (k c) -> p k c", k=4)

        def w_lo(m):
            return ring_lo[:, MOE_SLOTS[m % NSLOT], :, :]

        def units(i, m, half=1):
            return i * 24 + (2 * m + half + 1)

        def product_done(eng, i, m):
            eng.wait_ge(unit_used, units(i, m))

        @block.sync
        def _(eng):
            def load_mod(n):
                i, s = n // 4, n % 4
                for half in range(2):
                    if n >= 4:
                        eng.wait_ge(mod_used, 2 * (n - 4) + half + 1)
                    eng.dma_start(slot(s)[:, 2 * D * half:2 * D * half + 2 * D],
                                  w_mod[:, 2 * s + half, i * (2 * D):(i + 1) * (2 * D)]).then_inc(mod_loaded[2 * s + half], 16)

            def load_a(i, kind):
                eng.dma_start(wa(kind), w_in[:, :, bass.ds(i * 256 + kind * D, 256)]).then_inc(wa_loaded[kind], 16)

            def load_gates(i):
                for t in range(2):
                    for half in range(2):
                        eng.dma_start(gw[64 * half:64 * half + 64, t, :, 64 * half:64 * half + 64],
                                      gate_w[:, :, bass.ds(i * 4 + (2 * t + half), 1), :].rearrange("i g h j -> i g (h j)"))\
                            .then_inc(gw_loaded, 16)

            for n in range(4):
                load_mod(n)
            for t in range(NT):
                eng.dma_start(xr[:, t, :], x_prompt if t == 0 else x_sample[t - 1]).then_inc(x_loaded, 16)
            eng.dma_start(wr[:, :, :], w_router).then_inc(wr_loaded, 16)
            for n in range(4, 12):
                load_mod(n)
            eng.wait_ge(mod_used, 2 * 9 + 2)
            for kind in range(3):
                load_a(0, kind)
            eng.wait_ge(consts_ready, 4)
            load_gates(0)
            with eng.Fori(0, 3) as i:
                for kind, done in enumerate((xr_done, xv_done, xg_done)):
                    eng.wait_ge(done, i * 2 + 2)
                    load_a(i + 1, kind)
                eng.wait_ge(gate_done, i * 8 + 8)
                load_gates(i + 1)
            def load_piece(q):
                w, c = GROUPS[q // 4]
                eng.dma_start(b_raw[:, q % 4, :, :], w[:, 2 * (q % 4):2 * (q % 4) + 2, c:c + 512]).then_inc(piece_loaded[q % 4], 16)

            for q in range(36):
                if q < 4:
                    eng.wait_ge(xg_done if q >= 2 else xv_done, 8)
                else:
                    piece_done(eng, q - 4)
                load_piece(q)
                if q == 20:
                    eng.wait_ge(mod_row_stored, 16 * 3)
                    for s in range(2):
                        eng.dma_start(g1b_lo[:, s, :], mod_rows[2 + s:3 + s, 2 * D:3 * D].broadcast_to([P, D]))\
                            .then_inc(slot_rows_loaded, 16)
                    for g, first in ((g2b, 0), (g2b_lo, 2)):
                        for s, lo, hi in ((1, 0, CAP_S), (0, CAP_S, CAP)):
                            eng.dma_start(g[lo:hi, :], mod_rows[first + s:first + s + 1, 5 * D:6 * D].broadcast_to([hi - lo, D]))\
                                .then_inc(slot_rows_loaded, 16)
                    eng.dma_start(bias2, a["b_mod"][0:1, 5 * D:6 * D].broadcast_to([CAP, D])).then_inc(slot_rows_loaded, 16)
                for t in {32: (0,), 33: (1,), 34: (2,), 35: (3, 4)}.get(q, ()):
                    eng.dma_start(xr[:, t, :], x_prompt if t == 0 else x_sample[t - 1]).then_inc(x_reloaded, 16)
                if q == 12:
                    eng.wait_ge(last_ready, 1)
                    eng.dma_start(a["new_state"][0, 0].rearrange("s (k p) -> (s k) p", p=P), last_t[:, :]).then_inc(state_stored, 16)
            piece_done(eng, 32)
            load_piece(36)
            for part in range(2):
                eng.dma_start(g1b[:, part, :], mod_rows[part:part + 1, 2 * D:3 * D].broadcast_to([P, D])).then_inc(rows_loaded, 16)
            eng.dma_start(bias1, a["b_mod"][0:1, 2 * D:3 * D].broadcast_to([P, D])).then_inc(rows_loaded, 16)

            def load_chunk(e, m):
                eng.dma_start(chunk(m), chunk_source(e, m)).then_inc(w_loaded[MOE_SLOTS[m % NSLOT]], 16)

            for q in range(37, 40):
                piece_done(eng, q - 4)
                load_piece(q)
            eng.wait_ge(tile_done, NT * 10)
            load_chunk(0, 0)
            load_chunk(0, 1)
            eng.wait_ge(logit_done, NT)
            load_chunk(0, 2)
            load_chunk(0, 3)
            eng.wait_ge(vt_turned, NT)
            eng.wait_ge(rows_stored, 16 * 2 * NT)
            load_chunk(0, 4)
            load_chunk(0, 5)
            eng.dma_start(gf, a["final_norm_g"].rearrange("(o d) -> o d", o=1).broadcast_to([P, D])).then_inc(gf_loaded, 16)
            with eng.Fori(0, E - 1) as i:
                for n in range(12):
                    m = (n + NSLOT) % 12
                    e = i + (n + NSLOT) // 12
                    if m < 8:
                        w = (w_e1, w_e3)[m // 2 % 2][bass.ds(e, 1), :, :, :].rearrange("e p k f -> p (e k) f")
                        src = w[:, 4 * (m % 2):4 * (m % 2) + 4, (m // 4) * D:(m // 4 + 1) * D]
                    else:
                        src = w_e2_rows[:, bass.ds(e * 4 + (m - 8), 1), :, :].rearrange("p q k f -> p (q k) f")
                    product_done(eng, i, n)
                    eng.dma_start(chunk(m), src).then_inc(w_loaded[MOE_SLOTS[m % NSLOT]], 16)
            for m in range(NSLOT, 12):
                product_done(eng, E - 1, m - NSLOT)
                load_chunk(E - 1, m)
            eng.wait_ge(scattered, 16 * E)
            for t in range(NT):
                eng.dma_start(xr[:, t, :], acc_dram[P * t:P * t + P, :]).then_inc(fin_loaded[t], 16)
            for t in range(NT):
                eng.wait_ge(out_ready, t + 1)
                eng.dma_start(a["y_prompt"][0] if t == 0 else a["y_sample"][0].rearrange("(t p) d -> t p d", p=P)[t - 1],
                              xr[:, t, :]).then_inc(out_stored, 16)
            eng.wait_ge(out_stored, 16 * NT)
            eng.wait_ge(state_stored, 16)

        @block.gpsimd
        def _(eng):
            step = Steps(eng, pool_step)
            step.did(eng.memset(silu_c[:, :, :], 0.0))
            step.did(eng.memset(ident[:, :], 0.0))
            step.wait()
            eng.affine_select(out=ident[:, :], in_=ident[:, :], compare_op=ALU.not_equal, fill=1.0,
                              base=0, pattern=[[-1, P]], channel_multiplier=1).then_inc(consts_ready, 1)
            eng.memset(ones[:, :], 1.0).then_inc(consts_ready, 1)
            eng.memset(xpad[:, :, :], 0.0).then_inc(consts_ready, 1)
            eng.memset(gw[:, :, :, :], 0.0).then_inc(consts_ready, 1)

            def vec_in(rows, tile, src):
                n = src.shape[0]
                eng.dma_start(vecs[rows:rows + n, tile, :], src).then_inc(vec_loaded, 16)

            def rows_of(v):
                return v.rearrange("(r p) -> r p", p=P)

            vec_in(C_BMOD, 0, rows_of(a["b_mod"][0]))
            vec_in(C_N1, 0, rows_of(a["norm1_g"][0]))
            vec_in(C_N2, 0, rows_of(a["norm2_g"][0]))
            vec_in(C_LNG, 0, rows_of(a["conv_ln_g"][0]))
            vec_in(C_LNB, 0, rows_of(a["conv_ln_b"][0]))
            vec_in(C_TAB, 0, a["state_rglru"][0, 0].rearrange("s (r p) -> (s r) p", p=P))
            vec_in(C_TAB + 8 * G_RCB, 0, rows_of(a["rnn_conv_b"][0]))
            vec_in(C_TAB + 8 * G_CDB, 0, rows_of(a["conv_dw_b"][0]))
            vec_in(0, 1, a["rnn_conv_w"][0].rearrange("s (r p) -> (s r) p", p=P))
            vec_in(32, 1, a["rnn_gate_b"][0].rearrange("s g (r p) -> (s g r) p", p=P))
            vec_in(64, 1, a["rnn_lambda"][0].rearrange("s (r p) -> (s r) p", p=P))
            taps = a["conv_dw_w"][0].rearrange("s (r p) -> (s r) p", p=P)
            vec_in(0, 2, taps[0:P])
            vec_in(0, 3, taps[P:8 * TAPS31])

            for i in range(3):
                eng.wait_ge(mod_row_ready, i + 1)
                eng.dma_start(mod_rows[:, i * (2 * D):(i + 1) * (2 * D)], mod_row).then_inc(mod_row_stored, 16)

            with eng.Fori(0, 4) as i:
                for n in range(4):
                    t, d = n // 2, n % 2
                    eng.wait_ge(gate_sig, i * 8 + (2 * n + 2))
                    eng.wait_ge(xc_ready, i * 2 + (t + 1))
                    eng.tensor_tensor(lr_i[:, t, d, :], lr_i[:, t, d, :], xc[:, t, :], ALU.mult).then_inc(ix_ready, 1)
                for t in range(2):
                    eng.wait_ge(conv_done, i * 2 + (t + 1))
                    eng.tensor_copy(cu[:, bass.ds(i * 2 + t, 1), :], cv[:, t:t + 1, :]).then_inc(cv_copied, 1)

            def gather(col):
                step.did(eng.tensor_copy(idx_g[:, :], idx_t[:, bass.ds(col, 1)]))
                step.wait()
                eng.indirect_dma_start(out=xe, out_offset=None, in_=xn_dram,
                                       in_offset=bass.IndirectOffsetOnAxis(ap=idx_g[:, 0:1], axis=0))\
                    .then_inc(xe_loaded, 16)

            eng.wait_ge(idx_ready, 3)
            eng.wait_ge(rows_stored, 16 * 2 * NT)
            gather(0)
            step.restart()
            with eng.Fori(0, E) as i:
                eng.wait_ge(xe_turned, i + 1)
                eng.wait_ge(xe_loaded, i * 16 + 16)
                gather(i + 1)
                step.did(eng.tensor_copy(idx_s[:, :], idx_t[:, bass.ds(i, 1)]))
                step.wait()
                eng.wait_ge(ye_ready, i + 1)
                eng.indirect_dma_start(out=acc_dram, out_offset=bass.IndirectOffsetOnAxis(ap=idx_s[:, 0:1], axis=0),
                                       in_=ye, in_offset=None, compute_op=ALU.add).then_inc(scattered, 16)
                step.restart()
                eng.wait_ge(scattered, i * 16 + 16)

        @block.scalar
        def _(eng):
            for at, c in ((0, a["c_ctx"]), (KD, a["c"][0])):
                eng.dma_start(c_rows[at:at + KD, :], c.rearrange("(r p) -> r p", p=P)).then_inc(c_loaded, 16)
            step = Steps(eng, act_step)

            eng.wait_ge(c_turned, 1)
            step.did(eng.activation(silu_c[:, :, 0:2].rearrange("p k s -> p s k"),
                                    ps[:, 7, 0:2 * KD].rearrange("p (s k) -> p s k", s=2), ACT.Silu))
            step.wait()
            eng.activation(silu_parts[:, :, 0:2].rearrange("p k s -> p s k"), silu_c[:, :, 0:2].rearrange("p k s -> p s k"), ACT.Copy).then_inc(silu_ready, 1)

            def mod_high(n):
                for half in range(2):
                    eng.wait_ge(mod_loaded[2 * (n % 4) + half], 16 * (n // 4 + 1))
                    if n >= 4:
                        eng.wait_ge(mod_used, 2 * (n - 4) + half + 1)
                    eng.activation(mod_hi[:, n // 2 % 2, half, :], slot(n % 4)[:, 2 * D * half:2 * D * half + 2 * D], ACT.Copy)\
                        .then_inc(mod_hi_ready, 1)

            def mod_sums(i):
                eng.wait_ge(mod_used, 8 * i + 8)
                if i:
                    eng.wait_ge(mod_row_stored, 16 * i)
                    eng.wait_ge(mod_turned, i)
                b = 4 * (i % 2)
                eng.activation(mod_row.rearrange("s (b c) -> s b c", b=4), ps[0:4, b:b + 4, :], ACT.Copy).then_inc(mod_row_ready, 1)
                eng.wait_ge(mod_row_ready, i + 1)
                eng.dma_start(mod_tiles[:, :], mod_row.rearrange("s (j p) -> s j p", p=P)).then_inc(mod_tiled, 16)

            mod_high(0)
            mod_high(2)
            eng.wait_ge(x_loaded, 16 * NT)
            for t in range(NT):
                if t:
                    eng.wait_ge(ssq_ready, t)
                eng.activation(xn1[:, t, :], xr[:, t, :], ACT.Square, accum_out=rstat[:, 0, t:t + 1]).then_inc(ssq_ready, 1)
            eng.wait_ge(ms_ready, 1)
            eng.activation(rstat[:, 2, :], rstat[:, 1, :], ACT.Sqrt).then_inc(root_ready, 1)
            mod_high(4)
            mod_sums(0)
            eng.wait_ge(r_ready, 1)
            for t in range(NT):
                eng.activation(xn1[:, t, :], xr[:, t, :], ACT.Copy, scale=rstat[:, 3, t:t + 1]).then_inc(xn1_ready, 1)
            mod_high(6)

            def ut_part(k):
                eng.wait_ge(xt_turned, k + 1)
                eng.activation(uT[:, k, 0:NP], ps[:, 2 * (k % 2) + 1, 0:NP], ACT.Identity,
                               scale=a1[:, k, 0:1], bias=modc[:, k, 0:1]).then_inc(ut_prompt, 1)

            eng.wait_ge(a12_ready, 1)
            for n in (7, 8):
                for k in range(KD // 2):
                    ut_part(KD // 2 * (n - 7) + k)
                if n == 8:
                    mod_high(n)
            mod_high(10)
            mod_sums(1)
            eng.wait_ge(ut_sample, KD)
            eng.wait_ge(ut_prompt, KD)
            for h in range(2):
                eng.activation(u_hi[:, 4 * h:4 * h + 4, :], uT[:, 4 * h:4 * h + 4, :], ACT.Copy).then_inc(u_hi_ready, 1)
            eng.wait_ge(cols_ready, 1)
            lam = cols[:, C_TAB + 8 * G_LAM:C_TAB + 8 * G_LAM + 16]
            step.did(eng.activation(sp[:, 0, :], lam, ACT.Abs))
            step.wait()
            eng.activation(sp[:, 1, :], sp[:, 0, :], ACT.Exp, scale=-1.0).then_inc(exp_lam_ready, 1)
            mod_sums(2)

            step.restart()
            eng.wait_ge(consts_ready, 4)
            def a_high(i, kind, first=False):
                eng.wait_ge(wa_loaded[kind], i * 16 + 16)
                if kind == 2:
                    eng.wait_ge(xr_done, i * 2 + 2)
                elif not first:
                    eng.wait_ge((xg_done, xv_done)[kind], i * 2)
                eng.activation(a_hi[kind % 2][:, :, :], wa(kind), ACT.Copy).then_inc(a_hi_ready, 1)

            def copy_xr(i):
                for t in range(2):
                    eng.wait_ge(xr_done, i * 2 + (t + 1))
                    b = 2 * t
                    eng.activation(xpad[:, t, 2:2 + NP], ps[:, b, 0:NP], ACT.Copy)
                    eng.activation(xpad[:, t, S0 + 2:S0 + 2 + HALF - NP], ps[:, b, NP:HALF], ACT.Copy)
                    eng.activation(xpad[:, t, S0 + 2 + HALF - NP:S0 + 2 + NS], ps[:, b + 1, 0:HALF], ACT.Copy)\
                        .then_inc(xr_copied, 1)

            def piece_high(q):
                eng.wait_ge(piece_loaded[q % 4], 16 * (q // 4 + 1))
                if q < 4:
                    eng.wait_ge(xr_done if q < 2 else xg_done, 8)
                else:
                    piece_done(eng, q - 4)
                eng.activation(b_hi[q % 4][:, :, :], b_raw[:, q % 4, :, :], ACT.Copy).then_inc(piece_hi, 1)

            def gates_of(g):
                n = GATES.index(g)
                for t in range(NT):
                    eng.wait_ge(tile_done, NT * g + t + 1)
                    if n >= 2:
                        eng.wait_ge(m_ready, NT * (0, 2)[n - 2] + t + 1)
                    eng.activation((gate_rows2 if g == 1 else gate_rows)[t], ps[:, tile_bank(NT * g + t), :], ACT.Sigmoid)\
                        .then_inc(gate_ready, 1)

            def first_tap(i):
                eng.wait_ge(taps_ready, i + 1)
                eng.wait_ge(xr_copied, i * 2 + 2)
                for t in range(2):
                    eng.activation(xc[:, t, :], xpad[:, t, 0:LX], ACT.Identity, scale=cur_taps[:, G_RCW - G_RCB, t:t + 1],
                                   bias=cur_taps[:, 0, t:t + 1]).then_inc(tap0_ready, 1)

            def act_channels(i, final):
                eng.wait_ge(cur_ready, i + 1)
                for t in range(2):
                    eng.wait_ge(xg_done, i * 2 + (t + 1))
                    eng.activation(sg[:, t, :].rearrange("p (h c) -> p h c", h=2), ps[:, 2 * t:2 * t + 2, 0:HALF], ACT.Sigmoid)\
                        .then_inc(xg_sig, 1)
                if final:
                    piece_high(0)
                    piece_high(1)
                else:
                    a_high(i + 1, 0)
                    a_high(i + 1, 1)
                for n in range(8):
                    t, d, g = n // 4, n // 2 % 2, n % 2
                    b = GATE_BANKS[n % 4]
                    dst = (lr_r, lr_i)[g][:, t, d, :].rearrange("p (h c) -> p h c", h=2)
                    eng.wait_ge(gate_done, i * 8 + (n + 1))
                    eng.activation(dst, ps[:, b:b + 2, 0:LX // 2], ACT.Sigmoid,
                                   bias=cur[:, G_GB + 2 * d + g, t:t + 1]).then_inc(gate_sig, 1)
                eng.wait_ge(gate_sig, i * 8 + 8)
                for n in range(4):
                    t, d = n // 2, n % 2
                    step.did(eng.activation(lr_a[:, t, d, :], lr_r[:, t, d, :], ACT.Exp, scale=cur[:, G_NLAM + d, t:t + 1]))
                    step.did(eng.activation(lr_r[:, t, d, :], lr_r[:, t, d, :], ACT.Tanh, scale=cur[:, G_LAM + d, t:t + 1]))
                    step.wait(1)
                    eng.activation(lr_q[:, t, d, :], lr_a[:, t, d, :], ACT.Square).then_inc(decay_sq, 1)
                if final:
                    for q in range(2, 6):
                        piece_high(q)
                    gates_of(0)
                else:
                    a_high(i + 1, 2)
                    eng.wait_ge(xc_ready, i * 2 + 2)
                    copy_xr(i + 1)
                for n in range(4):
                    t, d = n // 2, n % 2
                    eng.wait_ge(in_sq, i * 4 + (n + 1))
                    eng.activation(lr_q[:, t, d, :], lr_q[:, t, d, :], ACT.Sqrt).then_inc(in_root, 1)
                if not final:
                    eng.wait_ge(ix_ready, i * 4 + 4)
                    first_tap(i + 1)
                step.restart()

            for kind in range(3):
                a_high(0, kind, first=True)
            copy_xr(0)
            first_tap(0)
            with eng.Fori(0, 3) as i:
                act_channels(i, False)
            act_channels(3, True)

            def squares(k0, k1):
                for k in range(k0, k1):
                    eng.wait_ge(ln_centred, k + 1)
                    if k >= 2:
                        eng.wait_ge(ln_sq_used, k - 1)
                    eng.activation(ln_sq[:, k % 2, :], cu[:, k, :], ACT.Square).then_inc(ln_squared, 1)

            def yb_high(k0, k1):
                for k in range(k0, k1):
                    eng.wait_ge(ln_scaled, k + 1)
                    for out in (y_hi, cu):
                        ins = eng.activation(out[:, k, :], cu[:, k, :], ACT.Silu, scale=cols[:, C_LNG + k:C_LNG + k + 1],
                                             bias=cols[:, C_LNB + k:C_LNB + k + 1])
                    ins.then_inc(yb_hi_ready, 1)

            piece_high(6)
            piece_high(7)
            eng.wait_ge(lru_done, 4)
            for h in range(2):
                eng.activation(y_hi[:, 4 * h:4 * h + 4, :], ya[:, 4 * h:4 * h + 4, :], ACT.Copy).then_inc(y_hi_ready, 1)
            piece_high(8)
            piece_high(9)
            gates_of(1)
            piece_high(10)
            squares(0, 2)
            piece_high(11)
            squares(2, 4)
            piece_high(12)
            squares(4, 6)
            piece_high(13)
            squares(6, 8)
            eng.wait_ge(ln_var, 1)
            eng.activation(ln_rs, ln_rs, ACT.Sqrt).then_inc(ln_root, 1)
            piece_high(14)
            piece_high(15)
            for g in range(3, 7):
                if g == 4:
                    eng.wait_ge(tile_done, NT * 4)
                    yb_high(0, 4)
                piece_high(4 * g + 4)
                if g == 4:
                    yb_high(4, 8)
                piece_high(4 * g + 5)
                if g in GATES:
                    gates_of(g)
                piece_high(4 * g + 6)
                piece_high(4 * g + 7)

            def merged_high(k):
                eng.wait_ge(mt_turned, k + 1)
                eng.activation(m_hi[:, k, :], turned_merged, ACT.Copy).then_inc(mt_hi_ready, 1)

            for k in range(4):
                merged_high(k)
                piece_high(32 + k)
            merged_high(4)
            piece_high(36)
            merged_high(5)
            merged_high(6)
            piece_high(37)
            merged_high(7)
            piece_high(38)
            piece_high(39)

            def norm_rows(t):
                eng.wait_ge(x2_ready, NT + t + 1)
                if t:
                    eng.wait_ge(xn2_ready, t)
                eng.activation(xn2[:, t, :], xr[:, t, :], ACT.Square, accum_out=rstat[:, 0, t:t + 1]).then_inc(ssq2_ready, 1)
                eng.wait_ge(ms2_ready, t + 1)
                eng.activation(rstat[:, 2, t:t + 1], rstat[:, 1, t:t + 1], ACT.Sqrt).then_inc(root2_ready, 1)
                eng.wait_ge(r2_ready, t + 1)
                eng.activation(xn2[:, t, :], xr[:, t, :], ACT.Copy, scale=rstat[:, 3, t:t + 1]).then_inc(xn2_ready, 1)
                eng.wait_ge(xn2_ready, t + 1)
                eng.dma_start(xn_dram[P * t:P * t + P, :], xn2[:, t, :]).then_inc(rows_stored, 16)
                eng.dma_start(acc_dram[P * t:P * t + P, :], xr[:, t, :]).then_inc(rows_stored, 16)

            def modulate_half(t):
                eng.wait_ge(vt_turned, t + 1)
                for k in range(4, KD):
                    ins = eng.activation(vT[:, k, P * t:P * t + P], ps[:, 2 * (t % 2) + 1, P * (k - 4):P * (k - 3)], ACT.Identity,
                                         scale=a2[:, k, min(t, 1):min(t, 1) + 1], bias=modc[:, 24 + k, min(t, 1):min(t, 1) + 1])
                ins.then_inc(vt_act, 1)

            for t in range(NT - 1):
                norm_rows(t)
                if t:
                    modulate_half(t - 1)
            modulate_half(NT - 2)
            norm_rows(NT - 1)
            modulate_half(NT - 1)
            for t in range(NT):
                eng.wait_ge(max_ready, 1)
                eng.activation(soft[:, t, :], ps[:, 5, 16 * t:16 * t + 16], ACT.Exp, bias=sstat[:, 0, t:t + 1],
                               accum_out=sstat[:, 1, t:t + 1]).then_inc(exp_ready, 1)

            def hi_piece(i, m, free):
                eng.wait_ge(w_loaded[MOE_SLOTS[m % NSLOT]], i * 32 + 16 * (m // NSLOT + 1))
                for half in range(2):
                    if free is not None:
                        eng.wait_ge(unit_used, units(*free, half))
                    eng.activation(w_hi[m % 2][:, 2 * half:2 * half + 2, :], chunk(m)[:, 2 * half:2 * half + 2, :],
                                   ACT.Copy).then_inc(unit_hi, 1)

            def hi_xe(n):
                eng.wait_ge(xe_modulated, n)
                eng.activation(xe_hi[:, :, :], xeT[:, :, :], ACT.Copy).then_inc(xe_hi_ready, 1)

            def swish(i, half):
                product_done(eng, i, 4 * half + 1)
                eng.activation(hs[:, half * D:(half + 1) * D].rearrange("c (b f) -> c b f", b=2), ps[0:CAP, 0:2, :],
                               ACT.Silu).then_inc(h1_silu, 1)

            def hi_h(i, half):
                eng.wait_ge(h_turned, i * 2 + (half + 1))
                eng.activation(h_hi[:, 8 * half:8 * half + 8, :].rearrange("p (b k) c -> p b (k c)", b=2),
                               ps[:, 6:8, 0:4 * CAP], ACT.Copy).then_inc(h_hi_ready, 1)

            def act_expert(i, final):
                for m in range(2, 12):
                    hi_piece(i, m, (i, m - 2))
                    if m == 3:
                        swish(i, 0)
                    if m == 7:
                        swish(i, 1)
                        hi_h(i, 0)
                    if m == 10:
                        hi_h(i, 1)
                hi_xe(i + 2)
                if not final:
                    for m in range(2):
                        hi_piece(i + 1, m, (i, m + 10))

            eng.wait_ge(logit_done, NT)
            eng.wait_ge(rows_stored, 16 * 2 * NT)
            for m in range(2):
                hi_piece(0, m, None)
            hi_xe(1)
            with eng.Fori(0, E - 1) as i:
                act_expert(i, False)
            act_expert(E - 1, True)

            eng.activation(rstat[:, 2, :], rstat[:, 1, :], ACT.Sqrt)
            for t in range(NT + 1):
                if t < NT:
                    eng.wait_ge(fin_loaded[t], 16)
                    if t >= 2:
                        eng.wait_ge(fin_ssq, t - 1)
                    eng.activation(xn1[:, t % 2, :], xr[:, t, :], ACT.Square, accum_out=rstat[:, 0, t:t + 1]).then_inc(fin_ssq, 1)
                if t:
                    eng.wait_ge(fin_ms, t)
                    eng.activation(rstat[:, 2, t - 1:t], rstat[:, 1, t - 1:t], ACT.Sqrt).then_inc(fin_root, 1)

        @block.vector
        def _(eng):
            step = Steps(eng, dve_step)

            def inverse_root(ssq_sem, n, ms_sem, root_sem, t0, t1):
                eng.wait_ge(ssq_sem, n)
                eng.tensor_scalar(rstat[:, 1, t0:t1], rstat[:, 0, t0:t1], 1.0 / D, EPS, ALU.mult, ALU.add).then_inc(ms_sem, 1)

            def mod_low(n):
                for half in range(2):
                    eng.wait_ge(mod_hi_ready, n + half + 1)
                    eng.tensor_tensor(mod_lo[:, n % 4, half, :], slot(n % 4)[:, 2 * D * half:2 * D * half + 2 * D],
                                      mod_hi[:, n // 2 % 2, half, :].bitcast(F32), ALU.subtract).then_inc(mod_split, 1)

            def mod_columns(i):
                eng.wait_ge(mod_turned, i + 1)
                src = ps[:, 4 * (i % 2), 0:64].rearrange("p (s j) -> p s j", s=4)
                for h in range(2):
                    step.did(eng.tensor_tensor(modc[:, 16 * i:16 * i + 16, h], src[:, 2 + h, :], cols[:, 16 * i:16 * i + 16], ALU.add))
                step.wait()
                for h in range(2):
                    ins = eng.tensor_tensor(modc[:, 16 * i:16 * i + 16, h], src[:, h, :], modc[:, 16 * i:16 * i + 16, h], ALU.add)
                ins.then_inc(modc_ready, 1)

            def modulated(dst, v, c):
                eng.wait_ge(modc_ready, 1 if v == 1 else 3)
                for s in range(2):
                    ins = eng.scalar_tensor_tensor(out=dst[:, :, s], in0=modc[:, v * KD:v * KD + KD, s], scalar=1.0,
                                                   in1=cols[:, c:c + KD], op0=ALU.add, op1=ALU.mult)
                ins.then_inc(a12_ready, 1)
                eng.wait_ge(a12_ready, 1 if v == 1 else 2)

            eng.wait_ge(silu_ready, 1)
            eng.tensor_tensor(silu_parts[:, :, 2:4].rearrange("p k s -> p s k"), silu_c[:, :, 0:2].rearrange("p k s -> p s k"),
                              silu_parts[:, :, 0:2].bitcast(F32).rearrange("p k s -> p s k"), ALU.subtract).then_inc(silu_split, 1)
            mod_low(0)
            mod_low(2)
            inverse_root(ssq_ready, NT, ms_ready, root_ready, 0, NT)
            eng.wait_ge(cols_turned, 1)
            eng.tensor_copy(cols[:, 0:C_TAB + 8 * G_NLAM], ps[:, 6, 0:C_TAB + 8 * G_NLAM]).then_inc(cols_ready, 1)
            eng.wait_ge(root_ready, 1)
            eng.reciprocal(rstat[:, 3, :], rstat[:, 2, :]).then_inc(r_ready, 1)
            mod_low(4)
            mod_low(6)
            mod_columns(0)
            modulated(a1, 1, C_N1)
            for n in (7, 8):
                for k in range(KD // 2 * (n - 7), KD // 2 * (n - 6)):
                    eng.wait_ge(xt_turned, k + 1)
                    eng.tensor_scalar(uT[:, k, NP:N], ps[:, 2 * (k % 2), :], a1[:, k, 1:2], modc[:, k, 1:2], ALU.mult, ALU.add)\
                        .then_inc(ut_sample, 1)
                if n == 8:
                    mod_low(n)
            mod_low(10)
            mod_columns(1)
            for h in range(2):
                eng.wait_ge(u_hi_ready, h + 1)
                eng.tensor_tensor(u_lo[:, 4 * h:4 * h + 4, :], uT[:, 4 * h:4 * h + 4, :], u_hi[:, 4 * h:4 * h + 4, :].bitcast(F32),
                                  ALU.subtract).then_inc(u_split, 1)
            lam = cols[:, C_TAB + 8 * G_LAM:C_TAB + 8 * G_LAM + 16]
            nlam = cols[:, C_TAB + 8 * G_NLAM:C_TAB + 8 * G_NLAM + 16]
            z, s, s2, poly = sp[:, 1, :], sp[:, 2, :], sp[:, 3, :], sp[:, 4, :]
            eng.wait_ge(exp_lam_ready, 1)
            step.did(eng.tensor_scalar(s2, z, 2.0, None, ALU.add))
            step.wait()
            step.did(eng.reciprocal(poly, s2))
            step.wait()
            step.did(eng.tensor_tensor(s, z, poly, ALU.mult))
            step.wait()
            step.did(eng.tensor_tensor(s2, s, s, ALU.mult))
            step.wait()
            step.did(eng.tensor_scalar(poly, s2, 1.0 / 17, 1.0 / 15, ALU.mult, ALU.add))
            for n in range(6, -1, -1):
                step.wait()
                step.did(eng.tensor_tensor(poly, poly, s2, ALU.mult))
                step.wait()
                step.did(eng.tensor_scalar(poly, poly, 1.0 / (2 * n + 1), None, ALU.add))
            step.wait()
            step.did(eng.tensor_tensor(poly, poly, s, ALU.mult))
            step.did(eng.tensor_scalar(s2, lam, -1.0, 0.0, ALU.mult, ALU.max))
            step.wait()
            step.did(eng.scalar_tensor_tensor(out=s, in0=poly, scalar=2.0, in1=s2, op0=ALU.mult, op1=ALU.add))
            step.wait()
            step.did(eng.tensor_scalar(lam, s, RG_C, None, ALU.mult))
            eng.tensor_scalar(nlam, s, -RG_C, None, ALU.mult).then_inc(decay_ready, 1)

            mod_columns(2)
            modulated(a2, 4, C_N2)
            eng.wait_ge(decay_ready, 1)
            eng.wait_ge(mod_row_stored, 48)

            table = cols[:, C_TAB:NCOLS].rearrange("p (g c) -> p g c", c=KD)
            ranges = conv_ranges()
            step.restart()

            def a_low(i, kind):
                eng.wait_ge(a_hi_ready, i * 3 + (kind + 1))
                eng.tensor_tensor(a_lo[:, kind, :, :], wa(kind), a_hi[kind % 2][:, :, :].bitcast(F32), ALU.subtract)\
                    .then_inc(a_split, 1)

            def piece_low(q):
                eng.wait_ge(piece_hi, q + 1)
                eng.tensor_tensor(b_lo[:, q % 4, :, :], b_raw[:, q % 4, :, :], b_hi[q % 4][:, :, :].bitcast(F32), ALU.subtract)\
                    .then_inc(piece_split, 1)

            def next_low(i, final, kind, pieces):
                if final:
                    for q in pieces:
                        piece_low(q)
                elif kind is not None:
                    a_low(i + 1, kind)

            def copy_taps(i):
                eng.tensor_copy(cur_taps[:, :, :], table[:, G_RCB:G_RCW + 1, bass.ds(i * 2, 2)]).then_inc(taps_ready, 1)

            def dve_channels(i, final):
                eng.tensor_copy(cur[:, :, :], table[:, :, bass.ds(i * 2, 2)]).then_inc(cur_ready, 1)
                eng.wait_ge(cur_ready, i + 1)
                for k in range(1, TAPS4):
                    for t in range(2):
                        if k == 1:
                            eng.wait_ge(tap0_ready, i * 2 + (t + 1))
                        else:
                            step.wait(0 if k == TAPS4 - 1 and t == 1 else 1)
                        ins = eng.scalar_tensor_tensor(out=xc[:, t, :], in0=xpad[:, t, k:k + LX], scalar=cur[:, G_RCW + k, t:t + 1],
                                                       in1=xc[:, t, :], op0=ALU.mult, op1=ALU.add)
                        if k < TAPS4 - 1:
                            step.did(ins)
                        else:
                            ins.then_inc(xc_ready, 1)
                for t in range(2):
                    b = 4 + 2 * t
                    eng.wait_ge(xv_done, i * 2 + (t + 1))
                    eng.wait_ge(xg_sig, i * 2 + (t + 1))
                    eng.tensor_tensor(glu[:, t, :].rearrange("p (h c) -> p h c", h=2), ps[:, b:b + 2, 0:HALF],
                                      sg[:, t, :].rearrange("p (h c) -> p h c", h=2), ALU.mult).then_inc(glu_ready, 1)
                eng.wait_ge(glu_ready, i * 2 + 2)
                next_low(i, final, 0, (0, 1))
                behind = {}
                for t in range(2):
                    step.did(eng.tensor_scalar(cv[:, t, :], glu[:, t, :], cur[:, G_CDW + MID, t:t + 1], cur[:, G_CDB, t:t + 1],
                                               ALU.mult, ALU.add))
                    behind[t, True] = behind[t, False] = step.n
                for n, (k, lo, hi, s) in enumerate(ranges):
                    if n == len(ranges) // 2:
                        next_low(i, final, 1, (2, 3))
                    for t in range(2):
                        eng.wait_ge(dve_step, behind[t, lo < NP])
                        ins = eng.scalar_tensor_tensor(out=cv[:, t, lo:hi], in0=glu[:, t, lo + s:hi + s],
                                                       scalar=cur[:, G_CDW + k, t:t + 1], in1=cv[:, t, lo:hi],
                                                       op0=ALU.mult, op1=ALU.add)
                        if n < len(ranges) - 1:
                            step.did(ins)
                            behind[t, lo < NP] = step.n
                        else:
                            ins.then_inc(conv_done, 1)
                next_low(i, final, 2, (4, 5))
                for n in range(4):
                    t, d = n // 2, n % 2
                    eng.wait_ge(decay_sq, i * 4 + (n + 1))
                    eng.scalar_tensor_tensor(out=lr_q[:, t, d, :], in0=lr_q[:, t, d, :], scalar=1.0, in1=lr_r[:, t, d, :],
                                             op0=ALU.add, op1=ALU.mult).then_inc(in_sq, 1)
                for n in range(4):
                    t, d = n // 2, n % 2
                    eng.wait_ge(in_root, i * 4 + (n + 1))
                    eng.wait_ge(ix_ready, i * 4 + (n + 1))
                    step.did(eng.tensor_tensor(lr_q[:, t, d, :], lr_q[:, t, d, :], lr_i[:, t, d, :], ALU.mult))
                if not final:
                    copy_taps(i + 1)
                step.wait()
                for n in range(4):
                    t, d = n // 2, n % 2
                    for lo, hi, h0 in ((0, NP, 0.0), (S0, S0 + NS, cur[:, G_STATE + d, t:t + 1])):
                        h, av, bv = lr_r[:, t, d, lo:hi], lr_a[:, t, d, lo:hi], lr_q[:, t, d, lo:hi]
                        if d:
                            h, av, bv = h[:, ::-1], av[:, ::-1], bv[:, ::-1]
                        step.did(eng.tensor_tensor_scan(out=h, data0=av, data1=bv, initial=h0, op0=ALU.mult, op1=ALU.add))
                    if n == 1:
                        next_low(i, final, None, (6,))
                step.wait()
                for t in range(2):
                    for lo, to, n in ((0, 0, NP), (S0, NP, NS)):
                        step.did(eng.tensor_tensor(ya[:, bass.ds(i * 2 + t, 1), to:to + n].rearrange("p a c -> p (a c)"),
                                                   lr_r[:, t, 0, lo:lo + n], lr_r[:, t, 1, lo:lo + n], ALU.add))
                step.did(eng.tensor_copy(last[:, 0, bass.ds(i * 2, 2)], lr_r[:, :, 0, NP - 1]))
                eng.wait_ge(cv_copied, i * 2 + 2)
                eng.tensor_copy(last[:, 1, bass.ds(i * 2, 2)], lr_r[:, :, 1, 0]).then_inc(lru_done, 1)
                step.restart()
            copy_taps(0)
            for kind in range(3):
                a_low(0, kind)
            with eng.Fori(0, 3) as i:
                dve_channels(i, False)
            dve_channels(3, True)

            def centre(k0, k1):
                for k in range(k0, k1):
                    eng.tensor_tensor(cu[:, k, :], cu[:, k, :], ln_mu, ALU.add).then_inc(ln_centred, 1)

            def yb_low(k0, k1):
                for k in range(k0, k1):
                    eng.wait_ge(yb_hi_ready, k + 1)
                    eng.tensor_tensor(yb_lo[:, k, :], cu[:, k, :], y_hi[:, k, :].bitcast(F32), ALU.subtract).then_inc(yb_split, 1)

            def merge_tiles(g):
                order = MERGES.index(g)
                rows = gate_rows2 if g == 3 else gate_rows
                for t in range(NT):
                    n = NT * g + t
                    eng.wait_ge(tile_done, n + 1)
                    eng.wait_ge(gate_ready, NT * order + t + 1)
                    m = merged[:, t, 512 * (order % 2):512 * (order % 2) + 512]
                    if g < 4:
                        eng.tensor_tensor(m, rows[t], ps[:, tile_bank(n), :], ALU.mult).then_inc(m_ready, 1)
                    else:
                        step.did(eng.tensor_tensor(rows[t], rows[t], ps[:, tile_bank(n), :], ALU.mult))
                        step.wait()
                        eng.tensor_tensor(m, m, rows[t], ALU.add).then_inc(m_ready, 1)

            piece_low(7)
            for h in range(2):
                eng.wait_ge(y_hi_ready, h + 1)
                eng.tensor_tensor(ya_lo[:, 4 * h:4 * h + 4, :], ya[:, 4 * h:4 * h + 4, :], y_hi[:, 4 * h:4 * h + 4, :].bitcast(F32),
                                  ALU.subtract).then_inc(y_split, 1)
            piece_low(8)
            piece_low(9)
            eng.wait_ge(last_turned, 1)
            eng.tensor_copy(last_t[:, :], ps[0:16, 7, 0:P]).then_inc(last_ready, 1)
            eng.wait_ge(ln_summed, 1)
            step.did(eng.tensor_scalar(ln_mu.rearrange("p (h c) -> p h c", h=2), ps[:, 5:7, 0:HALF], -1.0 / D, None, ALU.mult))
            step.wait()
            centre(0, 4)
            piece_low(10)
            centre(4, 8)
            for q in range(11, 14):
                piece_low(q)
            eng.wait_ge(ln_sq_used, KD)
            eng.tensor_scalar(ln_rs.rearrange("p (h c) -> p h c", h=2), ps[:, 5:7, 0:HALF], 1.0 / D, EPS, ALU.mult, ALU.add)\
                .then_inc(ln_var, 1)
            merge_tiles(2)
            piece_low(14)
            piece_low(15)
            eng.wait_ge(ln_root, 1)
            step.did(eng.reciprocal(ln_rs, ln_rs))
            eng.wait_ge(ln_centred, KD)
            for g in range(3, 7):
                if g == 4:
                    yb_low(0, 4)
                piece_low(4 * g + 4)
                if g == 3:
                    step.wait()
                    for k in range(KD):
                        eng.tensor_tensor(cu[:, k, :], cu[:, k, :], ln_rs, ALU.mult).then_inc(ln_scaled, 1)
                if g == 4:
                    yb_low(4, 8)
                piece_low(4 * g + 5)
                if g in MERGES:
                    merge_tiles(g)
                piece_low(4 * g + 6)
                piece_low(4 * g + 7)

            def merged_low(k):
                eng.wait_ge(mt_hi_ready, k + 1)
                eng.tensor_tensor(m_lo[:, k, :], turned_merged, m_hi[:, k, :].bitcast(F32), ALU.subtract).then_inc(mt_split, 1)

            for k in range(4):
                merged_low(k)
                if k == 2:
                    merge_tiles(7)
                piece_low(32 + k)
                if k == 0:
                    eng.wait_ge(slot_rows_loaded, 16 * 7)
                    step.did(eng.tensor_tensor(g2b, g2b, g2b_lo, ALU.add))
                    step.wait()
                    eng.tensor_tensor(g2b, g2b, bias2, ALU.add).then_inc(rows_ready, 1)
            merged_low(4)
            piece_low(36)
            merged_low(5)
            merged_low(6)
            piece_low(37)
            merged_low(7)
            eng.wait_ge(rows_loaded, 16 * 3)
            step.did(eng.tensor_tensor(g1b, g1b, g1b_lo, ALU.add))
            step.wait()
            for s in range(2):
                step.did(eng.tensor_tensor(g1b[:, s, :], g1b[:, s, :], bias1, ALU.add))
            piece_low(38)

            def residual(h, t):
                n = NT * (8 + h) + t
                eng.wait_ge(tile_done, n + 1)
                b = 5 + t % 2 if h else tile_bank(n)
                x = xr[:, t, 512 * h:512 * h + 512]
                step.did(eng.tensor_tensor(prod[:, n % 2, :], ps[:, b, :], g1b[:, min(t, 1), 512 * h:512 * h + 512], ALU.mult))
                step.wait()
                eng.tensor_tensor(x, x, prod[:, n % 2, :], ALU.add).then_inc(x2_ready, 1)

            def modulate_half(t):
                eng.wait_ge(vt_turned, t + 1)
                for k in range(4):
                    ins = eng.tensor_scalar(vT[:, k, P * t:P * t + P], ps[:, 2 * (t % 2), P * k:P * k + P],
                                            a2[:, k, min(t, 1):min(t, 1) + 1], modc[:, 24 + k, min(t, 1):min(t, 1) + 1],
                                            ALU.mult, ALU.add)
                ins.then_inc(vt_dve, 1)

            def logits(t):
                eng.wait_ge(logit_done, t + 1)
                eng.tensor_copy(lg[:, P * t:P * t + P], ps[0:E, 4, P * (t % 4):P * (t % 4) + P]).then_inc(lg_ready, 1)

            eng.wait_ge(x_reloaded, 16 * NT)
            step.wait()
            for t in range(NT):
                if t == 3:
                    piece_low(39)
                residual(0, t)
            for t in range(NT):
                residual(1, t)
                inverse_root(ssq2_ready, t + 1, ms2_ready, root2_ready, t, t + 1)
                eng.wait_ge(root2_ready, t + 1)
                eng.reciprocal(rstat[:, 3, t:t + 1], rstat[:, 2, t:t + 1]).then_inc(r2_ready, 1)
                if t:
                    modulate_half(t - 1)
                if t >= 2:
                    logits(t - 2)
            modulate_half(NT - 1)
            logits(NT - 2)
            logits(NT - 1)
            eng.wait_ge(lg_turned, 1)
            step.did(eng.tensor_reduce(sstat[:, 2, :], ps[:, 5, 0:16 * NT].rearrange("p (t e) -> p t e", e=E), AX.X, ALU.max))
            step.wait()
            eng.tensor_scalar(sstat[:, 0, :], sstat[:, 2, :], -1.0, None, ALU.mult).then_inc(max_ready, 1)
            eng.wait_ge(exp_ready, NT)
            step.did(eng.reciprocal(sstat[:, 2, :], sstat[:, 1, :]))
            step.wait()
            for t in range(NT):
                eng.tensor_scalar(soft[:, t, :], soft[:, t, :], sstat[:, 2, t:t + 1], None, ALU.mult).then_inc(soft_ready, 1)
            eng.wait_ge(soft_turned, NT)
            step.did(eng.tensor_copy(lg[:, 0:NP], ps[0:E, 6, 0:NP]))
            step.did(eng.tensor_copy(lg[:, NP:N], ps[0:E, 7, :]))
            step.wait()
            for rows, first, rounds in ((lg[:, NP:N], 0, CAP_S // 8), (lg[:, 0:NP], CAP_S, CAP_P // 8)):
                for r in range(rounds):
                    best = gates_e[:, first + 8 * r:first + 8 * r + 8]
                    step.did(eng.max(best, rows))
                    step.wait()
                    step.did(eng.max_index(idx[:, first + 8 * r:first + 8 * r + 8], best, rows))
                    if r < rounds - 1:
                        step.wait()
                        step.did(eng.match_replace(rows, best, rows, -1.0))
                        step.wait()
            step.wait()
            step.did(eng.tensor_scalar(idx_f[:, 0:CAP_S], idx[:, 0:CAP_S], float(NP), None, ALU.add))
            eng.tensor_copy(idx_f[:, CAP_S:CAP], idx[:, CAP_S:CAP]).then_inc(top_ready, 1)
            eng.wait_ge(top_turned, 1)
            eng.tensor_copy(idx_t[:, 0:E], ps[0:CAP, 0, 0:E]).then_inc(idx_ready, 1)
            eng.tensor_copy(idx_t[:, E:E + 1], ps[0:CAP, 0, E - 1:E]).then_inc(idx_ready, 1)
            eng.tensor_copy(gate_t[:, :], ps[0:CAP, 0, E:2 * E]).then_inc(idx_ready, 1)
            eng.wait_ge(idx_ready, 3)
            eng.wait_ge(rows_ready, 1)

            def modulate_xe():
                for k in range(KD):
                    b, c = 6 + k // 4, CAP * (k % 4)
                    for s, lo, hi in ((1, 0, CAP_S), (0, CAP_S, CAP)):
                        ins = eng.tensor_scalar(xeT[:, k, lo:hi], ps[:, b, c + lo:c + hi], a2[:, k, s:s + 1],
                                                modc[:, 24 + k, s:s + 1], ALU.mult, ALU.add)
                ins.then_inc(xe_modulated, 1)

            def split_piece(i, m):
                for half in range(2):
                    w = chunk(m)[:, 2 * half:2 * half + 2, :]
                    eng.wait_ge(unit_hi, units(i, m, half))
                    eng.tensor_tensor(w_lo(m)[:, 2 * half:2 * half + 2, :], w,
                                      w_hi[m % 2][:, 2 * half:2 * half + 2, :].bitcast(F32), ALU.subtract)\
                        .then_inc(unit_split, 1)

            def split_xe(n):
                eng.wait_ge(xe_turned, n)
                modulate_xe()
                eng.wait_ge(xe_hi_ready, n)
                eng.tensor_tensor(xe_lo[:, :, :], xeT[:, :, :], xe_hi[:, :, :].bitcast(F32), ALU.subtract).then_inc(xeT_ready, 1)

            def hidden(i, half):
                eng.wait_ge(h1_silu, i * 2 + (half + 1))
                product_done(eng, i, 4 * half + 3)
                v = hs[:, half * D:(half + 1) * D].rearrange("c (b f) -> c b f", b=2)
                eng.tensor_tensor(v, v, ps[0:CAP, 2:4, :], ALU.mult).then_inc(h_ready, 1)

            def split_h(i, half):
                eng.wait_ge(h_hi_ready, i * 2 + (half + 1))
                hi, lo = (x[:, 8 * half:8 * half + 8, :].rearrange("p (b k) c -> p b (k c)", b=2) for x in (h_hi, h_lo))
                eng.tensor_tensor(lo, ps[:, 6:8, 0:4 * CAP], hi.bitcast(F32), ALU.subtract).then_inc(hT_ready, 1)

            def output(i):
                product_done(eng, i, 11)
                gate = gate_t[:, E - 1:E] if type(i) is int else gate_t[:, bass.ds(i, 1)]
                eng.scalar_tensor_tensor(out=ye.rearrange("c (b f) -> c b f", b=2), in0=ps[0:CAP, 4:6, :], scalar=gate,
                                         in1=g2b.rearrange("c (b f) -> c b f", b=2), op0=ALU.mult, op1=ALU.mult)\
                    .then_inc(ye_ready, 1)

            def dve_expert(i, final):
                for m in range(2, 12):
                    split_piece(i, m)
                    if m == 5:
                        hidden(i, 0)
                    if m == 7:
                        split_h(i, 0)
                    if m == 9:
                        hidden(i, 1)
                    if m == 10:
                        split_h(i, 1)
                split_xe(i + 2)
                if not final:
                    for m in range(2):
                        split_piece(i + 1, m)
                output(i)

            split_piece(0, 0)
            split_xe(1)
            split_piece(0, 1)
            with eng.Fori(0, E - 1) as i:
                dve_expert(i, False)
            dve_expert(E - 1, True)

            eng.wait_ge(gf_loaded, 16)
            for t in range(NT + 1):
                if t < NT:
                    inverse_root(fin_ssq, t + 1, fin_ms, fin_root, t, t + 1)
                if t:
                    n = t - 1
                    eng.wait_ge(fin_root, t)
                    step.did(eng.reciprocal(rstat[:, 3, n:t], rstat[:, 2, n:t]))
                    step.wait()
                    eng.scalar_tensor_tensor(out=xr[:, n, :], in0=xr[:, n, :], scalar=rstat[:, 3, n:t], in1=gf,
                                             op0=ALU.mult, op1=ALU.mult).then_inc(out_ready, 1)

        @block.tensor
        def _(eng):
            eng.wait_ge(consts_ready, 4)
            eng.wait_ge(c_loaded, 32)
            eng.transpose(ps[:, 7, 0:2 * KD], c_rows[:, :], ident[0:2 * KD, 0:2 * KD]).then_inc(c_turned, 1)

            def mod_products(n):
                i, s = n // 4, n % 4
                for kk in range(2):
                    k = 2 * s + kk
                    if n % 2:
                        eng.wait_ge(mod_loaded[2 * s + kk], 16 * (i + 1))
                        operands = [(silu_c, slot(s)[:, 2 * D * kk:2 * D * kk + 2 * D])]
                    else:
                        eng.wait_ge(mod_split, n + kk + 1)
                        operands = [(silu_parts, mod_hi[:, n // 2 % 2, kk, :]), (silu_parts, mod_lo[:, s, kk, :])]
                    for b in range(4):
                        for part, (x, w) in enumerate(operands):
                            ins = eng.matmul(ps[0:4, 4 * (i % 2) + b, :], x[:, k, :], w[:, 512 * b:512 * b + 512],
                                             start=k == 0 and part == 0, stop=k == KD - 1)
                    ins.then_inc(mod_used, 1)

            def mod_turn(i):
                eng.wait_ge(mod_tiled, 16 * i + 16)
                eng.transpose(ps[:, 4 * (i % 2), 0:64], mod_tiles[:, :], ident[0:64, 0:64]).then_inc(mod_turned, 1)

            def turn_row_tile(rows, k, banks, done, emptied):
                if k >= banks // 2:
                    for e in emptied:
                        eng.wait_ge(e, k - banks // 2 + 1)
                for t in range(NT):
                    b = 2 * (k % (banks // 2)) + (t == 0)
                    c = 0 if t == 0 else P * (t - 1)
                    ins = eng.transpose(ps[:, b, c:c + P], rows[:, t, P * k:P * k + P], ident[:, :])
                ins.then_inc(done, 1)

            eng.wait_ge(silu_split, 1)
            for n in range(4):
                mod_products(n)
            eng.wait_ge(vec_loaded, 16 * 13)
            first = C_TAB + 8 * G_RCW
            for tile, rows, to in ((0, first, 0), (1, 80, first), (2, P, first + 80), (3, 8 * TAPS31 - P, first + 80 + P)):
                ins = eng.transpose(ps[:, 6, to:to + rows], vecs[0:rows, tile, :], ident[0:rows, 0:rows])
            ins.then_inc(cols_turned, 1)
            eng.wait_ge(cols_ready, 1)
            mod_products(4)
            mod_products(5)
            mod_turn(0)
            eng.wait_ge(xn1_ready, NT)
            eng.wait_ge(modc_ready, 1)
            mod_products(6)
            for k in range(KD // 2):
                turn_row_tile(xn1, k, 4, xt_turned, (ut_sample, ut_prompt))
            mod_products(7)
            for k in range(KD // 2, KD):
                turn_row_tile(xn1, k, 4, xt_turned, (ut_sample, ut_prompt))
            mod_products(8)
            mod_products(9)
            mod_products(10)
            mod_turn(1)
            mod_products(11)
            mod_turn(2)
            eng.wait_ge(modc_ready, 3)

            eng.wait_ge(u_split, 2)
            with eng.Fori(0, 4) as i:
                for n in range(6):
                    kind, t = n // 2, n % 2
                    if t == 0:
                        eng.wait_ge(a_split, i * 3 + (kind + 1))
                    if n >= 4:
                        eng.wait_ge(xr_copied, i * 2 + (n - 3))
                    b = 2 * (n % 4)
                    hi, lo = a_hi[kind % 2][:, :, P * t:P * t + P], a_lo[:, kind, :, P * t:P * t + P]
                    for k in range(KD):
                        for h in range(2):
                            for part, (w, x) in enumerate(((hi, u_hi), (lo, u_hi), (hi, u_lo))):
                                ins = eng.matmul(ps[:, b + h, 0:HALF], w[:, k, :], x[:, k, HALF * h:HALF * h + HALF],
                                                 start=k == 0 and part == 0, stop=k == KD - 1 and part == 2)
                    ins.then_inc((xr_done, xv_done, xg_done)[kind], 1)
                eng.wait_ge(gw_loaded, i * 64 + 64)
                for n in range(8):
                    t, d, g = n // 4, n // 2 % 2, n % 2
                    b = GATE_BANKS[n % 4]
                    if g == 0 and d == 0:
                        eng.wait_ge(xc_ready, i * 2 + (t + 1))
                    if n == 0 or n == 2:
                        eng.wait_ge(glu_ready, i * 2 + (n // 2 + 1))
                    if n >= 4:
                        eng.wait_ge(gate_sig, i * 8 + (n - 3))
                    for h in range(2):
                        ins = eng.matmul(ps[:, b + h, 0:LX // 2], gw[:, t, 2 * d + g, :],
                                         xc[:, t, LX // 2 * h:LX // 2 * (h + 1)], start=True, stop=True)
                    ins.then_inc(gate_done, 1)
                eng.wait_ge(gate_sig, i * 8 + 8)

            def bank_free(g, t):
                n = NT * g + t - 6
                if n >= 0:
                    readers, last_one = (GATES, gate_ready) if n // NT in GATES else (MERGES, m_ready)
                    eng.wait_ge(last_one, NT * readers.index(n // NT) + n % NT + 1)

            def products(g, p, x_hi, x_lo):
                q = 4 * g + p
                eng.wait_ge(piece_split, q + 1)
                for t in range(NT):
                    if p == 0:
                        bank_free(g, t)
                    for kk in range(2):
                        k = 2 * p + kk
                        for n, (x, w) in enumerate(((x_hi, b_hi[q % 4][:, kk, :]), (x_hi, b_lo[:, q % 4, kk, :]),
                                                    (x_lo, b_hi[q % 4][:, kk, :]))):
                            ins = eng.matmul(ps[:, tile_bank(NT * g + t), :], x[:, k, P * t:P * t + P], w,
                                             start=k == 0 and n == 0, stop=k == KD - 1 and n == 2)
                    if p == 3:
                        ins.then_inc(tile_done, 1)
                if p < 3:
                    ins.then_inc(piece_used, 1)

            def turn_merged(k):
                eng.wait_ge(m_ready, NT * (3 if k < 4 else 4))
                if k:
                    eng.wait_ge(mt_split, k)
                for t in range(NT):
                    ins = eng.transpose(turned_merged[:, P * t:P * t + P], merged[:, t, P * k:P * k + P], ident[:, :])
                ins.then_inc(mt_turned, 1)

            for g in range(2):
                for p in range(4):
                    products(g, p, u_hi, u_lo)
            eng.wait_ge(lru_done, 4)
            eng.wait_ge(gate_ready, NT + 1)
            eng.transpose(ps[0:16, 7, 0:P], flat(last), ident[:, :]).then_inc(last_turned, 1)
            for h in range(2):
                for k in range(KD):
                    ins = eng.matmul(ps[:, 5 + h, 0:HALF], ones[:, :], cu[:, k, HALF * h:HALF * h + HALF],
                                     start=k == 0, stop=k == KD - 1)
            ins.then_inc(ln_summed, 1)
            eng.wait_ge(last_ready, 1)
            for g in range(2, 8):
                for p in range(4):
                    if g in GATES:
                        products(g, p, u_hi, u_lo)
                    elif g < 4:
                        if g == 2:
                            eng.wait_ge(y_split, p // 2 + 1)
                        products(g, p, y_hi, ya_lo)
                    else:
                        if g == 5:
                            eng.wait_ge(yb_split, 2 * p + 2)
                        products(g, p, y_hi, yb_lo)
                    if g == 7:
                        turn_merged(p)
                    if g == 2:
                        for k in (2 * p, 2 * p + 1):
                            eng.wait_ge(ln_squared, k + 1)
                            for h in range(2):
                                ins = eng.matmul(ps[:, 5 + h, 0:HALF], ones[:, :], ln_sq[:, k % 2, HALF * h:HALF * h + HALF],
                                                 start=k == 0, stop=k == KD - 1)
                            ins.then_inc(ln_sq_used, 1)
            for k in range(KD):
                if k % 2 == 0:
                    eng.wait_ge(piece_split, 33 + k // 2)
                eng.wait_ge(mt_split, k + 1)
                for t in range(NT):
                    if k == 0:
                        bank_free(8, t)
                    parts = ((m_hi, b_hi[k // 2][:, k % 2, :]), (m_hi, b_lo[:, k // 2, k % 2, :]), (m_lo, b_hi[k // 2][:, k % 2, :]))
                    for n, (x, w) in enumerate(parts):
                        ins = eng.matmul(ps[:, tile_bank(NT * 8 + t), :], x[:, k, P * t:P * t + P], w,
                                         start=k == 0 and n == 0, stop=k == KD - 1 and n == 2)
                    if k == KD - 1:
                        ins.then_inc(tile_done, 1)
                if k in (1, 3, 5):
                    ins.then_inc(piece_used, 1)
                if 1 <= k <= 4:
                    turn_merged(k + 3)

            def last_products(t):
                if t >= 2:
                    eng.wait_ge(x2_ready, NT + t - 1)
                for k in range(KD):
                    if t == 0 and k % 2 == 0:
                        eng.wait_ge(piece_split, 37 + k // 2)
                    for n, (x, w) in enumerate(((m_hi, b_hi[k // 2][:, k % 2, :]), (m_hi, b_lo[:, k // 2, k % 2, :]),
                                                (m_lo, b_hi[k // 2][:, k % 2, :]))):
                        ins = eng.matmul(ps[:, 5 + t % 2, :], x[:, k, P * t:P * t + P], w,
                                         start=k == 0 and n == 0, stop=k == KD - 1 and n == 2)
                ins.then_inc(tile_done, 1)

            def turn_normed(t):
                eng.wait_ge(xn2_ready, t + 1)
                if t >= 2:
                    eng.wait_ge(vt_dve, t - 1)
                    eng.wait_ge(vt_act, t - 1)
                for k in range(KD):
                    ins = eng.transpose(ps[:, 2 * (t % 2) + k // 4, P * (k % 4):P * (k % 4) + P], xn2[:, t, P * k:P * k + P],
                                        ident[:, :])
                ins.then_inc(vt_turned, 1)

            def router(t):
                eng.wait_ge(vt_dve, t + 1)
                eng.wait_ge(vt_act, t + 1)
                if t >= 1:
                    eng.wait_ge(lg_ready, t)
                for k in range(KD):
                    ins = eng.matmul(ps[0:E, 4, P * (t % 4):P * (t % 4) + P], wr[:, k, :], vT[:, k, P * t:P * t + P],
                                     start=k == 0, stop=k == KD - 1)
                ins.then_inc(logit_done, 1)

            eng.wait_ge(wr_loaded, 16)
            for t in range(NT):
                last_products(t)
                if t == 2:
                    eng.wait_ge(x2_ready, NT)
                if t >= 2:
                    turn_normed(t - 2)
                if t >= 3:
                    router(t - 3)
            turn_normed(3)
            router(2)
            turn_normed(4)
            router(3)
            router(4)
            for t in range(NT):
                eng.wait_ge(lg_ready, t + 1)
                ins = eng.transpose(ps[:, 5, 16 * t:16 * t + 16], lg[:, P * t:P * t + P], ident[0:E, 0:E])
            ins.then_inc(lg_turned, 1)
            for t in range(NT):
                eng.wait_ge(soft_ready, t + 1)
                b, c = (6, 0) if t == 0 else (7, P * (t - 1))
                eng.transpose(ps[0:E, b, c:c + P], soft[:, t, :], ident[:, :]).then_inc(soft_turned, 1)
            eng.wait_ge(top_ready, 1)
            eng.transpose(ps[0:CAP, 0, 0:E], idx_f[:, :], ident[0:E, 0:E])
            eng.transpose(ps[0:CAP, 0, E:2 * E], gates_e[:, :], ident[0:E, 0:E]).then_inc(top_turned, 1)

            def turn_xe(n):
                eng.wait_ge(xe_loaded, n * 16)
                for k in range(KD):
                    ins = eng.transpose(ps[:, 6 + k // 4, CAP * (k % 4):CAP * (k % 4) + CAP], xe[:, P * k:P * k + P],
                                        ident[0:CAP, 0:CAP])
                ins.then_inc(xe_turned, 1)

            def turn_h(half):
                for k in range(8):
                    ins = eng.transpose(ps[:, 6 + k // 4, CAP * (k % 4):CAP * (k % 4) + CAP],
                                        hs[:, (8 * half + k) * P:(8 * half + k + 1) * P], ident[0:CAP, 0:CAP])
                ins.then_inc(h_turned, 1)

            eng.wait_ge(idx_ready, 3)
            turn_xe(1)
            with eng.Fori(0, E) as i:
                eng.wait_ge(xeT_ready, i + 1)

                def rows_times(m, bank, x_hi, x_lo, k0, first, last_one):
                    eng.wait_ge(unit_split, units(i, m))
                    for kk in range(4):
                        for b in range(2):
                            for n, (x, w) in enumerate(((x_hi, w_hi[m % 2]), (x_hi, w_lo(m)), (x_lo, w_hi[m % 2]))):
                                ins = eng.matmul(ps[0:CAP, bank + b, :], x[:, k0 + kk, :],
                                                 w[:, kk, 512 * b:512 * b + 512],
                                                 start=first and kk == 0 and n == 0, stop=last_one and kk == 3 and n == 2)
                        if kk % 2:
                            ins.then_inc(unit_used, 1)

                def token_product(m, bank):
                    for part in range(2):
                        rows_times(m + part, bank, xe_hi, xe_lo, 4 * part, part == 0, part == 1)

                def hidden_product(m):
                    rows_times(m, 4, h_hi, h_lo, 4 * (m - 8), m == 8, m == 11)

                token_product(0, 0)
                token_product(2, 2)
                eng.wait_ge(h1_silu, i * 2 + 1)
                token_product(4, 0)
                eng.wait_ge(h_ready, i * 2 + 1)
                turn_h(0)
                token_product(6, 2)
                eng.wait_ge(hT_ready, i * 2 + 1)
                hidden_product(8)
                eng.wait_ge(h_ready, i * 2 + 2)
                turn_h(1)
                hidden_product(9)
                eng.wait_ge(hT_ready, i * 2 + 2)
                turn_xe(i + 2)
                hidden_product(10)
                hidden_product(11)


_INS = ["x_prompt", "x_sample", "state_rglru", "c", "c_ctx", "norm1_g", "norm2_g", "w_mod", "b_mod", "w_in",
        "rnn_conv_w", "rnn_conv_b", "rnn_gate_w", "rnn_gate_b", "rnn_lambda", "w_rnn_out", "conv_dw_w", "conv_dw_b",
        "conv_ln_g", "conv_ln_b", "w_conv_out", "w_out", "w_router", "w_e1", "w_e3", "w_e2", "final_norm_g"]
_OUTS = [("y_prompt", (1, NP, D)), ("y_sample", (1, NS, D)), ("new_state", (1, 1, 2, D))]


def kernel(**inputs):
    import numpy as np
    from concourse import bacc
    from concourse.bass_utils import run_bass_kernel_spmd

    nc = bacc.Bacc("TRN2", target_bir_lowering=False, num_devices=1)
    arrays, args = {}, {}
    for name in _INS:
        x = np.ascontiguousarray(inputs[name])
        arrays[f"in_{name}"] = x
        args[name] = nc.dram_tensor(f"in_{name}", x.shape, mybir.dt.from_np(x.dtype), kind="ExternalInput").ap()
    for name, shape in _OUTS:
        args[name] = nc.dram_tensor(f"out_{name}", shape, F32, kind="ExternalOutput").ap()
    trunk_layer(nc, args)
    r = run_bass_kernel_spmd(nc, [arrays], core_ids=[0])
    return tuple(r.results[0][f"out_{name}"] for name, _ in _OUTS)
```
